# Optimizing a Trainium2 kernel written in Bass

```python
import jax, jax.numpy as jnp
from jax import lax
import numpy as np

D_MODEL = 1024
BATCH = 1
SEQ = 256
DEPTH = 2

N_EVEN = (DEPTH + 1) // 2
N_ODD = DEPTH // 2
EPS = 1e-5
CONV_DIM = D_MODEL // 2
CONV_GROUPS = 8
CONV_WIDTH = 3
GMLP_DIM = D_MODEL // 2
GMLP_HEADS = 4
GMLP_HEAD_DIM = GMLP_DIM // GMLP_HEADS
CHUNK = 128
MIX_IN = 3 * CONV_DIM + 2 * GMLP_DIM
HEAD_DIM = 64
N_Q_HEADS = D_MODEL // HEAD_DIM
N_KV_HEADS = max(1, N_Q_HEADS // 8)
Q_PER_KV = N_Q_HEADS // N_KV_HEADS
WINDOW = 128
ROPE_DIM = HEAD_DIM // 4
ROPE_THETA = 500000.0
ATTN_SCALE = HEAD_DIM ** -0.5
QKV_DIM = (N_Q_HEADS + 2 * N_KV_HEADS) * HEAD_DIM
MAX_POS_OFFSET = 4096
FFN_DIM = ((8 * D_MODEL // 3 + 255) // 256) * 256
N_EXPERTS = 8
TOP_K = 2
EXPERT_DIM = 7 * D_MODEL // 2
MOE_BLOCK = 256

kernel_name = "hybrid_conv_gmlp_swa_moe_trunk"

def rms_norm(x, g):
    xf = x.astype(jnp.float32)
    y = xf * lax.rsqrt(jnp.mean(xf * xf, axis=-1, keepdims=True) + EPS)
    return (y * g.astype(jnp.float32)).astype(x.dtype)

def layer_norm(x, g, b):
    xf = x.astype(jnp.float32)
    mu = jnp.mean(xf, axis=-1, keepdims=True)
    var = jnp.mean(jnp.square(xf - mu), axis=-1, keepdims=True)
    y = (xf - mu) * lax.rsqrt(var + EPS)
    return (y * g.astype(jnp.float32) + b.astype(jnp.float32)).astype(x.dtype)

def swiglu(x, wg, wu, wd):
    return (jax.nn.silu(x @ wg) * (x @ wu)) @ wd

def causal_depthwise_conv(h, w):
    K = w.shape[-1]
    S = h.shape[1]
    hp = jnp.pad(h, ((0, 0), (K - 1, 0), (0, 0)))
    out = hp[:, 0:S, :] * w[:, 0]
    for k in range(1, K):
        out = out + hp[:, k:k + S, :] * w[:, k]
    return out

def gmlp_spatial_gate(u, v, ln_g, ln_b, w_s, b_s):
    B, S, _ = v.shape
    nc = S // CHUNK
    vn = layer_norm(v, ln_g, ln_b).reshape(B, nc, CHUNK, GMLP_HEADS, GMLP_HEAD_DIM)
    causal = jnp.tril(jnp.ones((CHUNK, CHUNK), dtype=bool))
    w = jnp.where(causal[None], w_s, jnp.zeros_like(w_s)).astype(v.dtype)
    mixed = jnp.einsum('hij,bcjhd->bcihd', w, vn) + b_s.T.astype(v.dtype)[None, None, :, :, None]
    return u * mixed.reshape(B, S, GMLP_DIM)

def conv_gmlp_mixer(xn, w_in, conv_w, ln_g, ln_b, w_s, b_s, w_out):
    z = xn @ w_in
    a_b, a_c, a_x, b_u, b_v = jnp.split(
        z, [CONV_DIM, 2 * CONV_DIM, 3 * CONV_DIM, 3 * CONV_DIM + GMLP_DIM], axis=-1)
    y_a = a_b * causal_depthwise_conv(a_c * a_x, conv_w)
    y_b = gmlp_spatial_gate(jax.nn.gelu(b_u, approximate=False), jax.nn.gelu(b_v, approximate=False),
                            ln_g, ln_b, w_s, b_s)
    return jnp.concatenate([y_a, y_b], axis=-1) @ w_out

def partial_rope(t, cos, sin):
    half = ROPE_DIM // 2
    tr = t[..., :ROPE_DIM].astype(jnp.float32)
    t1, t2 = tr[..., :half], tr[..., half:]
    rot = jnp.concatenate([t1 * cos - t2 * sin, t2 * cos + t1 * sin], axis=-1).astype(t.dtype)
    return jnp.concatenate([rot, t[..., ROPE_DIM:]], axis=-1)

def swa_sink_attention(xn, positions, w_qkv, b_qkv, sinks, w_o, b_o):
    B, S, _ = xn.shape
    nb = S // WINDOW
    qkv = xn @ w_qkv + b_qkv
    q, k, v = jnp.split(qkv, [N_Q_HEADS * HEAD_DIM, (N_Q_HEADS + N_KV_HEADS) * HEAD_DIM], axis=-1)
    q = q.reshape(B, S, N_Q_HEADS, HEAD_DIM)
    k = k.reshape(B, S, N_KV_HEADS, HEAD_DIM)
    v = v.reshape(B, S, N_KV_HEADS, HEAD_DIM)
    inv_freq = ROPE_THETA ** (-jnp.arange(0, ROPE_DIM, 2, dtype=jnp.float32) / ROPE_DIM)
    ang = positions.astype(jnp.float32)[..., None] * inv_freq
    cos = jnp.cos(ang)[:, :, None, :]
    sin = jnp.sin(ang)[:, :, None, :]
    q = partial_rope(q, cos, sin)
    k = partial_rope(k, cos, sin)
    qb = q.reshape(B, nb, WINDOW, N_KV_HEADS, Q_PER_KV, HEAD_DIM)

    def band(t):
        tb = t.reshape(B, nb, WINDOW, N_KV_HEADS, HEAD_DIM)
        prev = jnp.pad(tb, ((0, 0), (1, 0), (0, 0), (0, 0), (0, 0)))[:, :-1]
        return jnp.concatenate([prev, tb], axis=2)

    kb, vb = band(k), band(v)
    s = jnp.einsum('bnqhgd,bnshd->bnhgqs', qb, kb, preferred_element_type=jnp.float32) * ATTN_SCALE
    qi = jnp.arange(WINDOW)[:, None]
    sj = jnp.arange(2 * WINDOW)[None, :]
    rel = qi + WINDOW - sj
    local = (rel >= 0) & (rel < WINDOW)
    valid = (jnp.arange(nb)[:, None] * WINDOW - WINDOW + sj) >= 0
    mask = local[None] & valid[:, None, :]
    s = jnp.where(mask[None, :, None, None], s, -jnp.inf)
    sink = sinks.astype(jnp.float32).reshape(N_KV_HEADS, Q_PER_KV)[None, None, :, :, None]
    m = jnp.maximum(jnp.max(s, axis=-1), sink)
    p = jnp.exp(s - m[..., None])
    denom = jnp.sum(p, axis=-1) + jnp.exp(sink - m)
    probs = (p / denom[..., None]).astype(vb.dtype)
    o = jnp.einsum('bnhgqs,bnshd->bnqhgd', probs, vb).reshape(B, S, N_Q_HEADS * HEAD_DIM)
    return o @ w_o + b_o

def moe_swiglu(xn, router_w, wg, wu, wd):
    B, S, D = xn.shape
    N = B * S
    NP = N * TOP_K
    xf = xn.reshape(N, D)
    logits = jnp.dot(xf, router_w, preferred_element_type=jnp.float32)
    top_vals, top_idx = lax.top_k(logits, TOP_K)
    gates = jax.nn.softmax(top_vals, axis=-1)
    expert_ids = top_idx.reshape(NP).astype(jnp.int32)
    token_ids = jnp.repeat(jnp.arange(N, dtype=jnp.int32), TOP_K)
    pair_gates = gates.reshape(NP)
    order = jnp.argsort(expert_ids)
    sorted_e = expert_ids[order]
    sizes = jnp.bincount(expert_ids, length=N_EXPERTS).astype(jnp.int32)
    padded = ((sizes + MOE_BLOCK - 1) // MOE_BLOCK) * MOE_BLOCK
    starts = jnp.cumsum(sizes) - sizes
    pends = jnp.cumsum(padded)
    pstarts = pends - padded
    dest = pstarts[sorted_e] + jnp.arange(NP, dtype=jnp.int32) - starts[sorted_e]
    n_rows = (-(-NP // MOE_BLOCK)) * MOE_BLOCK + N_EXPERTS * MOE_BLOCK
    n_blocks = n_rows // MOE_BLOCK
    row_token = jnp.zeros((n_rows,), jnp.int32).at[dest].set(token_ids[order])
    row_gate = jnp.zeros((n_rows,), jnp.float32).at[dest].set(pair_gates[order])
    block_start = jnp.arange(n_blocks, dtype=jnp.int32) * MOE_BLOCK
    block_expert = jnp.minimum(jnp.searchsorted(pends, block_start, side='right'), N_EXPERTS - 1)
    x_rows = xf[row_token].reshape(n_blocks, MOE_BLOCK, D)

    def expert_block(args):
        xb, e = args
        return (jax.nn.silu(xb @ wg[e]) * (xb @ wu[e])) @ wd[e]

    y_rows = lax.map(expert_block, (x_rows, block_expert)).reshape(n_rows, D)
    y = jnp.zeros((N, D), xn.dtype).at[row_token].add(y_rows * row_gate[:, None].astype(xn.dtype))
    return y.reshape(B, S, D)

def setup_inputs(seed: int = 0) -> dict:
    key = jax.random.key(seed)
    ks = iter(jax.random.split(key, 32))

    def nrm(shape, scale):
        return jax.random.normal(next(ks), shape, jnp.float32) * scale

    def gain(shape):
        return 1.0 + nrm(shape, 0.05)

    NE, NO, D = N_EVEN, N_ODD, D_MODEL
    x = nrm((BATCH, SEQ, D), 1.0)
    positions = (jax.random.randint(next(ks), (BATCH, 1), 0, MAX_POS_OFFSET, dtype=jnp.int32)
                 + jnp.arange(SEQ, dtype=jnp.int32)[None, :])
    return {
        "x": x,
        "positions": positions,
        "final_norm_g": gain((D,)),
        "ev_norm1_g": gain((NE, D)),
        "ev_w_in": nrm((NE, D, MIX_IN), D ** -0.5),
        "ev_conv_w": nrm((NE, CONV_DIM, CONV_WIDTH), CONV_WIDTH ** -0.5),
        "ev_ln_g": gain((NE, GMLP_DIM)),
        "ev_ln_b": nrm((NE, GMLP_DIM), 0.02),
        "ev_spatial_w": nrm((NE, GMLP_HEADS, CHUNK, CHUNK), CHUNK ** -0.5),
        "ev_spatial_b": 1.0 + nrm((NE, GMLP_HEADS, CHUNK), 0.1),
        "ev_w_out": nrm((NE, CONV_DIM + GMLP_DIM, D), (CONV_DIM + GMLP_DIM) ** -0.5),
        "ev_norm2_g": gain((NE, D)),
        "ev_ffn_wg": nrm((NE, D, FFN_DIM), D ** -0.5),
        "ev_ffn_wu": nrm((NE, D, FFN_DIM), D ** -0.5),
        "ev_ffn_wd": nrm((NE, FFN_DIM, D), FFN_DIM ** -0.5),
        "od_norm1_g": gain((NO, D)),
        "od_w_qkv": nrm((NO, D, QKV_DIM), D ** -0.5),
        "od_b_qkv": nrm((NO, QKV_DIM), 0.02),
        "od_sinks": nrm((NO, N_Q_HEADS), 1.0),
        "od_w_o": nrm((NO, N_Q_HEADS * HEAD_DIM, D), (N_Q_HEADS * HEAD_DIM) ** -0.5),
        "od_b_o": nrm((NO, D), 0.02),
        "od_norm2_g": gain((NO, D)),
        "od_router_w": nrm((NO, D, N_EXPERTS), D ** -0.5),
        "od_exp_wg": nrm((NO, N_EXPERTS, D, EXPERT_DIM), D ** -0.5),
        "od_exp_wu": nrm((NO, N_EXPERTS, D, EXPERT_DIM), D ** -0.5),
        "od_exp_wd": nrm((NO, N_EXPERTS, EXPERT_DIM, D), EXPERT_DIM ** -0.5),
    }

def reference(x, positions, final_norm_g,
              ev_norm1_g, ev_w_in, ev_conv_w, ev_ln_g, ev_ln_b, ev_spatial_w, ev_spatial_b,
              ev_w_out, ev_norm2_g, ev_ffn_wg, ev_ffn_wu, ev_ffn_wd,
              od_norm1_g, od_w_qkv, od_b_qkv, od_sinks, od_w_o, od_b_o, od_norm2_g,
              od_router_w, od_exp_wg, od_exp_wu, od_exp_wd):
    h = x
    for layer in range(DEPTH):
        i = layer // 2
        if layer % 2 == 0:
            h = h + conv_gmlp_mixer(rms_norm(h, ev_norm1_g[i]), ev_w_in[i], ev_conv_w[i],
                                    ev_ln_g[i], ev_ln_b[i], ev_spatial_w[i], ev_spatial_b[i],
                                    ev_w_out[i])
            h = h + swiglu(rms_norm(h, ev_norm2_g[i]), ev_ffn_wg[i], ev_ffn_wu[i], ev_ffn_wd[i])
        else:
            h = h + swa_sink_attention(rms_norm(h, od_norm1_g[i]), positions, od_w_qkv[i],
                                       od_b_qkv[i], od_sinks[i], od_w_o[i], od_b_o[i])
            h = h + moe_swiglu(rms_norm(h, od_norm2_g[i]), od_router_w[i], od_exp_wg[i],
                               od_exp_wu[i], od_exp_wd[i])
    return rms_norm(h, final_norm_g)


_drawn_inputs = setup_inputs


def setup_inputs(seed=0):
    import zlib

    import numpy as np

    out = dict(_drawn_inputs(seed))
    spreads = {}
    factors = {'ev_ln_b': 3.316, 'od_sinks': 2.829, 'od_b_qkv': 2.707, 'od_b_o': 4.172}
    for name, (base, spread) in spreads.items():
        noise = np.random.default_rng([zlib.crc32(name.encode()), seed]).standard_normal(out[name].shape)
        drawn = base * np.exp(spread * noise) if base else spread * noise
        out[name] = __import__('jax').numpy.asarray(drawn.astype(out[name].dtype))
    for name, factor in factors.items():
        out[name] = (out[name] * factor).astype(out[name].dtype)
    return out
```

```python
from contextlib import ExitStack

import numpy as np

import concourse.bass as bass
from concourse import mybir

ALU = mybir.AluOpType
ACT = mybir.ActivationFunctionType
F32 = mybir.dt.float32
F32R = mybir.dt.float32r
BF16 = mybir.dt.bfloat16
I32 = mybir.dt.int32
U32 = mybir.dt.uint32
AX_X = mybir.AxisListType.X

P = 128
D = 1024
KT = D // P
T = 256
TT = T // P
EPS = 1e-5
N = 512

CONV = 512
CT = CONV // P
CW = 3
GM = 512
MIX_IN = 3 * CONV + 2 * GM
GH = 4
FFN = 2816
FU = FFN // 256

HD = 64
NQ = 16
NKV = 2
QPK = NQ // NKV
QKV = (NQ + 2 * NKV) * HD
ROPE = HD // 4
RH = ROPE // 2
THETA = 500000.0
SCALE = HD ** -0.5
MASKED = -1e30

NE = 8
ED = 3584
EU = ED // N
BLOCKS = 2 * NE

PIECE = 2048
SPLITS = 3
RING_A = 7
RING = 14
EP = 6 * EU

V0, U0, C0, X0, B0 = 0, 2, 4, 6, 8
WOUT0 = 10
FFN0 = WOUT0 + 4
QKV0 = FFN0 + 3 * FU
WO0 = QKV0 + 5
FRONT = WO0 + 4
OUT_KT = (4, 5, 6, 7, 0, 1, 2, 3)

assert FRONT % RING_A == 0 and EP % RING == 0 and EP % SPLITS == 0


def ffn_pieces(u):
    g = FFN0 + (0 if u == 0 else 3 * u - 1)
    d = FFN0 + 3 * u + 4 if u < FU - 1 else FFN0 + 3 * FU - 1
    return g, g + 1, d


def expert_pieces(j):
    g = 0 if j == 0 else 6 * j - 2
    d = 6 * j + 8 if j < EU - 1 else EP - 2
    return g, g + 2, d


def build(nc, x, positions, final_norm_g, ev_norm1_g, ev_w_in, ev_conv_w, ev_ln_g, ev_ln_b,
          ev_spatial_w, ev_spatial_b, ev_w_out, ev_norm2_g, ev_ffn_wg, ev_ffn_wu, ev_ffn_wd,
          od_norm1_g, od_w_qkv, od_b_qkv, od_sinks, od_w_o, od_b_o, od_norm2_g, od_router_w,
          od_exp_wg, od_exp_wu, od_exp_wd, out):
    ctx = ExitStack()

    def sb(name, shape, dt=F32, scope=None):
        return (scope or ctx).enter_context(nc.sbuf_tensor(name, shape, dt))

    def sem(name):
        return ctx.enter_context(nc.semaphore(name))

    ring_a = [sb(f"ring{s}", [P, PIECE]) for s in range(RING_A)]
    w_hi = sb("w_hi", [P, SPLITS, PIECE], F32R)
    w_lo = sb("w_lo", [P, SPLITS, PIECE], F32R)
    h = sb("h", [P, TT, D])
    xn = sb("xn", [P, TT, D])
    ident = sb("ident", [P, P])
    gains = sb("gains", [P, 4, KT])
    final_g = sb("final_g", [P, D])
    ssq = sb("ssq", [P, TT])
    var = sb("var", [P, TT])
    sd = sb("sd", [P, TT])
    rstd = sb("rstd", [P, TT])
    router = sb("router", [P, KT, NE])
    ones = sb("ones", [P, P])
    tri = sb("tri", [P, P])
    iota_s = sb("iota_s", [P, P])
    count_max = sb("count_max", [P, 1], I32)
    slot_of = sb("slot_of", [P, TT, BLOCKS + 1])
    gate_of = sb("gate_of", [P, TT, BLOCKS])

    s1 = ExitStack()
    xT_hi = sb("xT_hi", [P, KT, T], F32R, s1)
    xT_lo = sb("xT_lo", [P, KT, T], F32R, s1)
    m_ = ExitStack()
    yT_hi = sb("yT_hi", [P, KT, T], F32R, m_)
    yT_lo = sb("yT_lo", [P, KT, T], F32R, m_)
    yT = sb("yT", [P, 4, T], F32, m_)
    v_act = sb("v_act", [P, TT, GM], F32, m_)
    uT = sb("uT", [P, GH, T], F32, m_)
    acT = sb("acT", [P, CT, T], F32, m_)
    hc = sb("hc", [P, CT, T + CW - 1], F32, m_)
    cv = sb("cv", [P, 2, T], F32, m_)
    ln_g = sb("ln_g", [P, GM], F32, m_)
    ln_b = sb("ln_b", [P, GM], F32, m_)
    sp_w = sb("sp_w", [P, GH, P], F32, m_)
    sp_wT = sb("sp_wT", [P, GH, P], F32, m_)
    sp_b = sb("sp_b", [P, GH, P], F32, m_)
    conv_w = sb("conv_w", [P, CT, CW], F32, m_)
    bn = sb("bn", [P, TT, 6], F32, m_)
    mv = sb("mv", [P, TT, 2], F32, m_)
    gain_rows = sb("gain_rows", [4 * KT, P], F32, m_)
    m_.close()

    f_ = ExitStack()
    f_s = sb("f_s", [P, 2, T], F32, f_)
    f_a = sb("f_a", [P, 2, T], F32, f_)
    fT_hi = sb("fT_hi", [P, 2, T], F32R, f_)
    fT_lo = sb("fT_lo", [P, 2, T], F32R, f_)
    f_.close()

    a_ = ExitStack()
    sb("ffn_space", [P, 8 * T], F32, a_)
    b_qkv = sb("b_qkv", [P, QKV], F32, a_)
    b_o = sb("b_o", [P, D], F32, a_)
    sinks = sb("sinks", [P, NQ], F32, a_)
    neg_sinks = sb("neg_sinks", [P, NQ], F32, a_)
    pos_i = sb("pos_i", [P, TT], I32, a_)
    pos_f = sb("pos_f", [P, TT], F32, a_)
    inv_freq = sb("inv_freq", [P, RH], F32, a_)
    ang = sb("ang", [P, TT, RH], F32, a_)
    turns = sb("turns", [P, TT, RH], F32, a_)
    red = sb("red", [P, TT, RH], F32, a_)
    red_c = sb("red_c", [P, TT, RH], F32, a_)
    sin_t = sb("sin_t", [P, TT, RH], F32, a_)
    cos_t = sb("cos_t", [P, TT, RH], F32, a_)
    mask0 = sb("mask0", [P, 4, P], BF16, a_)
    mask1 = sb("mask1", [P, 2, T], BF16, a_)
    ident_b = sb("ident_b", [P, P], BF16, a_)
    qkv = sb("qkv", [P, TT, QKV], F32, a_)
    rope_t = sb("rope_t", [P, 4, TT, (NQ + NKV) * RH], F32, a_)
    k_pad = sb("k_pad", [P, TT, NKV, 2, 2 * HD], F32, a_)
    qT = sb("qT", [P, NQ // 2, T], F32, a_)
    kT = sb("kT", [P, NKV, 2, T], F32, a_)
    probs = sb("probs", [P, 2, N], F32, a_)
    probsT = sb("probsT", [P, 2, N], F32, a_)
    raw_max = sb("raw_max", [P, TT, NQ], F32, a_)
    neg_max = sb("neg_max", [P, TT, NQ], F32, a_)
    den = sb("den", [P, TT, NQ], F32, a_)
    sink_e = sb("sink_e", [P, TT, NQ], F32, a_)
    o_tok = xn
    a_.close()
    s1.close()

    ring_b = [sb(f"ring{s}", [P, PIECE]) for s in range(RING_A, RING)]
    ring = ring_a + ring_b
    r_ = ExitStack()
    xT = sb("xT", [P, KT, T], F32, r_)
    r_.close()
    gT_hi = sb("gT_hi", [P, KT, P], F32R)
    gT_lo = sb("gT_lo", [P, KT, P], F32R)
    e_s = sb("e_s", [P, N])
    e_a = sb("e_a", [P, N])
    eT_hi = sb("eT_hi", [P, 4, P], F32R)
    eT_lo = sb("eT_lo", [P, 4, P], F32R)
    e_y = sb("e_y", [P, D])
    pick = sb("pick", [P, TT, P])
    pick_g = sb("pick_g", [P, TT, P])
    pick_gT = sb("pick_gT", [P, T])

    logits = sb("logits", [P, TT, NE])
    top_v = sb("top_v", [P, TT, 8])
    top_i = sb("top_i", [P, TT, 8], U32)
    top_f = sb("top_f", [P, TT, 2])
    diff = sb("diff", [P, TT])
    p2 = sb("p2", [P, TT])
    psum_g = sb("psum_g", [P, TT])
    g1 = sb("g1", [P, TT])
    g2 = sb("g2", [P, TT])
    oh = sb("oh", [P, TT, 2, NE])
    sel = sb("sel", [P, TT, NE])
    cmax_f = sb("cmax_f", [P, 1])

    bank = [ctx.enter_context(nc.psum_tensor(f"bank{i}", [P, N], F32)) for i in range(8)]

    landed = [sem(f"landed{s}") for s in range(RING)]
    hi_ready, lo_ready, piece_used = sem("hi_ready"), sem("lo_ready"), sem("piece_used")
    ld_x, ld_gain, ld_even, ld_odd, ld_late = (sem("ld_x"), sem("ld_gain"), sem("ld_even"),
                                               sem("ld_odd"), sem("ld_late"))
    stored = sem("stored")
    pool_step, pool_const, pool_spw = sem("pool_step"), sem("pool_const"), sem("pool_spw")
    dve_step, act_step = sem("dve_step"), sem("act_step")
    dve_const = sem("dve_const")
    gains_t, gains_ready = sem("gains_t"), sem("gains_ready")
    spw_t, spw_ready = sem("spw_t"), sem("spw_ready")
    sq_act, sq_dve, var_ready, sd_ready, rstd_ready = (sem("sq_act"), sem("sq_dve"), sem("var_ready"),
                                                       sem("sd_ready"), sem("rstd_ready"))
    xn_act, xn_dve = sem("xn_act"), sem("xn_dve")
    norm_t = sem("norm_t")
    xT_hi_ready, xT_lo_ready = sem("xT_hi_ready"), sem("xT_lo_ready")
    v_gelu = sem("v_gelu")
    ln_var, ln_sd, vn_ready = sem("ln_var"), sem("ln_sd"), sem("vn_ready")
    uT_ready, acT_ready, hc_ready = sem("uT_ready"), sem("acT_ready"), sem("hc_ready")
    mix_done, y_ready, yT_hi_ready, yT_lo_ready = sem("mix_done"), sem("y_ready"), sem("yT_hi_ready"), sem("yT_lo_ready")
    acc_done, h_added = sem("acc_done"), sem("h_added")
    silu_ready, act_ready = sem("silu_ready"), sem("act_ready")
    fT_hi_ready, fT_lo_ready = sem("fT_hi_ready"), sem("fT_lo_ready")
    red_ready, trig_ready = sem("red_ready"), sem("trig_ready")
    qkv_ready, rope_ready = sem("qkv_ready"), sem("rope_ready")
    qk_t, qkT_act, qkT_dve = sem("qk_t"), sem("qkT_act"), sem("qkT_dve")
    s_done, max_ready, probs_ready = sem("s_done"), sem("max_ready"), sem("probs_ready")
    probs_t, probsT_ready, pv_done = sem("probs_t"), sem("probsT_ready"), sem("pv_done")
    sink_arg, sink_ready, o_ready = sem("sink_arg"), sem("sink_ready"), sem("o_ready")
    h_final = sem("h_final")
    logits_done, diff_ready, p2_ready = sem("logits_done"), sem("diff_ready"), sem("p2_ready")
    xTr_ready, sel_ready, rank_done, routed = sem("xTr_ready"), sem("sel_ready"), sem("rank_done"), sem("routed")
    pick_ready, pickg_ready, pickg_t, pickgT_ready = sem("pick_ready"), sem("pickg_ready"), sem("pickg_t"), sem("pickgT_ready")
    gathered, gT_hi_ready, gT_lo_ready = sem("gathered"), sem("gT_hi_ready"), sem("gT_lo_ready")
    e_silu, e_act, e_t = sem("e_silu"), sem("e_act"), sem("e_t")
    eT_hi_ready, eT_lo_ready = sem("eT_hi_ready"), sem("eT_lo_ready")
    ey_act, ey_dve, scattered = sem("ey_act"), sem("ey_dve"), sem("scattered")
    e_added = sem("e_added")

    x_v = x[0].rearrange("(a p) d -> p a d", p=P)
    out_v = out[0].rearrange("(a p) d -> p a d", p=P)

    def rows(w, k0, nk, c0, ncol):
        return w[k0 * P:(k0 + nk) * P, c0:c0 + ncol].rearrange("(k p) n -> p k n", p=P)

    def spread(v, n):
        return v.rearrange("(o n) -> o n", o=1).broadcast_to([P, n])

    def front_source(p):
        if p < U0:
            return rows(ev_w_in[0], 4 * (p - V0), 4, 3 * CONV + GM, GM), 4
        if p < WOUT0:
            first = {U0: 3 * CONV, C0: CONV, X0: 2 * CONV, B0: 0}[p - p % 2]
            return rows(ev_w_in[0], 0, KT, first + 256 * (p % 2), 256), KT
        if p < FFN0:
            return rows(ev_w_out[0], OUT_KT[2 * (p - WOUT0)], 2, 0, D), 2
        if p < QKV0:
            for u in range(FU):
                g, up, d = ffn_pieces(u)
                if p == g:
                    return rows(ev_ffn_wg[0], 0, KT, 256 * u, 256), KT
                if p == up:
                    return rows(ev_ffn_wu[0], 0, KT, 256 * u, 256), KT
                if p == d:
                    return rows(ev_ffn_wd[0], 2 * u, 2, 0, D), 2
        if p == QKV0:
            return rows(od_w_qkv[0], 0, KT, NQ * HD, 2 * NKV * HD), KT
        if p < WO0:
            c, k = divmod(p - QKV0 - 1, 2)
            return rows(od_w_qkv[0], 4 * k, 4, N * c, N), 4
        return rows(od_w_o[0], 2 * (p - WO0), 2, 0, D), 2

    def hi(p, nk):
        return w_hi[:, p % SPLITS, :].rearrange("p (k n) -> p k n", k=nk)

    def lo(p, nk):
        return w_lo[:, p % SPLITS, :].rearrange("p (k n) -> p k n", k=nk)

    ACC = (2, 3, 6, 7)
    NORM_BANKS = (0, 1, 4, 5)
    WO_ACC = (0, 1, 4, 5)
    block = ctx.enter_context(nc.Block())

    @block.sync
    def _(sp):
        sp.dma_start(h[:, 0, :], x_v[:, 0, :]).then_inc(ld_x, 16)
        sp.dma_start(h[:, 1, :], x_v[:, 1, :]).then_inc(ld_x, 16)
        for p in range(FRONT):
            if p >= RING_A:
                sp.wait_ge(lo_ready, p - RING_A + 1)
            src, nk = front_source(p)
            sp.dma_start(ring_a[p % RING_A][:].rearrange("p (k n) -> p k n", k=nk), src).then_inc(
                landed[p % RING_A], 16)

        def expert_load(wait, e, q):
            for j in range(EU):
                g, up, d = expert_pieces(j)
                for w, first in ((od_exp_wg, g), (od_exp_wu, up)):
                    if first <= q < first + 2:
                        src = w[0][bass.ds(e, 1), (q - first) * 4 * P:(q - first + 1) * 4 * P, N * j:N * j + N]
                        src, nk = src.rearrange("o (k p) n -> p (o k) n", p=P), 4
                if d <= q < d + 2:
                    r0 = N * j + 2 * P * (q - d)
                    src = od_exp_wd[0][bass.ds(e, 1), r0:r0 + 2 * P, :]
                    src, nk = src.rearrange("o (k p) n -> p (o k) n", p=P), 2
            if wait is not None:
                sp.wait_ge(lo_ready, wait)
            sp.dma_start(ring[q % RING][:].rearrange("p (k n) -> p k n", k=nk), src).then_inc(landed[q % RING], 16)

        for q in range(RING):
            if q == RING_A:
                sp.wait_ge(h_added, 12)
            expert_load(FRONT + q - RING_A + 1 if q < RING_A else None, 0, q)
        for q in range(RING, EP):
            expert_load(FRONT + q - RING + 1, 0, q)
        with sp.Fori(1, NE) as e:
            for q in range(EP):
                expert_load(e * EP + (FRONT + q - RING + 1), e, q)
        sp.wait_ge(routed, 1)
        most = nc.sync.value_load(count_max[0:1, 0:1], min_val=0, max_val=T)
        with sp.If(most > P):
            with sp.Fori(0, NE) as e:
                for q in range(EP):
                    expert_load(e * EP + (NE * EP + FRONT + q - RING + 1), e, q)
        for a in range(TT):
            sp.wait_ge(h_final, a + 2)
            sp.dma_start(out_v[:, a, :], xn[:, a, :]).then_inc(stored, 16)
        sp.wait_ge(stored, 16 * TT)

    @block.gpsimd
    def _(pool):
        nc.gpsimd.memset(ident[:], 0.0).then_inc(pool_step, 1)
        nc.gpsimd.memset(ones[:], 1.0).then_inc(pool_step, 1)
        pool.wait_ge(pool_step, 2)
        nc.gpsimd.affine_select(out=ident[:], in_=ident[:], compare_op=ALU.not_equal, fill=1.0, base=0,
                                pattern=[[-1, P]], channel_multiplier=1).then_inc(pool_const, 1)
        nc.gpsimd.affine_select(out=tri[:], in_=ones[:], compare_op=ALU.is_ge, fill=0.0, base=0,
                                pattern=[[1, P]], channel_multiplier=-1).then_inc(pool_const, 1)
        nc.gpsimd.iota(iota_s[:], pattern=[[1, P]], base=0, channel_multiplier=0,
                       allow_small_or_imprecise_dtypes=True).then_inc(pool_const, 1)
        pool.wait_ge(ld_even, 16 * 5)
        nc.gpsimd.affine_select(out=sp_w[:], in_=sp_w[:], compare_op=ALU.is_ge, fill=0.0, base=0,
                                pattern=[[0, GH], [-1, P]], channel_multiplier=1).then_inc(pool_spw, 1)
        pool.wait_ge(h_added, 4)
        nc.gpsimd.memset(mask0[:], 0.0).then_inc(pool_step, 1)
        nc.gpsimd.memset(mask1[:], 0.0).then_inc(pool_step, 1)
        nc.gpsimd.memset(ident_b[:], 0.0).then_inc(pool_step, 1)
        nc.gpsimd.memset(k_pad[:], 0.0).then_inc(pool_step, 1)
        for k in range(RH):
            nc.gpsimd.memset(inv_freq[:, k:k + 1], float(np.float32(THETA ** (-2.0 * k / ROPE)))).then_inc(pool_step, 1)
        pool.wait_ge(pool_step, 6 + RH)
        nc.gpsimd.affine_select(out=ident_b[:], in_=ident_b[:], compare_op=ALU.not_equal, fill=1.0, base=0,
                                pattern=[[-1, P]], channel_multiplier=1).then_inc(pool_const, 1)
        nc.gpsimd.affine_select(out=mask0[:], in_=mask0[:], compare_op=ALU.is_ge, fill=MASKED, base=0,
                                pattern=[[0, 4], [-1, P]], channel_multiplier=1).then_inc(pool_const, 1)
        nc.gpsimd.affine_select(out=mask1[:, :, 0:P], in_=mask1[:, :, 0:P], compare_op=ALU.is_gt, fill=MASKED,
                                base=0, pattern=[[0, 2], [1, P]], channel_multiplier=-1).then_inc(pool_const, 1)
        nc.gpsimd.affine_select(out=mask1[:, :, P:T], in_=mask1[:, :, P:T], compare_op=ALU.is_ge, fill=MASKED,
                                base=0, pattern=[[0, 2], [-1, P]], channel_multiplier=1).then_inc(pool_const, 1)

    @block.scalar
    def _(act):
        for i, g in enumerate((ev_norm1_g, ev_norm2_g, od_norm1_g, od_norm2_g)):
            act.dma_start(gain_rows[i * KT:(i + 1) * KT, :], g[0].rearrange("(k p) -> k p", p=P)).then_inc(ld_gain, 16)
        act.dma_start(sp_w[:], ev_spatial_w[0].rearrange("h i j -> i h j")).then_inc(ld_even, 16)
        act.dma_start(ln_g[:], spread(ev_ln_g[0], GM)).then_inc(ld_even, 16)
        act.dma_start(ln_b[:], spread(ev_ln_b[0], GM)).then_inc(ld_even, 16)
        act.dma_start(sp_b[:], spread(ev_spatial_b[0].rearrange("h i -> (h i)"), GH * P).rearrange(
            "p (h i) -> p h i", h=GH)).then_inc(ld_even, 16)
        act.dma_start(conv_w[:], ev_conv_w[0].rearrange("(c p) k -> p c k", p=P)).then_inc(ld_even, 16)
        act.dma_start(router[:], od_router_w[0].rearrange("(k p) e -> p k e", p=P)).then_inc(ld_late, 16)
        act.dma_start(final_g[:], spread(final_norm_g, D)).then_inc(ld_late, 16)

        at = [0]

        def split_hi(upto):
            for p in range(at[0], upto + 1):
                act.wait_ge(landed[p % RING_A], 16 * (p // RING_A + 1))
                if p >= SPLITS:
                    act.wait_ge(piece_used, p - SPLITS + 1)
                nc.scalar.copy(w_hi[:, p % SPLITS, :], ring_a[p % RING_A][:]).then_inc(hi_ready, 1)
            at[0] = max(at[0], upto + 1)

        def norm_stats(n):
            act.wait_ge(ld_x, 32)
            if n:
                act.wait_ge(h_added, 4 * n)
                act.wait_ge(norm_t, 4 * n)
            nc.scalar.activation(xn[:, 0, :], h[:, 0, :], ACT.Square, accum_out=ssq[:, 0:1]).then_inc(sq_act, 1)
            act.wait_ge(var_ready, n + 1)
            nc.scalar.activation(sd[:], var[:], ACT.Sqrt).then_inc(sd_ready, 1)
            act.wait_ge(rstd_ready, n + 1)
            nc.scalar.activation(xn[:, 1, :], h[:, 1, :], ACT.Copy, scale=rstd[:, 1:2]).then_inc(xn_act, 1)

        def norm_hi(n):
            for k in range(KT):
                act.wait_ge(norm_t, 4 * n + k // 2 + 1)
                nc.scalar.activation(xT_hi[:, k, :], bank[NORM_BANKS[k // 2]][:, T * (k % 2):T * (k % 2) + T],
                                     ACT.Copy, scale=gains[:, n, k:k + 1]).then_inc(xT_hi_ready, 1)

        norm_stats(0)
        act.wait_ge(gains_ready, 1)
        split_hi(V0 + 1)
        norm_hi(0)
        split_hi(V0 + 1 + 2)
        for a in range(TT):
            act.wait_ge(piece_used, V0 + 2)
            nc.scalar.activation(v_act[:, a, :], bank[4 + a][:], ACT.Gelu).then_inc(v_gelu, 1)
        for c in range(2):
            split_hi(U0 + c + 2)
            act.wait_ge(piece_used, U0 + c + 1)
            nc.scalar.activation(uT[:, 2 * c:2 * c + 2, :], bank[c][:].rearrange("p (c t) -> p c t", c=2),
                                 ACT.Gelu).then_inc(uT_ready, 1)
        act.wait_ge(ln_var, 1)
        nc.scalar.activation(mv[:, :, 1], mv[:, :, 1], ACT.Sqrt).then_inc(ln_sd, 1)
        for c in range(2):
            split_hi(C0 + c + 2)
            act.wait_ge(piece_used, C0 + c + 1)
            nc.scalar.copy(acT[:, 2 * c:2 * c + 2, :], bank[2 + c][:].rearrange("p (c t) -> p c t", c=2)).then_inc(
                acT_ready, 1)
        split_hi(B0 + 1)
        for g in range(GH):
            act.wait_ge(y_ready, g + 1)
            nc.scalar.copy(yT_hi[:, CT + g, :], yT[:, g, :]).then_inc(yT_hi_ready, 1)
        split_hi(B0 + 1 + 2)
        for c in range(CT):
            act.wait_ge(y_ready, GH + c + 1)
            nc.scalar.copy(yT_hi[:, c, :], yT[:, c, :]).then_inc(yT_hi_ready, 1)
        split_hi(WOUT0 + 3)

        norm_stats(1)
        split_hi(FFN0 + 1)
        norm_hi(1)
        act.dma_start(b_qkv[:], spread(od_b_qkv[0], QKV)).then_inc(ld_odd, 16)
        act.dma_start(b_o[:], spread(od_b_o[0], D)).then_inc(ld_odd, 16)
        act.dma_start(sinks[:], spread(od_sinks[0], NQ)).then_inc(ld_odd, 16)
        for a in range(TT):
            act.dma_start(pos_i[:, a:a + 1], positions[0, P * a:P * a + P].unsqueeze(1)).then_inc(ld_odd, 16)
        for u in range(FU):
            g, up, d = ffn_pieces(u)
            split_hi(up + 2 if u < FU - 1 else up + 1)
            act.wait_ge(piece_used, g + 1)
            b = bank[(0, 4)[u % 2]]
            nc.scalar.activation(f_s[:], b[:].rearrange("p (c t) -> p c t", c=2), ACT.Silu).then_inc(silu_ready, 1)
            act.wait_ge(act_ready, u + 1)
            if u:
                act.wait_ge(piece_used, ffn_pieces(u - 1)[2] + 1)
            nc.scalar.copy(fT_hi[:], f_a[:]).then_inc(fT_hi_ready, 1)
        split_hi(QKV0 - 1)

        norm_stats(2)
        split_hi(QKV0 + 1)
        norm_hi(2)
        act.wait_ge(red_ready, 1)
        nc.scalar.activation(sin_t[:], red[:], ACT.Sin).then_inc(trig_ready, 1)
        nc.scalar.activation(cos_t[:], red_c[:], ACT.Sin).then_inc(trig_ready, 1)
        split_hi(WO0 - 1 + 2)
        for i in range(4):
            act.wait_ge(qk_t, NKV + i + 1)
            nc.scalar.copy(qT[:, 2 * i:2 * i + 2, :], bank[i][:].rearrange("p (c t) -> p c t", c=2)
                           ).then_inc(qkT_act, 1)
        for i in range(12):
            a, n, first = (0, 4, 4 * i) if i < 4 else (1, 2, 2 * (i - 4))
            act.wait_ge(max_ready, i + 1)
            if i >= 2:
                act.wait_ge(probs_t, i - 1)
            w = N // n
            for j in range(n):
                hq = first + j
                ins = nc.scalar.activation(probs[:, i % 2, w * j:w * j + w], bank[(3, 6, 7)[i % 3]][:, w * j:w * j + w],
                                           ACT.Exp, bias=neg_max[:, a, hq:hq + 1], scale=SCALE,
                                           accum_out=den[:, a, hq:hq + 1])
            ins.then_inc(probs_ready, 1)
            if i in (3, 11):
                act.wait_ge(sink_arg, a + 1)
                nc.scalar.activation(sink_e[:, a, :], sink_e[:, a, :], ACT.Exp).then_inc(sink_ready, 1)
        for k in range(KT):
            act.wait_ge(norm_t, 12 + k // 2 + 1)
            nc.scalar.copy(xT_hi[:, k, :], bank[(3, 6, 7, 2)[k // 2]][:, T * (k % 2):T * (k % 2) + T]
                           ).then_inc(xT_hi_ready, 1)
        split_hi(WO0 + 3)

        act.wait_ge(h_added, 12)
        nc.scalar.activation(xn[:, 0, :], h[:, 0, :], ACT.Square, accum_out=ssq[:, 0:1]).then_inc(sq_act, 1)
        act.wait_ge(var_ready, 4)
        nc.scalar.activation(sd[:], var[:], ACT.Sqrt).then_inc(sd_ready, 1)
        act.wait_ge(rstd_ready, 4)
        nc.scalar.activation(xn[:, 1, :], h[:, 1, :], ACT.Copy, scale=rstd[:, 1:2]).then_inc(xn_act, 1)
        for k in range(0, KT, 2):
            act.wait_ge(norm_t, 16 + k // 2 + 1)
            nc.scalar.activation(xT[:, k, :], bank[ACC[k // 2]][:, 0:T], ACT.Copy,
                                 scale=gains[:, 3, k:k + 1]).then_inc(xTr_ready, 1)
            nc.scalar.activation(xT[:, k + 1, :], bank[ACC[k // 2]][:, T:2 * T], ACT.Copy,
                                 scale=gains[:, 3, k + 1:k + 2]).then_inc(xTr_ready, 1)
        act.wait_ge(diff_ready, 1)
        nc.scalar.activation(p2[:], diff[:], ACT.Exp).then_inc(p2_ready, 1)

        def expert_hi(b, q):
            act.wait_ge(landed[q % RING], b * (16 * (EP // RING)) + 16 * (q // RING + 1 + (FRONT // RING_A if q % RING < RING_A else 0)))
            act.wait_ge(piece_used, b * EP + (FRONT + q - SPLITS + 1))
            nc.scalar.copy(w_hi[:, (FRONT + q) % SPLITS, :], ring[q % RING][:]).then_inc(hi_ready, 1)

        def gathered_hi(count):
            for k in range(KT):
                if k % 4 == 0:
                    act.wait_ge(gathered, count + k // 4 + 1)
                nc.scalar.activation(gT_hi[:, k, :], bank[2 + k // 4][:, P * (k % 4):P * (k % 4) + P], ACT.Copy,
                                     scale=gains[:, 3, k:k + 1]).then_inc(gT_hi_ready, 1)

        def expert_block(b):
            done = 0
            for j in range(EU):
                g, up, d = expert_pieces(j)
                if j:
                    while done < g + 2 + 2:
                        expert_hi(b, done)
                        done += 1
                    act.wait_ge(e_t, b * EU + j)
                    nc.scalar.copy(eT_hi[:], bank[6][:].rearrange("p (k s) -> p k s", k=4)).then_inc(eT_hi_ready, 1)
                while done < min(up + 2 + 2, EP):
                    expert_hi(b, done)
                    done += 1
                act.wait_ge(piece_used, b * EP + (FRONT + g + 2))
                nc.scalar.activation(e_s[:], bank[2 * (j % 2)][:], ACT.Silu).then_inc(e_silu, 1)
            while done < EP:
                expert_hi(b, done)
                done += 1
            gathered_hi(b * 2 + 2)
            act.wait_ge(e_t, b * EU + EU)
            nc.scalar.copy(eT_hi[:], bank[6][:].rearrange("p (k s) -> p k s", k=4)).then_inc(eT_hi_ready, 1)
            act.wait_ge(piece_used, b * EP + (FRONT + EP))
            nc.scalar.copy(e_y[:, 0:N], bank[4][:]).then_inc(ey_act, 1)

        act.wait_ge(routed, 1)
        gathered_hi(0)
        with act.Fori(0, NE) as b:
            expert_block(b)
        most = nc.scalar.value_load(count_max[0:1, 0:1], min_val=0, max_val=T)
        with act.If(most > P):
            with act.Fori(NE, BLOCKS) as b:
                expert_block(b)
        act.wait_ge(h_final, 1)
        nc.scalar.activation(xn[:, 0, :], h[:, 0, :], ACT.Square, accum_out=ssq[:, 0:1]).then_inc(sq_act, 1)
        act.wait_ge(var_ready, 5)
        nc.scalar.activation(sd[:], var[:], ACT.Sqrt).then_inc(sd_ready, 1)

    @block.vector
    def _(dve):
        steps = [0]

        def then(ins):
            steps[0] += 1
            ins.then_inc(dve_step, 1)
            dve.wait_ge(dve_step, steps[0])

        at = [0]

        def split_lo(upto):
            for p in range(at[0], upto + 1):
                dve.wait_ge(hi_ready, p + 1)
                nc.vector.tensor_tensor(w_lo[:, p % SPLITS, :], ring_a[p % RING_A][:],
                                        w_hi[:, p % SPLITS, :].bitcast(F32), ALU.subtract).then_inc(lo_ready, 1)
            at[0] = max(at[0], upto + 1)

        def norm_stats(n, scale_rows=True):
            dve.wait_ge(ld_x, 32)
            if n:
                dve.wait_ge(h_added, 4 * n)
                dve.wait_ge(norm_t, 4 * n)
            nc.vector.tensor_tensor_reduce(out=xn[:, 1, :], in0=h[:, 1, :], in1=h[:, 1, :], scale=1.0, scalar=0.0,
                                           op0=ALU.mult, op1=ALU.add, accum_out=ssq[:, 1:2]).then_inc(sq_dve, 1)
            dve.wait_ge(sq_dve, n + 1)
            dve.wait_ge(sq_act, n + 1)
            nc.vector.tensor_scalar(var[:], ssq[:], 1.0 / D, EPS, ALU.mult, ALU.add).then_inc(var_ready, 1)
            dve.wait_ge(sd_ready, n + 1)
            nc.vector.reciprocal(rstd[:], sd[:]).then_inc(rstd_ready, 1)
            dve.wait_ge(rstd_ready, n + 1)
            nc.vector.tensor_scalar(xn[:, 0, :], h[:, 0, :], rstd[:, 0:1], None, ALU.mult).then_inc(xn_dve, 1)

        def norm_lo(n):
            for k in range(KT):
                dve.wait_ge(xT_hi_ready, KT * n + k - k % 2 + 2)
                nc.vector.scalar_tensor_tensor(out=xT_lo[:, k, :], in0=bank[NORM_BANKS[k // 2]][:, T * (k % 2):T * (k % 2) + T],
                                               scalar=gains[:, n, k:k + 1], in1=xT_hi[:, k, :].bitcast(F32),
                                               op0=ALU.mult, op1=ALU.subtract).then_inc(xT_lo_ready, 1)

        def add_to_h(n, last, banks, a, half):
            if (a, half) == (1, 1):
                dve.wait_ge(piece_used, last + 1)
            else:
                dve.wait_ge(acc_done, 3 * n + 2 * a + half + 1)
            hs = h[:, a, N * half:N * half + N]
            nc.vector.tensor_tensor(hs, hs, bank[banks[2 * a + half]][:], ALU.add).then_inc(h_added, 1)

        nc.vector.memset(hc[:, :, 0:CW - 1], 0.0).then_inc(dve_const, 1)
        norm_stats(0)
        dve.wait_ge(gains_t, 1)
        nc.vector.tensor_copy(gains[:].rearrange("p a k -> p (a k)"), bank[7][:, 0:4 * KT]).then_inc(gains_ready, 1)
        dve.wait_ge(gains_ready, 1)
        split_lo(V0 + 1)
        norm_lo(0)
        dve.wait_ge(spw_t, 1)
        nc.vector.tensor_copy(sp_wT[:], bank[6][:].rearrange("p (h i) -> p h i", h=GH)).then_inc(spw_ready, 1)
        split_lo(V0 + 1 + 2)
        dve.wait_ge(ld_even, 16 * 5)
        for a in range(TT):
            dve.wait_ge(v_gelu, a + 1)
            then(nc.vector.bn_stats(bn[:, a, :], v_act[:, a, :]))
            then(nc.vector.bn_aggr(mv[:, a, :], bn[:, a, :]))
        nc.vector.tensor_scalar(mv[:, :, 1], mv[:, :, 1], EPS, None, ALU.add).then_inc(ln_var, 1)
        split_lo(U0 + 1 + 2)
        dve.wait_ge(ln_sd, 1)
        then(nc.vector.reciprocal(mv[:, :, 1], mv[:, :, 1]))
        for a in range(TT):
            then(nc.vector.tensor_scalar(v_act[:, a, :], v_act[:, a, :], mv[:, a, 0:1], mv[:, a, 1:2], ALU.subtract, ALU.mult))
            then(nc.vector.tensor_tensor(v_act[:, a, :], v_act[:, a, :], ln_g[:], ALU.mult))
            nc.vector.tensor_tensor(v_act[:, a, :], v_act[:, a, :], ln_b[:], ALU.add).then_inc(vn_ready, 1)
        split_lo(X0 + 2)
        for c in range(2):
            split_lo(X0 + c + 2)
            dve.wait_ge(acT_ready, c + 1)
            dve.wait_ge(piece_used, X0 + c + 1)
            nc.vector.tensor_tensor(hc[:, 2 * c:2 * c + 2, CW - 1:], acT[:, 2 * c:2 * c + 2, :],
                                    bank[6 + c][:].rearrange("p (c t) -> p c t", c=2), ALU.mult).then_inc(hc_ready, 1)
        split_lo(B0 + 1)
        for g in range(GH):
            dve.wait_ge(mix_done, 1 + g // 2)
            m = bank[4 + g // 2][:, T * (g % 2):T * (g % 2) + T].rearrange("p (a i) -> p a i", a=TT)
            then(nc.vector.tensor_tensor(yT[:, g, :].rearrange("p (a i) -> p a i", a=TT), m,
                                         sp_b[:, g:g + 1, :].broadcast_to([P, TT, P]), ALU.add))
            nc.vector.tensor_tensor(yT[:, g, :], yT[:, g, :], uT[:, g, :], ALU.mult).then_inc(y_ready, 1)
            dve.wait_ge(yT_hi_ready, g + 1)
            nc.vector.tensor_tensor(yT_lo[:, CT + g, :], yT[:, g, :], yT_hi[:, CT + g, :].bitcast(F32),
                                    ALU.subtract).then_inc(yT_lo_ready, 1)
        split_lo(B0 + 1 + 2)
        dve.wait_ge(dve_const, 1)
        dve.wait_ge(hc_ready, 2)
        dve.wait_ge(yT_lo_ready, GH)
        for c in range(CT):
            then(nc.vector.tensor_scalar(cv[:, 0, :], hc[:, c, 0:T], conv_w[:, c, 0:1], None, ALU.mult))
            for k in range(1, CW):
                then(nc.vector.scalar_tensor_tensor(out=cv[:, k % 2, :], in0=hc[:, c, k:k + T], scalar=conv_w[:, c, k:k + 1],
                                                    in1=cv[:, (k - 1) % 2, :], op0=ALU.mult, op1=ALU.add))
            dve.wait_ge(piece_used, B0 + c // 2 + 1)
            nc.vector.tensor_tensor(yT[:, c, :], cv[:, 0, :], bank[c // 2][:, T * (c % 2):T * (c % 2) + T],
                                    ALU.mult).then_inc(y_ready, 1)
            dve.wait_ge(yT_hi_ready, GH + c + 1)
            nc.vector.tensor_tensor(yT_lo[:, c, :], yT[:, c, :], yT_hi[:, c, :].bitcast(F32),
                                    ALU.subtract).then_inc(yT_lo_ready, 1)
        split_lo(WOUT0 + 3)
        for a in range(TT):
            for half in range(2):
                add_to_h(0, FFN0 - 1, ACC, a, half)

        norm_stats(1)
        split_lo(FFN0 + 1)
        norm_lo(1)
        for u in range(FU):
            g, up, d = ffn_pieces(u)
            split_lo(up + 2 if u < FU - 1 else up + 1)
            dve.wait_ge(silu_ready, u + 1)
            dve.wait_ge(piece_used, up + 1)
            b = bank[(1, 5)[u % 2]]
            if u:
                dve.wait_ge(fT_lo_ready, u)
            nc.vector.tensor_tensor(f_a[:], f_s[:], b[:].rearrange("p (c t) -> p c t", c=2), ALU.mult).then_inc(act_ready, 1)
            dve.wait_ge(fT_hi_ready, u + 1)
            nc.vector.tensor_tensor(fT_lo[:], f_a[:], fT_hi[:].bitcast(F32), ALU.subtract).then_inc(fT_lo_ready, 1)
        split_lo(QKV0 - 1)
        two_pi = 2.0 * np.pi
        c1 = 6.28125
        c2 = float(np.float32(np.round((two_pi - c1) * 2.0 ** 20) / 2.0 ** 20))
        c3 = float(np.float32(two_pi - c1 - c2))
        magic = 1.5 * 2.0 ** 23
        dve.wait_ge(ld_odd, 80)
        dve.wait_ge(pool_const, 7)
        then(nc.vector.tensor_copy(pos_f[:], pos_i[:]))
        for a in range(TT):
            then(nc.vector.tensor_scalar(ang[:, a, :], inv_freq[:], pos_f[:, a:a + 1], None, ALU.mult))
        then(nc.vector.tensor_scalar(turns[:], ang[:], float(np.float32(1.0 / two_pi)), magic, ALU.mult, ALU.add))
        then(nc.vector.tensor_scalar(turns[:], turns[:], magic, None, ALU.subtract))
        for i, c in enumerate((c1, c2, c3)):
            then(nc.vector.scalar_tensor_tensor(out=red[:], in0=turns[:], scalar=-c, in1=(ang if i == 0 else red)[:],
                                                op0=ALU.mult, op1=ALU.add))
        then(nc.vector.tensor_scalar(red[:], red[:], 3.1415925, -3.1415925, ALU.min, ALU.max))
        then(nc.vector.scalar_tensor_tensor(out=red_c[:], in0=red[:], scalar=-1.0, in1=red[:], op0=ALU.mult, op1=ALU.max))
        nc.vector.tensor_scalar(red_c[:], red_c[:], -1.0, float(np.float32(np.pi / 2)), ALU.mult, ALU.add).then_inc(red_ready, 1)
        then(nc.vector.tensor_scalar(neg_sinks[:], sinks[:], -1.0, None, ALU.mult))
        for a in range(TT):
            for half in range(2):
                add_to_h(1, QKV0 - 1, ACC, a, half)

        norm_stats(2)
        split_lo(QKV0 + 1)
        norm_lo(2)
        split_lo(QKV0 + 2)
        for c, (c0, w, b0) in enumerate(((NQ * HD, 2 * NKV * HD, 0), (0, N, 2), (N, N, 6))):
            split_lo((QKV0 + 2, QKV0 + 4, QKV0 + 6)[c])
            for a in range(TT):
                dve.wait_ge(piece_used, (QKV0 + 1, QKV0 + 3, QKV0 + 5)[c])
                nc.vector.tensor_tensor(qkv[:, a, c0:c0 + w], bank[b0 + a][:, 0:w], b_qkv[:, c0:c0 + w],
                                        ALU.add).then_inc(qkv_ready, 1)
        heads = NQ + NKV
        dve.wait_ge(qkv_ready, 6)
        dve.wait_ge(trig_ready, 2)
        for a in range(TT):
            qk = qkv[:, a, 0:heads * HD].rearrange("p (h d) -> p h d", d=HD)
            t1, t2 = qk[:, :, 0:RH], qk[:, :, RH:ROPE]
            r = [rope_t[:, i, a, :].rearrange("p (h d) -> p h d", d=RH) for i in range(4)]
            cs = cos_t[:, a:a + 1, :].broadcast_to([P, heads, RH])
            sn = sin_t[:, a:a + 1, :].broadcast_to([P, heads, RH])
            nc.vector.tensor_tensor(r[0], t1, cs, ALU.mult)
            nc.vector.tensor_tensor(r[1], t2, sn, ALU.mult)
            nc.vector.tensor_tensor(r[2], t2, cs, ALU.mult)
            then(nc.vector.tensor_tensor(r[3], t1, sn, ALU.mult))
            nc.vector.tensor_tensor(t1, r[0], r[1], ALU.subtract)
            then(nc.vector.tensor_tensor(t2, r[2], r[3], ALU.add))
            kk = qkv[:, a, NQ * HD:heads * HD].rearrange("p (g d) -> p g d", d=HD)
            for i in range(2):
                nc.vector.tensor_copy(k_pad[:, a, :, i, HD * i:HD * i + HD], kk).then_inc(rope_ready, 1)
        for g in range(NKV):
            dve.wait_ge(qk_t, g + 1)
            nc.vector.tensor_copy(kT[:, g, :, :], bank[4 + g][:].rearrange("p (i t) -> p i t", i=2)).then_inc(qkT_dve, 1)

        def evacuate_probs(i):
            dve.wait_ge(probs_t, i + 1)
            if i >= 2:
                dve.wait_ge(pv_done, i - 1)
            nc.vector.tensor_copy(probsT[:, i % 2, :], bank[4 + i % 2][:]).then_inc(probsT_ready, 1)

        def normalise(a):
            dve.wait_ge(sink_ready, a + 1)
            then(nc.vector.tensor_tensor(den[:, a, :], den[:, a, :], sink_e[:, a, :], ALU.add))
            then(nc.vector.reciprocal(den[:, a, :], den[:, a, :]))
            for g in range(2):
                dve.wait_ge(pv_done, (2, 4, 8, 12)[2 * a + g])
                nc.vector.tensor_tensor(
                    o_tok[:, a, N * g:N * g + N].rearrange("p (h d) -> p h d", d=HD),
                    bank[(0, 1, 2, 0)[2 * a + g]][:].rearrange("p (h d) -> p h d", d=HD),
                    den[:, a, QPK * g:QPK * g + QPK].unsqueeze(2).broadcast_to([P, QPK, HD]), ALU.mult).then_inc(o_ready, 1)

        for i in range(12):
            a, n, first = (0, 4, 4 * i) if i < 4 else (1, 2, 2 * (i - 4))
            dve.wait_ge(s_done, i + 1)
            then(nc.vector.tensor_reduce(raw_max[:, a, first:first + n],
                                         bank[(3, 6, 7)[i % 3]][:].rearrange("p (h k) -> p h k", h=n), AX_X, ALU.max))
            nc.vector.scalar_tensor_tensor(out=neg_max[:, a, first:first + n], in0=raw_max[:, a, first:first + n],
                                           scalar=-SCALE, in1=neg_sinks[:, first:first + n], op0=ALU.mult,
                                           op1=ALU.min).then_inc(max_ready, 1)
            if i in (3, 11):
                dve.wait_ge(max_ready, i + 1)
                nc.vector.tensor_tensor(sink_e[:, a, :], neg_max[:, a, :], sinks[:], ALU.add).then_inc(sink_arg, 1)
            if i:
                evacuate_probs(i - 1)
            if i == 5:
                normalise(0)
        evacuate_probs(11)
        for a in range(TT):
            nc.vector.tensor_tensor(h[:, a, :], h[:, a, :], b_o[:], ALU.add).then_inc(dve_const, 1)
        normalise(1)
        for k in range(KT):
            dve.wait_ge(xT_hi_ready, 3 * KT + k - k % 2 + 2)
            nc.vector.tensor_tensor(xT_lo[:, k, :], bank[(3, 6, 7, 2)[k // 2]][:, T * (k % 2):T * (k % 2) + T],
                                    xT_hi[:, k, :].bitcast(F32), ALU.subtract).then_inc(xT_lo_ready, 1)
        split_lo(WO0 + 3)
        dve.wait_ge(dve_const, 1 + TT)
        for a in range(TT):
            for half in range(2):
                add_to_h(2, FRONT - 1, WO_ACC, a, half)

        norm_stats(3)
        for a in range(TT):
            dve.wait_ge(logits_done, a + 1)
            then(nc.vector.tensor_copy(logits[:, a, :], bank[a][:, 0:NE]))
            then(nc.vector.max(top_v[:, a, :], logits[:, a, :]))
            then(nc.vector.max_index(top_i[:, a, :], top_v[:, a, :], logits[:, a, :]))
        nc.vector.tensor_tensor(diff[:], top_v[:, :, 1], top_v[:, :, 0], ALU.subtract).then_inc(diff_ready, 1)
        then(nc.vector.tensor_copy(top_f[:], top_i[:, :, 0:2]))
        for a in range(TT):
            for i in range(2):
                then(nc.vector.tensor_scalar(oh[:, a, i, :], iota_s[:, 0:NE], top_f[:, a, i:i + 1], None, ALU.is_equal))
        nc.vector.tensor_tensor(sel[:], oh[:, :, 0, :], oh[:, :, 1, :], ALU.add).then_inc(sel_ready, 1)
        dve.wait_ge(p2_ready, 1)
        then(nc.vector.tensor_scalar(psum_g[:], p2[:], 1.0, None, ALU.add))
        then(nc.vector.reciprocal(g1[:], psum_g[:]))
        then(nc.vector.tensor_tensor(g2[:], p2[:], g1[:], ALU.mult))
        for a in range(TT):
            then(nc.vector.tensor_scalar(gate_of[:, a, 0:NE], oh[:, a, 0, :], g1[:, a:a + 1], None, ALU.mult))
            then(nc.vector.scalar_tensor_tensor(out=gate_of[:, a, 0:NE], in0=oh[:, a, 1, :], scalar=g2[:, a:a + 1],
                                                in1=gate_of[:, a, 0:NE], op0=ALU.mult, op1=ALU.add))
        then(nc.vector.tensor_copy(gate_of[:, :, NE:BLOCKS], gate_of[:, :, 0:NE]))
        then(nc.vector.memset(slot_of[:], -1.0))
        dve.wait_ge(rank_done, 1)
        for a in range(TT):
            then(nc.vector.tensor_tensor(slot_of[:, a, 0:NE], sel[:, a, :], bank[4][:, NE * a:NE * a + NE], ALU.mult))
        then(nc.vector.tensor_scalar(slot_of[:, :, 0:NE], slot_of[:, :, 0:NE], 1.0, None, ALU.subtract))
        then(nc.vector.tensor_scalar(slot_of[:, :, NE:BLOCKS], slot_of[:, :, 0:NE], float(P), None, ALU.subtract))
        then(nc.vector.tensor_reduce(cmax_f[:], bank[4][:, TT * NE:(TT + 1) * NE], AX_X, ALU.max))
        nc.vector.tensor_copy(count_max[:], cmax_f[:]).then_inc(routed, 1)

        def expert_lo(b, q):
            dve.wait_ge(hi_ready, b * EP + (FRONT + q + 1))
            nc.vector.tensor_tensor(w_lo[:, (FRONT + q) % SPLITS, :], ring[q % RING][:],
                                    w_hi[:, (FRONT + q) % SPLITS, :].bitcast(F32), ALU.subtract).then_inc(lo_ready, 1)

        def make_pick(blk):
            for a in range(TT):
                nc.vector.tensor_scalar(pick[:, a, :], iota_s[:], slot_of[:, a, bass.ds(blk, 1)], None,
                                        ALU.is_equal).then_inc(pick_ready, 1)

        def gathered_lo(count):
            for k in range(KT):
                dve.wait_ge(gT_hi_ready, count + (k - k % 4 + 4))
                nc.vector.scalar_tensor_tensor(out=gT_lo[:, k, :], in0=bank[2 + k // 4][:, P * (k % 4):P * (k % 4) + P],
                                               scalar=gains[:, 3, k:k + 1], in1=gT_hi[:, k, :].bitcast(F32),
                                               op0=ALU.mult, op1=ALU.subtract).then_inc(gT_lo_ready, 1)

        def hidden_lo(count):
            dve.wait_ge(eT_hi_ready, count)
            nc.vector.tensor_tensor(eT_lo[:], bank[6][:].rearrange("p (k s) -> p k s", k=4), eT_hi[:].bitcast(F32),
                                    ALU.subtract).then_inc(eT_lo_ready, 1)

        def expert_block(b):
            done = 0
            for j in range(EU):
                g, up, d = expert_pieces(j)
                if j:
                    while done < g + 2 + 2:
                        expert_lo(b, done)
                        done += 1
                    hidden_lo(b * EU + j)
                while done < min(up + 2 + 2, EP):
                    expert_lo(b, done)
                    done += 1
                dve.wait_ge(e_silu, b * EU + (j + 1))
                dve.wait_ge(piece_used, b * EP + (FRONT + up + 2))
                nc.vector.tensor_tensor(e_a[:], e_s[:], bank[2 * (j % 2) + 1][:], ALU.mult).then_inc(e_act, 1)
                if j == 3:
                    for a in range(TT):
                        nc.vector.tensor_scalar(pick_g[:, a, :], iota_s[:], slot_of[:, a, bass.ds(b, 1)],
                                                gate_of[:, a, bass.ds(b, 1)], ALU.is_equal, ALU.mult).then_inc(pickg_ready, 1)
                    make_pick(b + 1)
            while done < EP:
                expert_lo(b, done)
                done += 1
            gathered_lo(b * KT + KT)
            hidden_lo(b * EU + EU)
            dve.wait_ge(pickg_t, b + 1)
            nc.vector.tensor_copy(pick_gT[:], bank[7][:, 0:T]).then_inc(pickgT_ready, 1)
            dve.wait_ge(piece_used, b * EP + (FRONT + EP))
            nc.vector.tensor_copy(e_y[:, N:D], bank[5][:]).then_inc(ey_dve, 1)
            for i in range(4):
                dve.wait_ge(scattered, b * 4 + (i + 1))
                dve.wait_ge(e_added, b * 4 + (i + 1))
                hs = h[:, i // 2, N * (i % 2):N * (i % 2) + N]
                nc.vector.tensor_tensor(hs, hs, bank[ACC[i]][:], ALU.add).then_inc(e_added, 1)

        dve.wait_ge(routed, 1)
        make_pick(0)
        gathered_lo(0)
        nc.vector.memset(cmax_f[:], 0.0).then_inc(e_added, 1)
        with dve.Fori(0, NE) as b:
            expert_block(b)
        dve.wait_ge(e_added, 4 * NE + 1)
        most = nc.vector.value_load(count_max[0:1, 0:1], min_val=0, max_val=T)
        with dve.If(most > P):
            with dve.Fori(NE, BLOCKS) as b:
                expert_block(b)
            dve.wait_ge(e_added, 4 * BLOCKS + 1)

        nc.vector.tensor_tensor_reduce(out=xn[:, 1, :], in0=h[:, 1, :], in1=h[:, 1, :], scale=1.0, scalar=0.0,
                                       op0=ALU.mult, op1=ALU.add, accum_out=ssq[:, 1:2]).then_inc(h_final, 1)
        dve.wait_ge(h_final, 1)
        dve.wait_ge(sq_act, 5)
        nc.vector.tensor_scalar(var[:], ssq[:], 1.0 / D, EPS, ALU.mult, ALU.add).then_inc(var_ready, 1)
        dve.wait_ge(sd_ready, 5)
        then(nc.vector.reciprocal(rstd[:], sd[:]))
        dve.wait_ge(ld_late, 32)
        for a in range(TT):
            nc.vector.scalar_tensor_tensor(out=xn[:, a, :], in0=h[:, a, :], scalar=rstd[:, a:a + 1], in1=final_g[:],
                                           op0=ALU.mult, op1=ALU.mult).then_inc(h_final, 1)

    @block.tensor
    def _(pe):
        mm = nc.tensor.matmul

        def mm3(dst, weight_moves, w, t, start, stop):
            (w_h, w_l), (t_h, t_l) = w, t
            for i, (a, b) in enumerate(((w_h, t_h), (w_h, t_l), (w_l, t_h))):
                fixed, moving = (b, a) if weight_moves else (a, b)
                ins = mm(dst, fixed, moving, start=start and i == 0, stop=stop and i == 2)
            return ins

        def transpose_rows(src, banks):
            for k in range(KT):
                for a in range(TT):
                    c0 = T * (k % 2) + P * a
                    ins = nc.tensor.transpose(bank[banks[k // 2]][:, c0:c0 + P], src[:, a, P * k:P * k + P], ident[:])
                if k % 2:
                    ins.then_inc(norm_t, 1)

        def norm_transposes(n, banks):
            pe.wait_ge(xn_dve, n + 1)
            pe.wait_ge(xn_act, n + 1)
            transpose_rows(xn, banks)

        def rows_product(p, kts, xh, xl, banks, first, last):
            pe.wait_ge(lo_ready, p + 1)
            for kk, k in enumerate(kts):
                for a in range(TT):
                    for half in range(2):
                        ins = mm3(bank[banks[2 * a + half]][:], True,
                                  (hi(p, 2)[:, kk, N * half:N * half + N], lo(p, 2)[:, kk, N * half:N * half + N]),
                                  (xh[:, k, P * a:P * a + P], xl[:, k, P * a:P * a + P]),
                                  first and kk == 0, last and kk == 1)
                        if last and kk == 1 and 2 * a + half < 3:
                            ins.then_inc(acc_done, 1)
            ins.then_inc(piece_used, 1)

        def columns_product(p, dst):
            pe.wait_ge(lo_ready, p + 1)
            for c in range(2):
                for k in range(KT):
                    ins = mm3(dst[:, T * c:T * c + T], False,
                              (hi(p, KT)[:, k, P * c:P * c + P], lo(p, KT)[:, k, P * c:P * c + P]),
                              (xT_hi[:, k, :], xT_lo[:, k, :]), k == 0, k == KT - 1)
            ins.then_inc(piece_used, 1)

        def tokens_product(p, k0, nk, w, banks):
            pe.wait_ge(lo_ready, p + 1)
            for a in range(TT):
                for kk in range(nk):
                    k = k0 + kk
                    ins = mm3(bank[banks[a]][:, 0:w], True, (hi(p, nk)[:, kk, :], lo(p, nk)[:, kk, :]),
                              (xT_hi[:, k, P * a:P * a + P], xT_lo[:, k, P * a:P * a + P]), k == 0, k == KT - 1)
            ins.then_inc(piece_used, 1)

        pe.wait_ge(pool_const, 3)
        pe.wait_ge(ld_gain, 64)
        nc.tensor.transpose(bank[7][:, 0:4 * KT], gain_rows[:], ident[0:4 * KT, 0:4 * KT]).then_inc(gains_t, 1)
        norm_transposes(0, NORM_BANKS)
        pe.wait_ge(pool_spw, 1)
        for g in range(GH):
            ins = nc.tensor.transpose(bank[6][:, P * g:P * g + P], sp_w[:, g, :], ident[:])
        ins.then_inc(spw_t, 1)
        pe.wait_ge(xT_lo_ready, KT)
        for i in range(2):
            tokens_product(V0 + i, 4 * i, 4, N, (4, 5))
        for c in range(2):
            columns_product(U0 + c, bank[c])
        for c in range(2):
            columns_product(C0 + c, bank[2 + c])
        pe.wait_ge(spw_ready, 1)
        pe.wait_ge(gains_ready, 1)
        for c in range(2):
            columns_product(X0 + c, bank[6 + c])
        pe.wait_ge(vn_ready, TT)
        for g in range(GH):
            for a in range(TT):
                c0 = T * (g % 2) + P * a
                ins = mm(bank[4 + g // 2][:, c0:c0 + P], v_act[:, a, P * g:P * g + P], sp_wT[:, g, :],
                         start=True, stop=True)
            if g % 2:
                ins.then_inc(mix_done, 1)
        pe.wait_ge(uT_ready, 2)
        for c in range(2):
            columns_product(B0 + c, bank[c])
        for i in range(4):
            pe.wait_ge(yT_lo_ready, GH if i < 2 else GH + CT)
            rows_product(WOUT0 + i, OUT_KT[2 * i:2 * i + 2], yT_hi, yT_lo, ACC, i == 0, i == 3)

        def ffn_down(u):
            pe.wait_ge(fT_lo_ready, u + 1)
            rows_product(ffn_pieces(u)[2], (0, 1), fT_hi, fT_lo, ACC, u == 0, u == FU - 1)

        norm_transposes(1, NORM_BANKS)
        pe.wait_ge(xT_lo_ready, 2 * KT)
        for u in range(FU):
            g, up, _ = ffn_pieces(u)
            if u >= 2:
                pe.wait_ge(act_ready, u - 1)
            columns_product(g, bank[(0, 4)[u % 2]])
            columns_product(up, bank[(1, 5)[u % 2]])
            if u:
                ffn_down(u - 1)
        ffn_down(FU - 1)

        norm_transposes(2, NORM_BANKS)
        pe.wait_ge(xT_lo_ready, 3 * KT)
        tokens_product(QKV0, 0, KT, 2 * NKV * HD, (0, 1))
        for c in range(2):
            for i in range(2):
                tokens_product(QKV0 + 1 + 2 * c + i, 4 * i, 4, N, ((2, 3), (6, 7))[c])
        pe.wait_ge(rope_ready, 4)
        for g in range(NKV):
            for i in range(2):
                for a in range(TT):
                    ins = nc.tensor.transpose(bank[4 + g][:, T * i + P * a:T * i + P * a + P], k_pad[:, a, g, i, :], ident[:])
            ins.then_inc(qk_t, 1)
        for i in range(4):
            for c in range(2):
                for a in range(TT):
                    hp = 2 * i + c
                    ins = nc.tensor.transpose(bank[i][:, T * c + P * a:T * c + P * a + P],
                                              qkv[:, a, P * hp:P * hp + P], ident[:])
            ins.then_inc(qk_t, 1)

        def scores(i):
            a, n, first = (0, 4, 4 * i) if i < 4 else (1, 2, 2 * (i - 4))
            if i >= 3:
                pe.wait_ge(probs_ready, i - 2)
            s, w = bank[(3, 6, 7)[i % 3]], N // n
            mask = mask0 if a == 0 else mask1
            mm(s[:], ident_b[:], mask[:].rearrange("p h k -> p (h k)"), start=True, stop=False)
            for j in range(n):
                hq = first + j
                ins = mm(s[:, w * j:w * j + w], qT[:, hq // 2, P * a:P * a + P], kT[:, hq // QPK, hq % 2, 0:w],
                         start=False, stop=j == n - 1)
            ins.then_inc(s_done, 1)

        def transpose_probs(i):
            pe.wait_ge(probs_ready, i + 1)
            if i >= 2:
                pe.wait_ge(probsT_ready, i - 1)
            for c in range(4):
                ins = nc.tensor.transpose(bank[4 + i % 2][:, P * c:P * c + P], probs[:, i % 2, P * c:P * c + P], ident[:])
            ins.then_inc(probs_t, 1)

        def weigh_values(i):
            a, n, first = (0, 4, 4 * i) if i < 4 else (1, 2, 2 * (i - 4))
            pe.wait_ge(probsT_ready, i + 1)
            if i == 8:
                pe.wait_ge(o_ready, 2)
            for j in range(n):
                hq = first + j
                o = bank[(0, 1, 2, 0)[2 * a + hq // QPK]][:, HD * (hq % QPK):HD * (hq % QPK) + HD]
                v0 = (NQ + NKV + hq // QPK) * HD
                for kt in range(a + 1):
                    c = (a + 1) * j + kt
                    ins = mm(o, probsT[:, i % 2, P * c:P * c + P], qkv[:, kt, v0:v0 + HD], start=kt == 0, stop=kt == a)
            ins.then_inc(pv_done, 1)

        pe.wait_ge(pool_const, 7)
        pe.wait_ge(qkT_act, 4)
        pe.wait_ge(qkT_dve, NKV)
        for i in range(14):
            if i < 12:
                scores(i)
            if 1 <= i < 13:
                transpose_probs(i - 1)
            if i >= 2:
                weigh_values(i - 2)
        pe.wait_ge(o_ready, 4)
        transpose_rows(o_tok, (3, 6, 7, 2))
        pe.wait_ge(xT_lo_ready, 4 * KT)
        for i in range(4):
            rows_product(WO0 + i, (2 * i, 2 * i + 1), xT_hi, xT_lo, WO_ACC, i == 0, i == 3)

        norm_transposes(3, ACC)
        pe.wait_ge(xTr_ready, KT)
        pe.wait_ge(ld_late, 32)
        for a in range(TT):
            for k in range(KT):
                ins = mm(bank[a][:, 0:NE], xT[:, k, P * a:P * a + P], router[:, k, :], start=k == 0, stop=k == KT - 1)
            ins.then_inc(logits_done, 1)
        pe.wait_ge(sel_ready, 1)
        r = bank[4]
        mm(r[:, 0:NE], tri[:], sel[:, 0, :], start=True, stop=True)
        mm(r[:, NE:2 * NE], ones[:], sel[:, 0, :], start=True, stop=False)
        mm(r[:, NE:2 * NE], tri[:], sel[:, 1, :], start=False, stop=True)
        mm(r[:, 2 * NE:3 * NE], ones[:], sel[:, 0, :], start=True, stop=False)
        mm(r[:, 2 * NE:3 * NE], ones[:], sel[:, 1, :], start=False, stop=True).then_inc(rank_done, 1)

        def gather():
            for k in range(KT):
                for a in range(TT):
                    ins = mm(bank[2 + k // 4][:, P * (k % 4):P * (k % 4) + P], xn[:, a, P * k:P * k + P], pick[:, a, :],
                             start=a == 0, stop=a == TT - 1)
                if k % 4 == 3:
                    ins.then_inc(gathered, 1)

        def expert_in(b, q, k0, dst):
            s = FRONT + q
            pe.wait_ge(lo_ready, b * EP + (s + 1))
            for kk in range(4):
                k = k0 + kk
                ins = mm3(dst[:], True, (hi(s, 4)[:, kk, :], lo(s, 4)[:, kk, :]), (gT_hi[:, k, :], gT_lo[:, k, :]),
                          k == 0, k == KT - 1)
            ins.then_inc(piece_used, 1)

        def expert_down(b, j):
            d = expert_pieces(j)[2]
            pe.wait_ge(eT_lo_ready, b * EU + (j + 1))
            for i in range(2):
                s = FRONT + d + i
                pe.wait_ge(lo_ready, b * EP + (s + 1))
                for kk in range(2):
                    k = 2 * i + kk
                    for half in range(2):
                        ins = mm3(bank[4 + half][:], True,
                                  (hi(s, 2)[:, kk, N * half:N * half + N], lo(s, 2)[:, kk, N * half:N * half + N]),
                                  (eT_hi[:, k, :], eT_lo[:, k, :]), j == 0 and k == 0, j == EU - 1 and k == 3)
                ins.then_inc(piece_used, 1)

        def transpose_hidden(b, j):
            pe.wait_ge(e_act, b * EU + (j + 1))
            for k in range(4):
                ins = nc.tensor.transpose(bank[6][:, P * k:P * k + P], e_a[:, P * k:P * k + P], ident[:])
            ins.then_inc(e_t, 1)

        def expert_block(b):
            pe.wait_ge(gT_lo_ready, b * KT + KT)
            for j in range(EU):
                g, up, _ = expert_pieces(j)
                if j == 1:
                    pe.wait_ge(e_added, b * 4 + 1)
                if j >= 2:
                    pe.wait_ge(e_act, b * EU + (j - 1))
                for i in range(2):
                    expert_in(b, g + i, 4 * i, bank[2 * (j % 2)])
                if j:
                    transpose_hidden(b, j - 1)
                for i in range(2):
                    expert_in(b, up + i, 4 * i, bank[2 * (j % 2) + 1])
                if j:
                    expert_down(b, j - 1)
            pe.wait_ge(pick_ready, b * TT + 2 * TT)
            gather()
            pe.wait_ge(pickg_ready, b * TT + TT)
            for a in range(TT):
                ins = nc.tensor.transpose(bank[7][:, P * a:P * a + P], pick_g[:, a, :], ident[:])
            ins.then_inc(pickg_t, 1)
            transpose_hidden(b, EU - 1)
            expert_down(b, EU - 1)
            pe.wait_ge(pickgT_ready, b + 1)
            pe.wait_ge(gT_lo_ready, b * KT + 2 * KT)
            pe.wait_ge(ey_act, b + 1)
            pe.wait_ge(ey_dve, b + 1)
            for i in range(4):
                a, half = i // 2, i % 2
                mm(bank[ACC[i]][:], pick_gT[:, P * a:P * a + P], e_y[:, N * half:N * half + N],
                   start=True, stop=True).then_inc(scattered, 1)

        pe.wait_ge(pick_ready, TT)
        gather()
        with pe.Fori(0, NE) as b:
            expert_block(b)
        most = nc.tensor.value_load(count_max[0:1, 0:1], min_val=0, max_val=T)
        with pe.If(most > P):
            with pe.Fori(NE, BLOCKS) as b:
                expert_block(b)

    ctx.close()


_INS = ['x', 'positions', 'final_norm_g', 'ev_norm1_g', 'ev_w_in', 'ev_conv_w', 'ev_ln_g', 'ev_ln_b',
        'ev_spatial_w', 'ev_spatial_b', 'ev_w_out', 'ev_norm2_g', 'ev_ffn_wg', 'ev_ffn_wu', 'ev_ffn_wd',
        'od_norm1_g', 'od_w_qkv', 'od_b_qkv', 'od_sinks', 'od_w_o', 'od_b_o', 'od_norm2_g', 'od_router_w',
        'od_exp_wg', 'od_exp_wu', 'od_exp_wd']


def kernel(**inputs):
    import concourse.bacc as bacc
    from concourse.bass_utils import run_bass_kernel_spmd

    nc = bacc.Bacc("TRN2", target_bir_lowering=False, num_devices=1)
    arrays, args = {}, []
    for name in _INS:
        a = np.ascontiguousarray(inputs[name])
        arrays[f"in_{name}"] = a
        args.append(nc.dram_tensor(f"in_{name}", a.shape, mybir.dt.from_np(a.dtype), kind="ExternalInput").ap())
    out = nc.dram_tensor("out_0", (1, T, D), F32, kind="ExternalOutput").ap()
    build(nc, *args, out)
    return run_bass_kernel_spmd(nc, [arrays], core_ids=[0]).results[0]["out_0"]
```

```python
from contextlib import ExitStack

import numpy as np

import concourse.bass as bass
from concourse import mybir

ALU = mybir.AluOpType
ACT = mybir.ActivationFunctionType
F32 = mybir.dt.float32
F32R = mybir.dt.float32r
BF16 = mybir.dt.bfloat16
I32 = mybir.dt.int32
U32 = mybir.dt.uint32
AX_X = mybir.AxisListType.X

P = 128
D = 1024
KT = D // P
T = 256
TT = T // P
EPS = 1e-5
N = 512

CONV = 512
CT = CONV // P
CW = 3
GM = 512
MIX_IN = 3 * CONV + 2 * GM
GH = 4
FFN = 2816
FU = FFN // 256

HD = 64
NQ = 16
NKV = 2
QPK = NQ // NKV
QKV = (NQ + 2 * NKV) * HD
ROPE = HD // 4
RH = ROPE // 2
THETA = 500000.0
SCALE = HD ** -0.5
MASKED = -1e30

NE = 8
ED = 3584
EU = ED // N
BLOCKS = 2 * NE

PIECE = 2048
SPLITS = 3
RING_A = 7
RING = 14
AHEAD = 2
EP = 6 * EU

V0, U0, C0, X0, B0 = 0, 2, 4, 6, 8
WOUT0 = 10
FFN0 = WOUT0 + 4
QKV0 = FFN0 + 3 * FU
WO0 = QKV0 + 5
FRONT = WO0 + 4
OUT_KT = (4, 5, 6, 7, 0, 1, 2, 3)

assert FRONT % RING_A == 0 and EP % RING == 0 and EP % SPLITS == 0


def ffn_pieces(u):
    g = FFN0 + (0 if u == 0 else 3 * u - 1)
    d = FFN0 + 3 * u + 4 if u < FU - 1 else FFN0 + 3 * FU - 1
    return g, g + 1, d


def expert_pieces(j):
    g = 0 if j == 0 else 6 * j - 2
    d = 6 * j + 8 if j < EU - 1 else EP - 2
    return g, g + 2, d


def build(nc, x, positions, final_norm_g, ev_norm1_g, ev_w_in, ev_conv_w, ev_ln_g, ev_ln_b,
          ev_spatial_w, ev_spatial_b, ev_w_out, ev_norm2_g, ev_ffn_wg, ev_ffn_wu, ev_ffn_wd,
          od_norm1_g, od_w_qkv, od_b_qkv, od_sinks, od_w_o, od_b_o, od_norm2_g, od_router_w,
          od_exp_wg, od_exp_wu, od_exp_wd, out):
    ctx = ExitStack()

    def sb(name, shape, dt=F32, scope=None):
        return (scope or ctx).enter_context(nc.sbuf_tensor(name, shape, dt))

    def sem(name):
        return ctx.enter_context(nc.semaphore(name))

    ring_a = [sb(f"ring{s}", [P, PIECE]) for s in range(RING_A)]
    w_hi = sb("w_hi", [P, SPLITS, PIECE], F32R)
    w_lo = sb("w_lo", [P, SPLITS, PIECE], F32R)
    h = sb("h", [P, TT, D])
    xn = sb("xn", [P, TT, D])
    ident = sb("ident", [P, P])
    gain = sb("gain", [P, 2, D])
    ssq = sb("ssq", [P, TT])
    var = sb("var", [P, TT])
    newton = sb("newton", [P, TT])
    rstd = sb("rstd", [P, TT])
    router = sb("router", [P, KT, NE])
    ones = sb("ones", [P, P])
    tri = sb("tri", [P, P])
    iota_s = sb("iota_s", [P, P])
    cmax_f = sb("cmax_f", [P, 1])
    count_max = sb("count_max", [P, 1], I32)
    slot_of = sb("slot_of", [P, TT, BLOCKS + 1])
    gate_of = sb("gate_of", [P, TT, BLOCKS])

    s1 = ExitStack()
    xT_hi = sb("xT_hi", [P, KT, T], F32R, s1)
    xT_lo = sb("xT_lo", [P, KT, T], F32R, s1)
    m_ = ExitStack()
    yT_hi = sb("yT_hi", [P, KT, T], F32R, m_)
    yT_lo = sb("yT_lo", [P, KT, T], F32R, m_)
    yT = sb("yT", [P, 4, T], F32, m_)
    v_act = sb("v_act", [P, TT, GM], F32, m_)
    uT = sb("uT", [P, GH, T], F32, m_)
    acT = sb("acT", [P, CT, T], F32, m_)
    hc = sb("hc", [P, CT, T + CW - 1], F32, m_)
    cv = sb("cv", [P, CT, T], F32, m_)
    ln_g = sb("ln_g", [P, GM], F32, m_)
    ln_b = sb("ln_b", [P, GM], F32, m_)
    sp_w = sb("sp_w", [P, GH, P], F32, m_)
    sp_wT = sb("sp_wT", [P, GH, P], F32, m_)
    sp_b = sb("sp_b", [P, GH, P], F32, m_)
    conv_w = sb("conv_w", [P, CT, CW], F32, m_)
    bn = sb("bn", [P, TT, 6], F32, m_)
    mv = sb("mv", [P, TT, 2], F32, m_)
    m_.close()

    f_ = ExitStack()
    f_s = sb("f_s", [P, 2, T], F32, f_)
    f_a = sb("f_a", [P, 2, T], F32, f_)
    fT_hi = sb("fT_hi", [P, 2, 2, T], F32R, f_)
    fT_lo = sb("fT_lo", [P, 2, 2, T], F32R, f_)
    f_.close()

    a_ = ExitStack()
    qT = sb("qT", [P, NQ // 2, T], F32, a_)
    probs = sb("probs", [P, 2, N], F32, a_)
    b_qkv = sb("b_qkv", [P, QKV], F32, a_)
    b_o = sb("b_o", [P, D], F32, a_)
    sinks = sb("sinks", [P, NQ], F32, a_)
    neg_sinks = sb("neg_sinks", [P, NQ], F32, a_)
    pos_i = sb("pos_i", [P, TT], I32, a_)
    pos_f = sb("pos_f", [P, TT], F32, a_)
    inv_freq = sb("inv_freq", [P, RH], F32, a_)
    ang = sb("ang", [P, TT, RH], F32, a_)
    turns = sb("turns", [P, TT, RH], F32, a_)
    red = sb("red", [P, TT, RH], F32, a_)
    red_c = sb("red_c", [P, TT, RH], F32, a_)
    sin_t = sb("sin_t", [P, TT, RH], F32, a_)
    cos_t = sb("cos_t", [P, TT, RH], F32, a_)
    mask0 = sb("mask0", [P, 4, P], BF16, a_)
    mask1 = sb("mask1", [P, 2, T], BF16, a_)
    ident_b = sb("ident_b", [P, P], BF16, a_)
    qkv = sb("qkv", [P, TT, QKV], F32, a_)
    rope_t = sb("rope_t", [P, 4, TT, (NQ + NKV) * RH], F32, a_)
    k_pad = sb("k_pad", [P, TT, NKV, 2, 2 * HD], F32, a_)
    kT = sb("kT", [P, NKV, 2, T], F32, a_)
    probsT = sb("probsT", [P, 2, N], F32, a_)
    raw_max = sb("raw_max", [P, TT, NQ], F32, a_)
    neg_max = sb("neg_max", [P, TT, NQ], F32, a_)
    den = sb("den", [P, TT, NQ], F32, a_)
    sink_e = sb("sink_e", [P, TT, NQ], F32, a_)
    o_tok = xn
    a_.close()
    s1.close()

    ring_b = [sb(f"ring{s}", [P, PIECE]) for s in range(RING_A, RING)]
    ring = ring_a + ring_b
    r_ = ExitStack()
    xT = sb("xT", [P, KT, T], F32, r_)
    r_.close()
    gT_hi = sb("gT_hi", [P, KT, P], F32R)
    gT_lo = sb("gT_lo", [P, KT, P], F32R)
    t_ = ExitStack()
    logits = sb("logits", [P, TT, NE], F32, t_)
    top_v = sb("top_v", [P, TT, 8], F32, t_)
    top_i = sb("top_i", [P, TT, 8], U32, t_)
    top_f = sb("top_f", [P, TT, 2], F32, t_)
    diff = sb("diff", [P, TT], F32, t_)
    p2 = sb("p2", [P, TT], F32, t_)
    psum_g = sb("psum_g", [P, TT], F32, t_)
    g1 = sb("g1", [P, TT], F32, t_)
    g2 = sb("g2", [P, TT], F32, t_)
    oh = sb("oh", [P, TT, 2, NE], F32, t_)
    sel = sb("sel", [P, TT, NE], F32, t_)
    t_.close()
    e_a = sb("e_a", [P, N])
    eT_hi = sb("eT_hi", [P, 4, P], F32R)
    eT_lo = sb("eT_lo", [P, 4, P], F32R)
    e_y = sb("e_y", [P, D])
    pick = sb("pick", [P, TT, P])
    pick_g = sb("pick_g", [P, TT, P])
    pick_gT = sb("pick_gT", [P, T])

    bank = [ctx.enter_context(nc.psum_tensor(f"bank{i}", [P, N], F32)) for i in range(8)]

    landed = [sem(f"landed{s}") for s in range(RING)]
    hi_ready, lo_ready, piece_used = sem("hi_ready"), sem("lo_ready"), sem("piece_used")
    ld_x, ld_gain = [sem("ld_x0"), sem("ld_x1")], [sem("ld_gain0"), sem("ld_gain1")]
    ld_even, ld_odd, ld_router = sem("ld_even"), sem("ld_odd"), sem("ld_router")
    stored = sem("stored")
    pool_step, pool_const, pool_spw = sem("pool_step"), sem("pool_const"), sem("pool_spw")
    dve_step, act_step = sem("dve_step"), sem("act_step")
    dve_const = sem("dve_const")
    spw_t, spw_ready = sem("spw_t"), sem("spw_ready")
    sq_ready, xn_ready = sem("sq_ready"), sem("xn_ready")
    norm_t = sem("norm_t")
    xT_hi_ready, xT_lo_ready = sem("xT_hi_ready"), sem("xT_lo_ready")
    v_gelu = sem("v_gelu")
    vn_ready = sem("vn_ready")
    uT_ready, acT_ready, hc_ready = sem("uT_ready"), sem("acT_ready"), sem("hc_ready")
    mix_done, y_ready, yT_hi_ready, yT_lo_ready = sem("mix_done"), sem("y_ready"), sem("yT_hi_ready"), sem("yT_lo_ready")
    acc_done, h_added = sem("acc_done"), sem("h_added")
    silu_ready, act_ready = sem("silu_ready"), sem("act_ready")
    fT_hi_ready, fT_lo_ready = sem("fT_hi_ready"), sem("fT_lo_ready")
    red_ready, trig_ready = sem("red_ready"), sem("trig_ready")
    qkv_done, qkv_ready, rope_ready = sem("qkv_done"), sem("qkv_ready"), sem("rope_ready")
    qk_t, qkT_act, qkT_dve = sem("qk_t"), sem("qkT_act"), sem("qkT_dve")
    s_done, max_ready, probs_ready = sem("s_done"), sem("max_ready"), sem("probs_ready")
    probs_t, probsT_ready, pv_done = sem("probs_t"), sem("probsT_ready"), sem("pv_done")
    sink_arg, sink_ready, o_ready = sem("sink_arg"), sem("sink_ready"), sem("o_ready")
    h_final = sem("h_final")
    logits_done, diff_ready, p2_ready = sem("logits_done"), sem("diff_ready"), sem("p2_ready")
    xTr_ready, sel_ready, rank_done, routed = sem("xTr_ready"), sem("sel_ready"), sem("rank_done"), sem("routed")
    pick_ready, pickg_ready, pickg_t, pickgT_ready = sem("pick_ready"), sem("pickg_ready"), sem("pickg_t"), sem("pickgT_ready")
    gathered, gT_hi_ready, gT_lo_ready = sem("gathered"), sem("gT_hi_ready"), sem("gT_lo_ready")
    e_silu, e_act, e_t = sem("e_silu"), sem("e_act"), sem("e_t")
    eT_hi_ready, eT_lo_ready = sem("eT_hi_ready"), sem("eT_lo_ready")
    ey_ready, scattered = sem("ey_ready"), sem("scattered")
    e_added, zeroed = sem("e_added"), sem("zeroed")

    x_v = x[0].rearrange("(a p) d -> p a d", p=P)
    out_v = out[0].rearrange("(a p) d -> p a d", p=P)

    def rows(w, k0, nk, c0, ncol):
        return w[k0 * P:(k0 + nk) * P, c0:c0 + ncol].rearrange("(k p) n -> p k n", p=P)

    def spread(v, n):
        return v.rearrange("(o n) -> o n", o=1).broadcast_to([P, n])

    def front_source(p):
        if p < U0:
            return rows(ev_w_in[0], 4 * (p - V0), 4, 3 * CONV + GM, GM), 4
        if p < WOUT0:
            first = {U0: 3 * CONV, C0: CONV, X0: 2 * CONV, B0: 0}[p - p % 2]
            return rows(ev_w_in[0], 0, KT, first + 256 * (p % 2), 256), KT
        if p < FFN0:
            return rows(ev_w_out[0], OUT_KT[2 * (p - WOUT0)], 2, 0, D), 2
        if p < QKV0:
            for u in range(FU):
                g, up, d = ffn_pieces(u)
                if p == g:
                    return rows(ev_ffn_wg[0], 0, KT, 256 * u, 256), KT
                if p == up:
                    return rows(ev_ffn_wu[0], 0, KT, 256 * u, 256), KT
                if p == d:
                    return rows(ev_ffn_wd[0], 2 * u, 2, 0, D), 2
        if p == QKV0:
            return rows(od_w_qkv[0], 0, KT, NQ * HD, 2 * NKV * HD), KT
        if p < WO0:
            c, k = divmod(p - QKV0 - 1, 2)
            return rows(od_w_qkv[0], 4 * k, 4, N * c, N), 4
        return rows(od_w_o[0], 2 * (p - WO0), 2, 0, D), 2

    def hi(p, nk):
        return w_hi[:, p % SPLITS, :].rearrange("p (k n) -> p k n", k=nk)

    def lo(p, nk):
        return w_lo[:, p % SPLITS, :].rearrange("p (k n) -> p k n", k=nk)

    ACC = (2, 3, 6, 7)
    NORM_BANKS = (0, 1, 4, 5)
    O_BANKS = (0, 1, 2, 7)
    S_BANKS = (6, 3)
    OT_BANKS = (0, 1, 3, 6)
    WO_ACC = (4, 5, 2, 7)
    block = ctx.enter_context(nc.Block())

    @block.sync
    def _(sp):
        for a in range(TT):
            sp.dma_start(h[:, a, :], x_v[:, a, :]).then_inc(ld_x[a], 16)
        for p in range(FRONT):
            if p >= RING_A:
                sp.wait_ge(lo_ready, p - RING_A + 1)
            src, nk = front_source(p)
            sp.dma_start(ring_a[p % RING_A][:].rearrange("p (k n) -> p k n", k=nk), src).then_inc(
                landed[p % RING_A], 16)

        def expert_load(wait, e, q):
            for j in range(EU):
                g, up, d = expert_pieces(j)
                for w, first in ((od_exp_wg, g), (od_exp_wu, up)):
                    if first <= q < first + 2:
                        src = w[0][bass.ds(e, 1), (q - first) * 4 * P:(q - first + 1) * 4 * P, N * j:N * j + N]
                        src, nk = src.rearrange("o (k p) n -> p (o k) n", p=P), 4
                if d <= q < d + 2:
                    r0 = N * j + 2 * P * (q - d)
                    src = od_exp_wd[0][bass.ds(e, 1), r0:r0 + 2 * P, :]
                    src, nk = src.rearrange("o (k p) n -> p (o k) n", p=P), 2
            if wait is not None:
                sp.wait_ge(lo_ready, wait)
            sp.dma_start(ring[q % RING][:].rearrange("p (k n) -> p k n", k=nk), src).then_inc(landed[q % RING], 16)

        for q in range(RING):
            if q == RING_A:
                sp.wait_ge(h_added, 12)
            expert_load(FRONT + q - RING_A + 1 if q < RING_A else None, 0, q)
        for q in range(RING, EP):
            expert_load(FRONT + q - RING + 1, 0, q)
        with sp.Fori(1, NE) as e:
            for q in range(EP):
                expert_load(e * EP + (FRONT + q - RING + 1), e, q)
        sp.wait_ge(routed, 1)
        most = nc.sync.value_load(count_max[0:1, 0:1], min_val=0, max_val=T)
        with sp.If(most > P):
            with sp.Fori(0, NE) as e:
                for q in range(EP):
                    expert_load(e * EP + (NE * EP + FRONT + q - RING + 1), e, q)
        for a in range(TT):
            sp.wait_ge(h_final, a + 2)
            sp.dma_start(out_v[:, a, :], xn[:, a, :]).then_inc(stored, 16)
        sp.wait_ge(stored, 16 * TT)

    @block.gpsimd
    def _(pool):
        nc.gpsimd.memset(ident[:], 0.0).then_inc(pool_step, 1)
        nc.gpsimd.memset(ones[:], 1.0).then_inc(pool_step, 1)
        pool.wait_ge(pool_step, 2)
        nc.gpsimd.affine_select(out=ident[:], in_=ident[:], compare_op=ALU.not_equal, fill=1.0, base=0,
                                pattern=[[-1, P]], channel_multiplier=1).then_inc(pool_const, 1)
        nc.gpsimd.affine_select(out=tri[:], in_=ones[:], compare_op=ALU.is_ge, fill=0.0, base=0,
                                pattern=[[1, P]], channel_multiplier=-1).then_inc(pool_const, 1)
        nc.gpsimd.iota(iota_s[:], pattern=[[1, P]], base=0, channel_multiplier=0,
                       allow_small_or_imprecise_dtypes=True).then_inc(pool_const, 1)
        pool.wait_ge(ld_even, 16 * 5)
        nc.gpsimd.affine_select(out=sp_w[:], in_=sp_w[:], compare_op=ALU.is_ge, fill=0.0, base=0,
                                pattern=[[0, GH], [-1, P]], channel_multiplier=1).then_inc(pool_spw, 1)
        pool.wait_ge(h_added, 4)
        nc.gpsimd.memset(mask0[:], 0.0).then_inc(pool_step, 1)
        nc.gpsimd.memset(mask1[:], 0.0).then_inc(pool_step, 1)
        nc.gpsimd.memset(ident_b[:], 0.0).then_inc(pool_step, 1)
        nc.gpsimd.memset(k_pad[:], 0.0).then_inc(pool_step, 1)
        for k in range(RH):
            nc.gpsimd.memset(inv_freq[:, k:k + 1], float(np.float32(THETA ** (-2.0 * k / ROPE)))).then_inc(pool_step, 1)
        pool.wait_ge(pool_step, 6 + RH)
        nc.gpsimd.affine_select(out=ident_b[:], in_=ident_b[:], compare_op=ALU.not_equal, fill=1.0, base=0,
                                pattern=[[-1, P]], channel_multiplier=1).then_inc(pool_const, 1)
        nc.gpsimd.affine_select(out=mask0[:], in_=mask0[:], compare_op=ALU.is_ge, fill=MASKED, base=0,
                                pattern=[[0, 4], [-1, P]], channel_multiplier=1).then_inc(pool_const, 1)
        nc.gpsimd.affine_select(out=mask1[:, :, 0:P], in_=mask1[:, :, 0:P], compare_op=ALU.is_gt, fill=MASKED,
                                base=0, pattern=[[0, 2], [1, P]], channel_multiplier=-1).then_inc(pool_const, 1)
        nc.gpsimd.affine_select(out=mask1[:, :, P:T], in_=mask1[:, :, P:T], compare_op=ALU.is_ge, fill=MASKED,
                                base=0, pattern=[[0, 2], [-1, P]], channel_multiplier=1).then_inc(pool_const, 1)

    @block.scalar
    def _(act):
        norm_gains = (ev_norm1_g[0], ev_norm2_g[0], od_norm1_g[0], od_norm2_g[0], final_norm_g)

        def load_gain(n):
            if n >= 2:
                act.wait_ge(xn_ready, TT * (n - 1))
            act.dma_start(gain[:, n % 2, :], spread(norm_gains[n], D)).then_inc(ld_gain[n % 2], 16)

        load_gain(0)
        act.dma_start(sp_w[:], ev_spatial_w[0].rearrange("h i j -> i h j")).then_inc(ld_even, 16)
        act.dma_start(ln_g[:], spread(ev_ln_g[0], GM)).then_inc(ld_even, 16)
        act.dma_start(ln_b[:], spread(ev_ln_b[0], GM)).then_inc(ld_even, 16)
        act.dma_start(sp_b[:], spread(ev_spatial_b[0].rearrange("h i -> (h i)"), GH * P).rearrange(
            "p (h i) -> p h i", h=GH)).then_inc(ld_even, 16)
        act.dma_start(conv_w[:], ev_conv_w[0].rearrange("(c p) k -> p c k", p=P)).then_inc(ld_even, 16)
        load_gain(1)
        act.dma_start(router[:], od_router_w[0].rearrange("(k p) e -> p k e", p=P)).then_inc(ld_router, 16)

        at = [0]

        def split_hi(upto):
            for p in range(at[0], upto + 1):
                act.wait_ge(landed[p % RING_A], 16 * (p // RING_A + 1))
                if p >= SPLITS:
                    act.wait_ge(piece_used, p - SPLITS + 1)
                nc.scalar.copy(w_hi[:, p % SPLITS, :], ring_a[p % RING_A][:]).then_inc(hi_ready, 1)
            at[0] = max(at[0], upto + 1)

        def norm_square(n, a):
            if n:
                act.wait_ge(h_added, 4 * (n - 1) + 2 * a + 2)
            else:
                act.wait_ge(ld_x[a], 16)
            nc.scalar.activation(xn[:, a, :], h[:, a, :], ACT.Square, accum_out=ssq[:, a:a + 1]).then_inc(sq_ready, 1)

        def turned_hi(first, a, banks):
            for i in range(2):
                act.wait_ge(norm_t, first + 2 * a + i + 1)
                nc.scalar.copy(xT_hi[:, 4 * i:4 * i + 4, P * a:P * a + P],
                               bank[banks[2 * a + i]][:].rearrange("p (k t) -> p k t", k=4)).then_inc(xT_hi_ready, 1)

        def norm(n, p0):
            norm_square(n, 0)
            if n:
                split_hi(p0)
            turned_hi(4 * n, 0, NORM_BANKS)
            split_hi(p0 + 1)
            norm_square(n, 1)
            turned_hi(4 * n, 1, NORM_BANKS)
            split_hi(p0 + 2)

        norm_square(0, 0)
        norm_square(0, 1)
        turned_hi(0, 0, NORM_BANKS)
        split_hi(V0)
        turned_hi(0, 1, NORM_BANKS)
        split_hi(V0 + 1 + 2)
        for a in range(TT):
            act.wait_ge(piece_used, V0 + 2)
            nc.scalar.activation(v_act[:, a, :], bank[6 + a][:], ACT.Gelu).then_inc(v_gelu, 1)
        for c in range(2):
            split_hi(U0 + c + 2)
            act.wait_ge(piece_used, U0 + c + 1)
            nc.scalar.activation(uT[:, 2 * c:2 * c + 2, :], bank[c][:].rearrange("p (c t) -> p c t", c=2),
                                 ACT.Gelu).then_inc(uT_ready, 1)
        for c in range(2):
            split_hi(C0 + c + 2)
            act.wait_ge(piece_used, C0 + c + 1)
            nc.scalar.copy(acT[:, 2 * c:2 * c + 2, :], bank[2 + c][:].rearrange("p (c t) -> p c t", c=2)).then_inc(
                acT_ready, 1)
        split_hi(B0 + 1)
        for i in range(4):
            split_hi((B0 + 1, B0 + 1, B0 + 2, B0 + 3)[i])
            k = (4, 6, 0, 2)[i]
            act.wait_ge(y_ready, i + 1)
            nc.scalar.copy(yT_hi[:, k:k + 2, :], yT[:, k % 4:k % 4 + 2, :]).then_inc(yT_hi_ready, 1)
        split_hi(WOUT0 + 3)

        norm(1, FFN0)
        load_gain(2)
        act.dma_start(b_qkv[:], spread(od_b_qkv[0], QKV)).then_inc(ld_odd, 16)
        act.dma_start(b_o[:], spread(od_b_o[0], D)).then_inc(ld_odd, 16)
        act.dma_start(sinks[:], spread(od_sinks[0], NQ)).then_inc(ld_odd, 16)
        for a in range(TT):
            act.dma_start(pos_i[:, a:a + 1], positions[0, P * a:P * a + P].unsqueeze(1)).then_inc(ld_odd, 16)
        for u in range(FU):
            g, up, d = ffn_pieces(u)
            split_hi(up + 2 if u < FU - 1 else up + 1)
            act.wait_ge(piece_used, g + 1)
            b = bank[(0, 4)[u % 2]]
            nc.scalar.activation(f_s[:], b[:].rearrange("p (c t) -> p c t", c=2), ACT.Silu).then_inc(silu_ready, 1)
            act.wait_ge(act_ready, u + 1)
            if u >= 2:
                act.wait_ge(piece_used, ffn_pieces(u - 2)[2] + 1)
            nc.scalar.copy(fT_hi[:, u % 2], f_a[:]).then_inc(fT_hi_ready, 1)
        split_hi(QKV0 - 1)

        norm(2, QKV0)
        load_gain(3)
        act.wait_ge(red_ready, 1)
        nc.scalar.activation(sin_t[:], red[:], ACT.Sin).then_inc(trig_ready, 1)
        nc.scalar.activation(cos_t[:], red_c[:], ACT.Sin).then_inc(trig_ready, 1)
        split_hi(QKV0 + 4)

        def turned_queries(a):
            for i in range(2):
                act.wait_ge(qk_t, 3 * a + 2 + i)
                nc.scalar.copy(qT[:, 4 * i:4 * i + 4, P * a:P * a + P],
                               bank[2 * a + i][:].rearrange("p (c t) -> p c t", c=4)).then_inc(qkT_act, 1)

        turned_queries(0)
        split_hi(WO0)
        for i in range(12):
            a, n, first = (0, 4, 4 * i) if i < 4 else (1, 2, 2 * (i - 4))
            if i == 1:
                turned_queries(1)
            act.wait_ge(max_ready, i + 1)
            if i >= 2:
                act.wait_ge(probs_t, i - 1)
            w = N // n
            for j in range(n):
                hq = first + j
                ins = nc.scalar.activation(probs[:, i % 2, w * j:w * j + w], bank[S_BANKS[i % 2]][:, w * j:w * j + w],
                                           ACT.Exp, bias=neg_max[:, a, hq:hq + 1], scale=SCALE,
                                           accum_out=den[:, a, hq:hq + 1])
            ins.then_inc(probs_ready, 1)
            if i in (3, 11):
                act.wait_ge(sink_arg, a + 1)
                nc.scalar.activation(sink_e[:, a, :], sink_e[:, a, :], ACT.Exp).then_inc(sink_ready, 1)
            if i == 4:
                split_hi(WO0 + 2)
            if i == 9:
                turned_hi(12, 0, OT_BANKS)
        turned_hi(12, 1, OT_BANKS)
        split_hi(WO0 + 3)

        for a in range(TT):
            norm_square(3, a)
            for i in range(2):
                act.wait_ge(norm_t, 16 + 2 * a + i + 1)
                nc.scalar.copy(xT[:, 4 * i:4 * i + 4, P * a:P * a + P],
                               bank[OT_BANKS[2 * a + i]][:].rearrange("p (k t) -> p k t", k=4)).then_inc(xTr_ready, 1)
        load_gain(4)
        act.wait_ge(diff_ready, 1)
        nc.scalar.activation(p2[:], diff[:], ACT.Exp).then_inc(p2_ready, 1)

        def expert_hi(b, q):
            act.wait_ge(landed[q % RING], b * (16 * (EP // RING)) + 16 * (q // RING + 1 + (FRONT // RING_A if q % RING < RING_A else 0)))
            act.wait_ge(piece_used, b * EP + (FRONT + q - SPLITS + 1))
            nc.scalar.copy(w_hi[:, (FRONT + q) % SPLITS, :], ring[q % RING][:]).then_inc(hi_ready, 1)

        def expert_his(b, q0, q1):
            for q in range(q0, q1):
                expert_hi(b, q)

        def gathered_hi(count):
            for i in range(2):
                act.wait_ge(gathered, count + (i + 1))
                nc.scalar.copy(gT_hi[:, 4 * i:4 * i + 4, :], bank[2 + i][:].rearrange("p (k s) -> p k s", k=4)).then_inc(
                    gT_hi_ready, 1)

        def hidden_hi(count):
            act.wait_ge(e_t, count)
            nc.scalar.copy(eT_hi[:], bank[6][:].rearrange("p (k s) -> p k s", k=4)).then_inc(eT_hi_ready, 1)

        def expert_block(b, last):
            at = AHEAD
            for j in range(EU):
                g, up, d = expert_pieces(j)
                if j:
                    expert_his(b, at, g + 4)
                    at = g + 4
                    hidden_hi(b * EU + j)
                expert_his(b, at, min(up + 4, EP))
                at = min(up + 4, EP)
                act.wait_ge(piece_used, b * EP + (FRONT + g + 2))
                nc.scalar.activation(e_a[:], bank[2 * (j % 2)][:], ACT.Silu).then_inc(e_silu, 1)
            expert_his(b, at, EP)
            hidden_hi(b * EU + EU)
            if not last:
                gathered_hi(b * 2 + 2)
                expert_his(b + 1, 0, AHEAD)
            act.wait_ge(piece_used, b * EP + (FRONT + EP))
            nc.scalar.copy(e_y[:, 0:N], bank[4][:])
            nc.scalar.copy(e_y[:, N:D], bank[5][:]).then_inc(ey_ready, 1)

        def no_outputs():
            nc.scalar.activation(e_y[:].rearrange("p (k n) -> p k n", n=P), ones[:].unsqueeze(1).broadcast_to([P, D // P, P]),
                                 ACT.Copy, scale=0.0).then_inc(ey_ready, 1)

        act.wait_ge(routed, 1)
        no_outputs()
        gathered_hi(0)
        expert_his(0, 0, AHEAD)
        with act.Fori(0, NE - 1) as b:
            expert_block(b, False)
        most = nc.scalar.value_load(count_max[0:1, 0:1], min_val=0, max_val=T)
        expert_block(NE - 1, True)
        with act.If(most > P):
            no_outputs()
            gathered_hi(2 * NE)
            expert_his(NE, 0, AHEAD)
            with act.Fori(NE, BLOCKS - 1) as b:
                expert_block(b, False)
            expert_block(BLOCKS - 1, True)
        act.wait_ge(h_final, 1)
        nc.scalar.activation(xn[:, 0, :], h[:, 0, :], ACT.Square, accum_out=ssq[:, 0:1]).then_inc(sq_ready, 1)

    @block.vector
    def _(dve):
        steps = [0]

        def then(ins):
            steps[0] += 1
            ins.then_inc(dve_step, 1)
            dve.wait_ge(dve_step, steps[0])

        at = [0]

        def split_lo(upto):
            for p in range(at[0], upto + 1):
                dve.wait_ge(hi_ready, p + 1)
                nc.vector.tensor_tensor(w_lo[:, p % SPLITS, :], ring_a[p % RING_A][:],
                                        w_hi[:, p % SPLITS, :].bitcast(F32), ALU.subtract).then_inc(lo_ready, 1)
            at[0] = max(at[0], upto + 1)

        def rsqrt(y, v, t):
            then(nc.vector.tensor_scalar(y.bitcast(I32), v.bitcast(I32), -0.5, float(0x5F3759DF), ALU.mult, ALU.add))
            for _ in range(3):
                then(nc.vector.tensor_tensor(t, y, y, ALU.mult))
                then(nc.vector.scalar_tensor_tensor(out=t, in0=t, scalar=-0.5, in1=v, op0=ALU.mult, op1=ALU.mult))
                then(nc.vector.scalar_tensor_tensor(out=y, in0=t, scalar=1.5, in1=y, op0=ALU.add, op1=ALU.mult))

        def norm_scale(n, a):
            dve.wait_ge(sq_ready, TT * n + a + 1)
            then(nc.vector.tensor_scalar(var[:, a:a + 1], ssq[:, a:a + 1], 1.0 / D, EPS, ALU.mult, ALU.add))
            rsqrt(rstd[:, a:a + 1], var[:, a:a + 1], newton[:, a:a + 1])
            dve.wait_ge(ld_gain[n % 2], 16 * (n // 2 + 1))
            nc.vector.scalar_tensor_tensor(out=xn[:, a, :], in0=h[:, a, :], scalar=rstd[:, a:a + 1], in1=gain[:, n % 2, :],
                                           op0=ALU.mult, op1=ALU.mult).then_inc(xn_ready, 1)

        def turned_lo(first, a, banks):
            for i in range(2):
                dve.wait_ge(xT_hi_ready, first + 2 * a + i + 1)
                c = slice(P * a, P * a + P)
                nc.vector.tensor_tensor(xT_lo[:, 4 * i:4 * i + 4, c], bank[banks[2 * a + i]][:].rearrange("p (k t) -> p k t", k=4),
                                        xT_hi[:, 4 * i:4 * i + 4, c].bitcast(F32), ALU.subtract).then_inc(xT_lo_ready, 1)

        def norm(n, last, p0):
            add_to_h(n - 1, last, ACC, 0)
            norm_scale(n, 0)
            split_lo(p0)
            turned_lo(4 * n, 0, NORM_BANKS)
            add_to_h(n - 1, last, ACC, 1)
            split_lo(p0 + 1)
            norm_scale(n, 1)
            turned_lo(4 * n, 1, NORM_BANKS)
            split_lo(p0 + 2)

        def add_to_h(n, last, banks, a):
            for half in range(2):
                if (a, half) == (1, 1):
                    dve.wait_ge(piece_used, last + 1)
                else:
                    dve.wait_ge(acc_done, 3 * n + 2 * a + half + 1)
                hs = h[:, a, N * half:N * half + N]
                nc.vector.tensor_tensor(hs, hs, bank[banks[2 * a + half]][:], ALU.add).then_inc(h_added, 1)

        def reduce_angles():
            two_pi = 2.0 * np.pi
            c1 = 6.28125
            c2 = float(np.round((two_pi - c1) * 2.0 ** 20) / 2.0 ** 20)
            c3 = float(np.float32(two_pi - c1 - c2))
            magic = 1.5 * 2.0 ** 23
            dve.wait_ge(ld_odd, 80)
            dve.wait_ge(pool_const, 7)
            then(nc.vector.tensor_copy(pos_f[:], pos_i[:]))
            for a in range(TT):
                then(nc.vector.tensor_scalar(ang[:, a, :], inv_freq[:], pos_f[:, a:a + 1], None, ALU.mult))
            then(nc.vector.tensor_scalar(turns[:], ang[:], float(np.float32(1.0 / two_pi)), magic, ALU.mult, ALU.add))
            then(nc.vector.tensor_scalar(turns[:], turns[:], magic, None, ALU.subtract))
            for i, c in enumerate((c1, c2, c3)):
                then(nc.vector.scalar_tensor_tensor(out=red[:], in0=turns[:], scalar=-c, in1=(ang if i == 0 else red)[:],
                                                    op0=ALU.mult, op1=ALU.add))
            then(nc.vector.tensor_scalar(red[:], red[:], 3.1415925, -3.1415925, ALU.min, ALU.max))
            then(nc.vector.scalar_tensor_tensor(out=red_c[:], in0=red[:], scalar=-1.0, in1=red[:], op0=ALU.mult, op1=ALU.max))
            nc.vector.tensor_scalar(red_c[:], red_c[:], -1.0, float(np.float32(np.pi / 2)), ALU.mult, ALU.add).then_inc(red_ready, 1)
            then(nc.vector.tensor_scalar(neg_sinks[:], sinks[:], -1.0, None, ALU.mult))

        nc.vector.memset(hc[:, :, 0:CW - 1], 0.0).then_inc(dve_const, 1)
        norm_scale(0, 0)
        norm_scale(0, 1)
        turned_lo(0, 0, NORM_BANKS)
        split_lo(V0)
        turned_lo(0, 1, NORM_BANKS)
        split_lo(V0 + 1)
        dve.wait_ge(spw_t, 1)
        nc.vector.tensor_copy(sp_wT[:], bank[4][:].rearrange("p (h i) -> p h i", h=GH)).then_inc(spw_ready, 1)
        split_lo(V0 + 1 + 2)
        for a in range(TT):
            dve.wait_ge(v_gelu, a + 1)
            then(nc.vector.bn_stats(bn[:, a, :], v_act[:, a, :]))
            then(nc.vector.bn_aggr(mv[:, a, :], bn[:, a, :]))
        then(nc.vector.tensor_scalar(var[:], mv[:, :, 1], EPS, None, ALU.add))
        rsqrt(rstd[:], var[:], newton[:])
        split_lo(U0 + 2)
        dve.wait_ge(ld_even, 16 * 5)
        for a in range(TT):
            then(nc.vector.tensor_scalar(v_act[:, a, :], v_act[:, a, :], mv[:, a, 0:1], rstd[:, a:a + 1], ALU.subtract, ALU.mult))
            then(nc.vector.tensor_tensor(v_act[:, a, :], v_act[:, a, :], ln_g[:], ALU.mult))
            nc.vector.tensor_tensor(v_act[:, a, :], v_act[:, a, :], ln_b[:], ALU.add).then_inc(vn_ready, 1)
            split_lo(U0 + 3 + a)
        dve.wait_ge(dve_const, 1)

        def convolve(c):
            dve.wait_ge(acT_ready, c + 1)
            dve.wait_ge(piece_used, X0 + c + 1)
            then(nc.vector.tensor_tensor(hc[:, 2 * c:2 * c + 2, CW - 1:], acT[:, 2 * c:2 * c + 2, :],
                                         bank[6 + c][:].rearrange("p (c t) -> p c t", c=2), ALU.mult))
            for i in (2 * c, 2 * c + 1):
                then(nc.vector.tensor_scalar(cv[:, i, :], hc[:, i, 0:T], conv_w[:, i, 0:1], None, ALU.mult))
                for k in range(1, CW):
                    then(nc.vector.scalar_tensor_tensor(out=cv[:, i, :], in0=hc[:, i, k:k + T], scalar=conv_w[:, i, k:k + 1],
                                                        in1=cv[:, i, :], op0=ALU.mult, op1=ALU.add))

        def low_of_y(i, k):
            dve.wait_ge(yT_hi_ready, i + 1)
            nc.vector.tensor_tensor(yT_lo[:, k:k + 2, :], yT[:, k % 4:k % 4 + 2, :], yT_hi[:, k:k + 2, :].bitcast(F32),
                                    ALU.subtract).then_inc(yT_lo_ready, 1)

        split_lo(X0 + 2)
        convolve(0)
        split_lo(B0 + 1)
        for g in range(2):
            dve.wait_ge(mix_done, 1 + g)
            b = sp_b[:, 2 * g:2 * g + 2, :].unsqueeze(2).broadcast_to([P, 2, TT, P])
            ys = yT[:, 2 * g:2 * g + 2, :]
            then(nc.vector.tensor_tensor(ys.rearrange("p g (a i) -> p g a i", a=TT),
                                         bank[4 + g][:].rearrange("p (g a i) -> p g a i", g=2, a=TT), b, ALU.add))
            nc.vector.tensor_tensor(ys, ys, uT[:, 2 * g:2 * g + 2, :], ALU.mult).then_inc(y_ready, 1)
            low_of_y(g, CT + 2 * g)
        convolve(1)
        dve.wait_ge(yT_lo_ready, 2)
        for c in range(2):
            split_lo(B0 + c + 2)
            dve.wait_ge(piece_used, B0 + c + 1)
            nc.vector.tensor_tensor(yT[:, 2 * c:2 * c + 2, :], cv[:, 2 * c:2 * c + 2, :],
                                    bank[c][:].rearrange("p (c t) -> p c t", c=2), ALU.mult).then_inc(y_ready, 1)
            low_of_y(2 + c, 2 * c)
        split_lo(WOUT0 + 3)

        norm(1, FFN0 - 1, FFN0)
        for u in range(FU):
            g, up, d = ffn_pieces(u)
            split_lo(up + 2 if u < FU - 1 else up + 1)
            dve.wait_ge(silu_ready, u + 1)
            dve.wait_ge(piece_used, up + 1)
            b = bank[(1, 5)[u % 2]]
            if u:
                dve.wait_ge(fT_lo_ready, u)
            nc.vector.tensor_tensor(f_a[:], f_s[:], b[:].rearrange("p (c t) -> p c t", c=2), ALU.mult).then_inc(act_ready, 1)
            dve.wait_ge(fT_hi_ready, u + 1)
            nc.vector.tensor_tensor(fT_lo[:, u % 2], f_a[:], fT_hi[:, u % 2].bitcast(F32), ALU.subtract).then_inc(fT_lo_ready, 1)
            if u == 3:
                reduce_angles()
        split_lo(QKV0 - 1)

        norm(2, QKV0 - 1, QKV0)

        def add_bias(i, c, a):
            c0, w, b0 = ((NQ * HD, 2 * NKV * HD, 0), (0, N, 2), (N, N, 6))[c]
            if a == 0:
                dve.wait_ge(qkv_done, c + 1)
            else:
                dve.wait_ge(piece_used, (QKV0 + 1, QKV0 + 3, QKV0 + 5)[c])
            nc.vector.tensor_tensor(qkv[:, a, c0:c0 + w], bank[b0 + a][:, 0:w], b_qkv[:, c0:c0 + w],
                                    ALU.add).then_inc(qkv_ready, 1)

        def rotate(a):
            heads = NQ + NKV
            dve.wait_ge(qkv_ready, 5 + a)
            qk = qkv[:, a, 0:heads * HD].rearrange("p (h d) -> p h d", d=HD)
            t1, t2 = qk[:, :, 0:RH], qk[:, :, RH:ROPE]
            r = [rope_t[:, i, a, :].rearrange("p (h d) -> p h d", d=RH) for i in range(4)]
            cs = cos_t[:, a:a + 1, :].broadcast_to([P, heads, RH])
            sn = sin_t[:, a:a + 1, :].broadcast_to([P, heads, RH])
            nc.vector.tensor_tensor(r[0], t1, cs, ALU.mult)
            nc.vector.tensor_tensor(r[1], t2, sn, ALU.mult)
            nc.vector.tensor_tensor(r[2], t2, cs, ALU.mult)
            then(nc.vector.tensor_tensor(r[3], t1, sn, ALU.mult))
            nc.vector.tensor_tensor(t1, r[0], r[1], ALU.subtract)
            then(nc.vector.tensor_tensor(t2, r[2], r[3], ALU.add))
            kk = qkv[:, a, NQ * HD:heads * HD].rearrange("p (g d) -> p g d", d=HD)
            for i in range(2):
                nc.vector.tensor_copy(k_pad[:, a, :, i, HD * i:HD * i + HD], kk).then_inc(rope_ready, 1)

        def turned_keys(a):
            dve.wait_ge(qk_t, 3 * a + 1)
            nc.vector.tensor_copy(kT[:].rearrange("p g i t -> p (g i) t")[:, :, P * a:P * a + P],
                                  bank[4 + a][:].rearrange("p (g t) -> p g t", g=4)).then_inc(qkT_dve, 1)

        add_bias(0, 0, 0)
        split_lo(QKV0 + 3)
        add_bias(1, 0, 1)
        add_bias(2, 1, 0)
        add_bias(3, 1, 1)
        split_lo(QKV0 + 4)
        dve.wait_ge(trig_ready, 2)
        add_bias(4, 2, 0)
        rotate(0)
        add_bias(5, 2, 1)
        turned_keys(0)
        rotate(1)
        split_lo(WO0)

        def row_max(i):
            a, n, first = (0, 4, 4 * i) if i < 4 else (1, 2, 2 * (i - 4))
            dve.wait_ge(s_done, i + 1)
            then(nc.vector.tensor_reduce(raw_max[:, a, first:first + n],
                                         bank[S_BANKS[i % 2]][:].rearrange("p (h k) -> p h k", h=n), AX_X, ALU.max))
            nc.vector.scalar_tensor_tensor(out=neg_max[:, a, first:first + n], in0=raw_max[:, a, first:first + n],
                                           scalar=-SCALE, in1=neg_sinks[:, first:first + n], op0=ALU.mult,
                                           op1=ALU.min).then_inc(max_ready, 1)
            if i in (3, 11):
                dve.wait_ge(max_ready, i + 1)
                nc.vector.tensor_tensor(sink_e[:, a, :], neg_max[:, a, :], sinks[:], ALU.add).then_inc(sink_arg, 1)

        def evacuate_probs(i):
            dve.wait_ge(probs_t, i + 1)
            if i >= 2:
                dve.wait_ge(pv_done, i - 1)
            nc.vector.tensor_copy(probsT[:, i % 2, :], bank[4 + i % 2][:]).then_inc(probsT_ready, 1)

        def normalise(a):
            dve.wait_ge(sink_ready, a + 1)
            then(nc.vector.tensor_tensor(den[:, a, :], den[:, a, :], sink_e[:, a, :], ALU.add))
            then(nc.vector.reciprocal(den[:, a, :], den[:, a, :]))
            for g in range(2):
                dve.wait_ge(pv_done, (2, 4, 8, 12)[2 * a + g])
                nc.vector.tensor_tensor(
                    o_tok[:, a, N * g:N * g + N].rearrange("p (h d) -> p h d", d=HD),
                    bank[O_BANKS[2 * a + g]][:].rearrange("p (h d) -> p h d", d=HD),
                    den[:, a, QPK * g:QPK * g + QPK].unsqueeze(2).broadcast_to([P, QPK, HD]), ALU.mult).then_inc(o_ready, 1)

        for i in range(12):
            row_max(i)
            if i == 0:
                turned_keys(1)
            if i:
                evacuate_probs(i - 1)
            if i == 5:
                normalise(0)
            if i == 7:
                split_lo(WO0 + 2)
            if i in (9, 10):
                nc.vector.tensor_tensor(h[:, i - 9, :], h[:, i - 9, :], b_o[:], ALU.add).then_inc(dve_const, 1)
            if i == 10:
                turned_lo(12, 0, OT_BANKS)
        evacuate_probs(11)
        normalise(1)
        turned_lo(12, 1, OT_BANKS)
        split_lo(WO0 + 3)
        dve.wait_ge(dve_const, 1 + TT)

        for a in range(TT):
            add_to_h(2, FRONT - 1, WO_ACC, a)
            norm_scale(3, a)
        for a in range(TT):
            dve.wait_ge(logits_done, a + 1)
            then(nc.vector.tensor_copy(logits[:, a, :], bank[OT_BANKS[2 * a]][:, 0:NE]))
            then(nc.vector.max(top_v[:, a, :], logits[:, a, :]))
            then(nc.vector.max_index(top_i[:, a, :], top_v[:, a, :], logits[:, a, :]))
        nc.vector.tensor_tensor(diff[:], top_v[:, :, 1], top_v[:, :, 0], ALU.subtract).then_inc(diff_ready, 1)
        then(nc.vector.tensor_copy(top_f[:], top_i[:, :, 0:2]))
        for a in range(TT):
            for i in range(2):
                then(nc.vector.tensor_scalar(oh[:, a, i, :], iota_s[:, 0:NE], top_f[:, a, i:i + 1], None, ALU.is_equal))
        nc.vector.tensor_tensor(sel[:], oh[:, :, 0, :], oh[:, :, 1, :], ALU.add).then_inc(sel_ready, 1)
        dve.wait_ge(p2_ready, 1)
        then(nc.vector.tensor_scalar(psum_g[:], p2[:], 1.0, None, ALU.add))
        then(nc.vector.reciprocal(g1[:], psum_g[:]))
        then(nc.vector.tensor_tensor(g2[:], p2[:], g1[:], ALU.mult))
        for a in range(TT):
            then(nc.vector.tensor_scalar(gate_of[:, a, 0:NE], oh[:, a, 0, :], g1[:, a:a + 1], None, ALU.mult))
            then(nc.vector.scalar_tensor_tensor(out=gate_of[:, a, 0:NE], in0=oh[:, a, 1, :], scalar=g2[:, a:a + 1],
                                                in1=gate_of[:, a, 0:NE], op0=ALU.mult, op1=ALU.add))
        then(nc.vector.tensor_copy(gate_of[:, :, NE:BLOCKS], gate_of[:, :, 0:NE]))
        then(nc.vector.memset(slot_of[:], -1.0))
        dve.wait_ge(rank_done, 1)
        for a in range(TT):
            then(nc.vector.tensor_tensor(slot_of[:, a, 0:NE], sel[:, a, :], bank[4][:, NE * a:NE * a + NE], ALU.mult))
        then(nc.vector.tensor_scalar(slot_of[:, :, 0:NE], slot_of[:, :, 0:NE], 1.0, None, ALU.subtract))
        then(nc.vector.tensor_scalar(slot_of[:, :, NE:BLOCKS], slot_of[:, :, 0:NE], float(P), None, ALU.subtract))
        then(nc.vector.tensor_reduce(cmax_f[:], bank[4][:, TT * NE:(TT + 1) * NE], AX_X, ALU.max))
        nc.vector.tensor_copy(count_max[:], cmax_f[:]).then_inc(routed, 1)

        def expert_lo(b, q):
            dve.wait_ge(hi_ready, b * EP + (FRONT + q + 1))
            nc.vector.tensor_tensor(w_lo[:, (FRONT + q) % SPLITS, :], ring[q % RING][:],
                                    w_hi[:, (FRONT + q) % SPLITS, :].bitcast(F32), ALU.subtract).then_inc(lo_ready, 1)

        def make_pick(blk):
            for a in range(TT):
                nc.vector.tensor_scalar(pick[:, a, :], iota_s[:], slot_of[:, a, bass.ds(blk, 1)], None,
                                        ALU.is_equal).then_inc(pick_ready, 1)

        def gathered_lo(count):
            for i in range(2):
                dve.wait_ge(gT_hi_ready, count + (i + 1))
                nc.vector.tensor_tensor(gT_lo[:, 4 * i:4 * i + 4, :], bank[2 + i][:].rearrange("p (k s) -> p k s", k=4),
                                        gT_hi[:, 4 * i:4 * i + 4, :].bitcast(F32), ALU.subtract).then_inc(gT_lo_ready, 1)

        def hidden_lo(count):
            dve.wait_ge(eT_hi_ready, count)
            nc.vector.tensor_tensor(eT_lo[:], bank[6][:].rearrange("p (k s) -> p k s", k=4), eT_hi[:].bitcast(F32),
                                    ALU.subtract).then_inc(eT_lo_ready, 1)

        def expert_los(b, q0, q1):
            for q in range(q0, q1):
                expert_lo(b, q)

        def add_scattered(n, i, dst_bank):
            dve.wait_ge(scattered, n * 4 + (i + 1))
            dve.wait_ge(e_added, n * 4 + (i + 1))
            hs = h[:, i // 2, N * (i % 2):N * (i % 2) + N]
            nc.vector.tensor_tensor(hs, hs, dst_bank[:], ALU.add).then_inc(e_added, 1)

        def expert_block(b, n, last):
            at = AHEAD
            for j in range(EU):
                g, up, d = expert_pieces(j)
                if j:
                    expert_los(b, at, g + 4)
                    at = g + 4
                    hidden_lo(b * EU + j)
                expert_los(b, at, min(up + 4, EP))
                at = min(up + 4, EP)
                dve.wait_ge(e_silu, b * EU + (j + 1))
                dve.wait_ge(piece_used, b * EP + (FRONT + up + 2))
                nc.vector.tensor_tensor(e_a[:], e_a[:], bank[2 * (j % 2) + 1][:], ALU.mult).then_inc(e_act, 1)
                if j < 4:
                    add_scattered(n, j, bank[7])
                if j == 4:
                    for a in range(TT):
                        nc.vector.tensor_scalar(pick_g[:, a, :], iota_s[:], slot_of[:, a, bass.ds(b, 1)],
                                                gate_of[:, a, bass.ds(b, 1)], ALU.is_equal, ALU.mult).then_inc(pickg_ready, 1)
                    if not last:
                        make_pick(b + 1)
            expert_los(b, at, EP)
            hidden_lo(b * EU + EU)
            if not last:
                gathered_lo(b * 2 + 2)
            dve.wait_ge(pickg_t, b + 1)
            nc.vector.tensor_copy(pick_gT[:], bank[7][:, 0:T]).then_inc(pickgT_ready, 1)
            if not last:
                expert_los(b + 1, 0, AHEAD)

        def last_scatter(n):
            for i in range(4):
                add_scattered(n, i, bank[ACC[i]])
            dve.wait_ge(e_added, 4 * n + 5)

        def nothing_scattered():
            nc.vector.memset(pick_gT[:], 0.0).then_inc(zeroed, 1)

        dve.wait_ge(routed, 1)
        make_pick(0)
        nothing_scattered()
        gathered_lo(0)
        expert_los(0, 0, AHEAD)
        nc.vector.memset(cmax_f[:], 0.0).then_inc(e_added, 1)
        with dve.Fori(0, NE - 1) as b:
            expert_block(b, b, False)
        most = nc.vector.value_load(count_max[0:1, 0:1], min_val=0, max_val=T)
        expert_block(NE - 1, NE - 1, True)
        last_scatter(NE)
        with dve.If(most > P):
            make_pick(NE)
            nothing_scattered()
            gathered_lo(2 * NE)
            expert_los(NE, 0, AHEAD)
            with dve.Fori(NE, BLOCKS - 1) as b:
                expert_block(b, b + 1, False)
            expert_block(BLOCKS - 1, BLOCKS, True)
            last_scatter(BLOCKS + 1)

        nc.vector.tensor_tensor_reduce(out=xn[:, 1, :], in0=h[:, 1, :], in1=h[:, 1, :], scale=1.0, scalar=0.0,
                                       op0=ALU.mult, op1=ALU.add, accum_out=ssq[:, 1:2]).then_inc(h_final, 1)
        dve.wait_ge(h_final, 1)
        dve.wait_ge(sq_ready, 4 * TT + 1)
        then(nc.vector.tensor_scalar(var[:], ssq[:], 1.0 / D, EPS, ALU.mult, ALU.add))
        rsqrt(rstd[:], var[:], newton[:])
        dve.wait_ge(ld_gain[0], 16 * 3)
        for a in range(TT):
            nc.vector.scalar_tensor_tensor(out=xn[:, a, :], in0=h[:, a, :], scalar=rstd[:, a:a + 1], in1=gain[:, 0, :],
                                           op0=ALU.mult, op1=ALU.mult).then_inc(h_final, 1)

    @block.tensor
    def _(pe):
        mm = nc.tensor.matmul

        def mm3(dst, weight_moves, w, t, start, stop):
            (w_h, w_l), (t_h, t_l) = w, t
            for i, (a, b) in enumerate(((w_h, t_h), (w_h, t_l), (w_l, t_h))):
                fixed, moving = (b, a) if weight_moves else (a, b)
                ins = mm(dst, fixed, moving, start=start and i == 0, stop=stop and i == 2)
            return ins

        def turn(src, a, banks):
            for k in range(KT):
                ins = nc.tensor.transpose(bank[banks[2 * a + k // 4]][:, P * (k % 4):P * (k % 4) + P],
                                          src[:, a, P * k:P * k + P], ident[:])
                if k % 4 == 3:
                    ins.then_inc(norm_t, 1)

        def norm_turn(n, a, banks=NORM_BANKS):
            pe.wait_ge(xn_ready, TT * n + a + 1)
            turn(xn, a, banks)

        def rows_product(p, kts, xh, xl, banks, first, last, tiles=(0, 1)):
            pe.wait_ge(lo_ready, p + 1)
            for a in tiles:
                for half in range(2):
                    for kk, k in enumerate(kts):
                        ins = mm3(bank[banks[2 * a + half]][:], True,
                                  (hi(p, 2)[:, kk, N * half:N * half + N], lo(p, 2)[:, kk, N * half:N * half + N]),
                                  (xh[:, k, P * a:P * a + P], xl[:, k, P * a:P * a + P]),
                                  first and kk == 0, last and kk == 1)
                    if last and (a, half) != (1, 1):
                        ins.then_inc(acc_done, 1)
            if 1 in tiles:
                ins.then_inc(piece_used, 1)

        def columns_product(p, dst, tiles=None):
            pe.wait_ge(lo_ready, p + 1)
            t0, t1 = (0, T) if tiles is None else (P * tiles[0], P * tiles[0] + P)
            for c in range(2):
                for k in range(KT):
                    ins = mm3(dst[:, T * c + t0:T * c + t1], False,
                              (hi(p, KT)[:, k, P * c:P * c + P], lo(p, KT)[:, k, P * c:P * c + P]),
                              (xT_hi[:, k, t0:t1], xT_lo[:, k, t0:t1]), k == 0, k == KT - 1)
            if tiles != (0,):
                ins.then_inc(piece_used, 1)

        def tokens_product(p, k0, nk, w, banks, tiles=(0, 1), signal=None):
            pe.wait_ge(lo_ready, p + 1)
            for a in tiles:
                for kk in range(nk):
                    k = k0 + kk
                    ins = mm3(bank[banks[a]][:, 0:w], True, (hi(p, nk)[:, kk, :], lo(p, nk)[:, kk, :]),
                              (xT_hi[:, k, P * a:P * a + P], xT_lo[:, k, P * a:P * a + P]), k == 0, k == KT - 1)
                if a == 0 and signal is not None:
                    ins.then_inc(signal, 1)
            if 1 in tiles:
                ins.then_inc(piece_used, 1)


        pe.wait_ge(pool_const, 3)
        norm_turn(0, 0)
        pe.wait_ge(xT_lo_ready, 2)
        for i in range(2):
            tokens_product(V0 + i, 4 * i, 4, N, (6, 7), tiles=(0,))
            if i == 0:
                norm_turn(0, 1)
        pe.wait_ge(xT_lo_ready, 4)
        for i in range(2):
            tokens_product(V0 + i, 4 * i, 4, N, (6, 7), tiles=(1,))
        pe.wait_ge(pool_spw, 1)
        for g in range(GH):
            ins = nc.tensor.transpose(bank[4][:, P * g:P * g + P], sp_w[:, g, :], ident[:])
        ins.then_inc(spw_t, 1)
        for c in range(2):
            columns_product(U0 + c, bank[c])
        for c in range(2):
            columns_product(C0 + c, bank[2 + c])
        pe.wait_ge(v_gelu, TT)
        for c in range(2):
            columns_product(X0 + c, bank[6 + c])
        pe.wait_ge(spw_ready, 1)
        pe.wait_ge(vn_ready, TT)
        for g in range(GH):
            for a in range(TT):
                c0 = T * (g % 2) + P * a
                ins = mm(bank[4 + g // 2][:, c0:c0 + P], v_act[:, a, P * g:P * g + P], sp_wT[:, g, :],
                         start=True, stop=True)
            if g % 2:
                ins.then_inc(mix_done, 1)
        pe.wait_ge(uT_ready, 2)
        for c in range(2):
            columns_product(B0 + c, bank[c])

        def mixer_out(i, tiles=(0, 1)):
            rows_product(WOUT0 + i, OUT_KT[2 * i:2 * i + 2], yT_hi, yT_lo, ACC, i == 0, i == 3, tiles)

        pe.wait_ge(yT_lo_ready, 2)
        mixer_out(0)
        mixer_out(1, (0,))
        pe.wait_ge(yT_lo_ready, 4)
        for i in (2, 3):
            mixer_out(i, (0,))
        for i in (1, 2):
            mixer_out(i, (1,))
        norm_turn(1, 0)
        mixer_out(3, (1,))

        def ffn_down(u, tiles=(0, 1)):
            pe.wait_ge(fT_lo_ready, u + 1)
            rows_product(ffn_pieces(u)[2], (0, 1), fT_hi[:, u % 2], fT_lo[:, u % 2], ACC, u == 0, u == FU - 1, tiles)

        for u in range(FU):
            g, up, _ = ffn_pieces(u)
            gb, ub = bank[(0, 4)[u % 2]], bank[(1, 5)[u % 2]]
            if u == 0:
                pe.wait_ge(xT_lo_ready, 6)
                columns_product(g, gb, (0,))
                columns_product(up, ub, (0,))
                norm_turn(1, 1)
                pe.wait_ge(xT_lo_ready, 8)
                columns_product(g, gb, (1,))
                columns_product(up, ub, (1,))
            else:
                if u >= 2:
                    pe.wait_ge(act_ready, u - 1)
                columns_product(g, gb)
                columns_product(up, ub)
                ffn_down(u - 1, (0, 1) if u < FU - 1 else (0,))
        ffn_down(FU - 1, (0,))
        ffn_down(FU - 2, (1,))
        norm_turn(2, 0)
        ffn_down(FU - 1, (1,))

        KV, Q0, Q1 = (0, 1), (2, 3), (6, 7)
        pe.wait_ge(xT_lo_ready, 10)
        tokens_product(QKV0, 0, KT, 2 * NKV * HD, KV, (0,), qkv_done)
        tokens_product(QKV0 + 1, 0, 4, N, Q0, (0,))
        norm_turn(2, 1)
        pe.wait_ge(xT_lo_ready, 12)
        tokens_product(QKV0, 0, KT, 2 * NKV * HD, KV, (1,))
        tokens_product(QKV0 + 1, 0, 4, N, Q0, (1,))
        tokens_product(QKV0 + 2, 4, 4, N, Q0, (0, 1), qkv_done)
        for a in range(TT):
            tokens_product(QKV0 + 3, 0, 4, N, Q1, (a,))
            tokens_product(QKV0 + 4, 4, 4, N, Q1, (a,), qkv_done if a == 0 else None)

        def turn_heads(a):
            pe.wait_ge(rope_ready, 2 * a + 2)
            for g in range(NKV):
                for i in range(2):
                    c0 = P * (2 * g + i)
                    ins = nc.tensor.transpose(bank[4 + a][:, c0:c0 + P], k_pad[:, a, g, i, :], ident[:])
            ins.then_inc(qk_t, 1)
            for c in range(NQ // 2):
                ins = nc.tensor.transpose(bank[2 * a + c // 4][:, P * (c % 4):P * (c % 4) + P],
                                          qkv[:, a, P * c:P * c + P], ident[:])
                if c % 4 == 3:
                    ins.then_inc(qk_t, 1)

        def scores(i):
            a, n, first = (0, 4, 4 * i) if i < 4 else (1, 2, 2 * (i - 4))
            if i >= 2:
                pe.wait_ge(probs_ready, i - 1)
            s, w = bank[S_BANKS[i % 2]], N // n
            mask = mask0 if a == 0 else mask1
            mm(s[:], ident_b[:], mask[:].rearrange("p h k -> p (h k)"), start=True, stop=False)
            for j in range(n):
                hq = first + j
                ins = mm(s[:, w * j:w * j + w], qT[:, hq // 2, P * a:P * a + P], kT[:, hq // QPK, hq % 2, 0:w],
                         start=False, stop=j == n - 1)
            ins.then_inc(s_done, 1)

        def transpose_probs(i):
            pe.wait_ge(probs_ready, i + 1)
            if i >= 2:
                pe.wait_ge(probsT_ready, i - 1)
            for c in range(4):
                ins = nc.tensor.transpose(bank[4 + i % 2][:, P * c:P * c + P], probs[:, i % 2, P * c:P * c + P], ident[:])
            ins.then_inc(probs_t, 1)

        def weigh_values(i):
            a, n, first = (0, 4, 4 * i) if i < 4 else (1, 2, 2 * (i - 4))
            pe.wait_ge(probsT_ready, i + 1)
            for j in range(n):
                hq = first + j
                o = bank[O_BANKS[2 * a + hq // QPK]][:, HD * (hq % QPK):HD * (hq % QPK) + HD]
                v0 = (NQ + NKV + hq // QPK) * HD
                for kt in range(a + 1):
                    c = (a + 1) * j + kt
                    ins = mm(o, probsT[:, i % 2, P * c:P * c + P], qkv[:, kt, v0:v0 + HD], start=kt == 0, stop=kt == a)
            ins.then_inc(pv_done, 1)

        turn_heads(0)
        turn_heads(1)
        pe.wait_ge(pool_const, 7)
        pe.wait_ge(qkT_act, 2)
        pe.wait_ge(qkT_dve, 1)
        for i in range(14):
            if i == 1:
                pe.wait_ge(qkT_act, 4)
                pe.wait_ge(qkT_dve, 2)
            if i < 12:
                scores(i)
            if 1 <= i < 13:
                transpose_probs(i - 1)
            if i >= 2:
                weigh_values(i - 2)
            if i == 8:
                pe.wait_ge(o_ready, 2)
                turn(o_tok, 0, OT_BANKS)

        def attention_out(i, tiles):
            rows_product(WO0 + i, (2 * i, 2 * i + 1), xT_hi, xT_lo, WO_ACC, i == 0, i == 3, tiles)

        pe.wait_ge(xT_lo_ready, 14)
        for i in range(3):
            attention_out(i, (0,))
        pe.wait_ge(o_ready, 4)
        turn(o_tok, 1, OT_BANKS)
        pe.wait_ge(xT_lo_ready, 16)
        attention_out(0, (1,))
        attention_out(3, (0,))
        attention_out(1, (1,))
        attention_out(2, (1,))
        norm_turn(3, 0, OT_BANKS)
        attention_out(3, (1,))

        pe.wait_ge(ld_router, 16)
        for a in range(TT):
            if a:
                norm_turn(3, 1, OT_BANKS)
            pe.wait_ge(xTr_ready, 2 * a + 2)
            for k in range(KT):
                ins = mm(bank[OT_BANKS[2 * a]][:, 0:NE], xT[:, k, P * a:P * a + P], router[:, k, :],
                         start=k == 0, stop=k == KT - 1)
            ins.then_inc(logits_done, 1)
        pe.wait_ge(sel_ready, 1)
        r = bank[4]
        mm(r[:, 0:NE], tri[:], sel[:, 0, :], start=True, stop=True)
        mm(r[:, NE:2 * NE], ones[:], sel[:, 0, :], start=True, stop=False)
        mm(r[:, NE:2 * NE], tri[:], sel[:, 1, :], start=False, stop=True)
        mm(r[:, 2 * NE:3 * NE], ones[:], sel[:, 0, :], start=True, stop=False)
        mm(r[:, 2 * NE:3 * NE], ones[:], sel[:, 1, :], start=False, stop=True).then_inc(rank_done, 1)

        def gather():
            for k in range(KT):
                for a in range(TT):
                    ins = mm(bank[2 + k // 4][:, P * (k % 4):P * (k % 4) + P], xn[:, a, P * k:P * k + P], pick[:, a, :],
                             start=a == 0, stop=a == TT - 1)
                if k % 4 == 3:
                    ins.then_inc(gathered, 1)

        def expert_in(b, q, k0, dst):
            s = FRONT + q
            pe.wait_ge(lo_ready, b * EP + (s + 1))
            for kk in range(4):
                k = k0 + kk
                ins = mm3(dst[:], True, (hi(s, 4)[:, kk, :], lo(s, 4)[:, kk, :]), (gT_hi[:, k, :], gT_lo[:, k, :]),
                          k == 0, k == KT - 1)
            ins.then_inc(piece_used, 1)

        def expert_down(b, j):
            d = expert_pieces(j)[2]
            pe.wait_ge(eT_lo_ready, b * EU + (j + 1))
            for i in range(2):
                s = FRONT + d + i
                pe.wait_ge(lo_ready, b * EP + (s + 1))
                for kk in range(2):
                    k = 2 * i + kk
                    for half in range(2):
                        ins = mm3(bank[4 + half][:], True,
                                  (hi(s, 2)[:, kk, N * half:N * half + N], lo(s, 2)[:, kk, N * half:N * half + N]),
                                  (eT_hi[:, k, :], eT_lo[:, k, :]), j == 0 and k == 0, j == EU - 1 and k == 3)
                ins.then_inc(piece_used, 1)

        def transpose_hidden(b, j):
            pe.wait_ge(e_act, b * EU + (j + 1))
            for k in range(4):
                ins = nc.tensor.transpose(bank[6][:, P * k:P * k + P], e_a[:, P * k:P * k + P], ident[:])
            ins.then_inc(e_t, 1)

        def scatter(i, dst_bank):
            a, half = i // 2, i % 2
            mm(dst_bank[:], pick_gT[:, P * a:P * a + P], e_y[:, N * half:N * half + N],
               start=True, stop=True).then_inc(scattered, 1)

        def expert_block(b, n, last):
            pe.wait_ge(gT_lo_ready, b * 2 + 2)
            for j in range(EU):
                g, up, _ = expert_pieces(j)
                if j >= 2:
                    pe.wait_ge(e_act, b * EU + (j - 1))
                for i in range(2):
                    expert_in(b, g + i, 4 * i, bank[2 * (j % 2)])
                if j:
                    transpose_hidden(b, j - 1)
                for i in range(2):
                    expert_in(b, up + i, 4 * i, bank[2 * (j % 2) + 1])
                if j == 0:
                    pe.wait_ge(ey_ready, n + 1)
                if j < 4:
                    pe.wait_ge(e_added, n * 4 + (j + 1))
                    scatter(j, bank[7])
                if j:
                    expert_down(b, j - 1)
            transpose_hidden(b, EU - 1)
            if not last:
                pe.wait_ge(pick_ready, b * TT + 2 * TT)
                gather()
            pe.wait_ge(pickg_ready, b * TT + TT)
            for a in range(TT):
                ins = nc.tensor.transpose(bank[7][:, P * a:P * a + P], pick_g[:, a, :], ident[:])
            ins.then_inc(pickg_t, 1)
            expert_down(b, EU - 1)
            pe.wait_ge(pickgT_ready, b + 1)
            if last:
                pe.wait_ge(ey_ready, n + 2)
                for i in range(4):
                    scatter(i, bank[ACC[i]])

        pe.wait_ge(pick_ready, TT)
        gather()
        pe.wait_ge(zeroed, 1)
        with pe.Fori(0, NE - 1) as b:
            expert_block(b, b, False)
        most = nc.tensor.value_load(count_max[0:1, 0:1], min_val=0, max_val=T)
        expert_block(NE - 1, NE - 1, True)
        with pe.If(most > P):
            pe.wait_ge(pick_ready, NE * TT + TT)
            gather()
            pe.wait_ge(zeroed, 2)
            with pe.Fori(NE, BLOCKS - 1) as b:
                expert_block(b, b + 1, False)
            expert_block(BLOCKS - 1, BLOCKS, True)

    ctx.close()


_INS = ['x', 'positions', 'final_norm_g', 'ev_norm1_g', 'ev_w_in', 'ev_conv_w', 'ev_ln_g', 'ev_ln_b',
        'ev_spatial_w', 'ev_spatial_b', 'ev_w_out', 'ev_norm2_g', 'ev_ffn_wg', 'ev_ffn_wu', 'ev_ffn_wd',
        'od_norm1_g', 'od_w_qkv', 'od_b_qkv', 'od_sinks', 'od_w_o', 'od_b_o', 'od_norm2_g', 'od_router_w',
        'od_exp_wg', 'od_exp_wu', 'od_exp_wd']


def kernel(**inputs):
    import concourse.bacc as bacc
    from concourse.bass_utils import run_bass_kernel_spmd

    nc = bacc.Bacc("TRN2", target_bir_lowering=False, num_devices=1)
    arrays, args = {}, []
    for name in _INS:
        a = np.ascontiguousarray(inputs[name])
        arrays[f"in_{name}"] = a
        args.append(nc.dram_tensor(f"in_{name}", a.shape, mybir.dt.from_np(a.dtype), kind="ExternalInput").ap())
    out = nc.dram_tensor("out_0", (1, T, D), F32, kind="ExternalOutput").ap()
    build(nc, *args, out)
    return run_bass_kernel_spmd(nc, [arrays], core_ids=[0]).results[0]["out_0"]
```

```python
from contextlib import ExitStack

import numpy as np

import concourse.bass as bass
from concourse import mybir

ALU = mybir.AluOpType
ACT = mybir.ActivationFunctionType
F32 = mybir.dt.float32
F32R = mybir.dt.float32r
BF16 = mybir.dt.bfloat16
I32 = mybir.dt.int32
U32 = mybir.dt.uint32
AX_X = mybir.AxisListType.X

P = 128
D = 1024
KT = D // P
T = 256
TT = T // P
EPS = 1e-5
N = 512

CONV = 512
CT = CONV // P
CW = 3
GM = 512
MIX_IN = 3 * CONV + 2 * GM
GH = 4
FFN = 2816
FU = FFN // 256

HD = 64
NQ = 16
NKV = 2
QPK = NQ // NKV
QKV = (NQ + 2 * NKV) * HD
ROPE = HD // 4
RH = ROPE // 2
THETA = 500000.0
SCALE = HD ** -0.5
MASKED = -1e30

NE = 8
ED = 3584
EU = ED // N
BLOCKS = 2 * NE

PIECE = 2048
SPLITS = 3
RING_A = 7
RING = 14
AHEAD = 3
EP = 6 * EU

V0, U0, C0, X0, B0 = 0, 2, 4, 6, 8
WOUT0 = 10
FFN0 = WOUT0 + 4
QKV0 = FFN0 + 3 * FU
WO0 = QKV0 + 5
FRONT = WO0 + 4
OUT_KT = (4, 5, 6, 7, 0, 1, 2, 3)

assert FRONT % RING_A == 0 and EP % RING == 0 and EP % SPLITS == 0


def ffn_pieces(u):
    g = FFN0 + (0 if u == 0 else 3 * u - 1)
    d = FFN0 + 3 * u + 4 if u < FU - 1 else FFN0 + 3 * FU - 1
    return g, g + 1, d


def expert_pieces(j):
    g = 0 if j == 0 else 6 * j - 2
    d = 6 * j + 8 if j < EU - 1 else EP - 2
    return g, g + 2, d


def build(nc, x, positions, final_norm_g, ev_norm1_g, ev_w_in, ev_conv_w, ev_ln_g, ev_ln_b,
          ev_spatial_w, ev_spatial_b, ev_w_out, ev_norm2_g, ev_ffn_wg, ev_ffn_wu, ev_ffn_wd,
          od_norm1_g, od_w_qkv, od_b_qkv, od_sinks, od_w_o, od_b_o, od_norm2_g, od_router_w,
          od_exp_wg, od_exp_wu, od_exp_wd, out):
    ctx = ExitStack()

    def sb(name, shape, dt=F32, scope=None):
        return (scope or ctx).enter_context(nc.sbuf_tensor(name, shape, dt))

    def sem(name):
        return ctx.enter_context(nc.semaphore(name))

    ring_a = [sb(f"ring{s}", [P, PIECE]) for s in range(RING_A)]
    w_hi = sb("w_hi", [P, SPLITS, PIECE], F32R)
    w_lo = sb("w_lo", [P, SPLITS, PIECE], F32R)
    h = sb("h", [P, TT, D])
    xn = sb("xn", [P, TT, D])
    ident = sb("ident", [P, P])
    gain_even = sb("gain_even", [P, D])
    ssq = sb("ssq", [P, TT])
    ssq_half = sb("ssq_half", [P, TT, 2])
    neg_var = sb("neg_var", [P, TT])
    newton = sb("newton", [P, TT])
    table_warm = sb("table_warm", [P, 1])
    rstd = sb("rstd", [P, TT])
    router = sb("router", [P, KT, NE])
    ones = sb("ones", [P, P])
    tri = sb("tri", [P, P])
    iota_s = sb("iota_s", [P, P])
    cmax_f = sb("cmax_f", [P, 1])
    count_max = sb("count_max", [P, 1], I32)
    slot_of = sb("slot_of", [P, TT, BLOCKS + 1])
    gate_of = sb("gate_of", [P, TT, BLOCKS])

    g_ = ExitStack()
    gain_odd = sb("gain_odd", [P, D], F32, g_)
    gain = (gain_even, gain_odd)

    s1 = ExitStack()
    xT_hi = sb("xT_hi", [P, KT, T], F32R, s1)
    xT_lo = sb("xT_lo", [P, KT, T], F32R, s1)
    m_ = ExitStack()
    yT_hi = sb("yT_hi", [P, KT, T], F32R, m_)
    yT_lo = sb("yT_lo", [P, KT, T], F32R, m_)
    yT = sb("yT", [P, 4, T], F32, m_)
    v_act = sb("v_act", [P, TT, GM], F32, m_)
    uT = sb("uT", [P, GH, T], F32, m_)
    acT = sb("acT", [P, CT, T], F32, m_)
    hc = sb("hc", [P, CT, T + CW - 1], F32, m_)
    cv = sb("cv", [P, CT, T], F32, m_)
    ln_g = sb("ln_g", [P, GM], F32, m_)
    ln_b = sb("ln_b", [P, GM], F32, m_)
    sp_w = sb("sp_w", [P, GH, P], F32, m_)
    sp_wT = sb("sp_wT", [P, GH, P], F32, m_)
    sp_b = sb("sp_b", [P, GH, P], F32, m_)
    conv_w = sb("conv_w", [P, CT, CW], F32, m_)
    bn = sb("bn", [P, TT, 6], F32, m_)
    mv = sb("mv", [P, TT, 2], F32, m_)
    m_.close()

    f_ = ExitStack()
    f_s = sb("f_s", [P, 2, T], F32, f_)
    f_a = sb("f_a", [P, 2, T], F32, f_)
    fT_hi = sb("fT_hi", [P, 2, 2, T], F32R, f_)
    fT_lo = sb("fT_lo", [P, 2, 2, T], F32R, f_)
    f_.close()

    a_ = ExitStack()
    qT = sb("qT", [P, NQ // 2, T], F32, a_)
    probs = sb("probs", [P, 2, N], F32, a_)
    b_qkv = sb("b_qkv", [P, QKV], F32, a_)
    b_o = sb("b_o", [P, D], F32, a_)
    sinks = sb("sinks", [P, NQ], F32, a_)
    neg_sinks = sb("neg_sinks", [P, NQ], F32, a_)
    pos_i = sb("pos_i", [P, TT], I32, a_)
    pos_f = sb("pos_f", [P, TT], F32, a_)
    inv_freq = sb("inv_freq", [P, RH], F32, a_)
    ang = sb("ang", [P, TT, RH], F32, a_)
    turns = sb("turns", [P, TT, RH], F32, a_)
    red = sb("red", [P, TT, RH], F32, a_)
    red_c = sb("red_c", [P, TT, RH], F32, a_)
    sin_t = sb("sin_t", [P, TT, RH], F32, a_)
    cos_t = sb("cos_t", [P, TT, RH], F32, a_)
    mask0 = sb("mask0", [P, 4, P], BF16, a_)
    mask1 = sb("mask1", [P, 2, T], BF16, a_)
    ident_b = sb("ident_b", [P, P], BF16, a_)
    qkv = sb("qkv", [P, TT, QKV], F32, a_)
    rope_t = sb("rope_t", [P, 4, TT, (NQ + NKV) * RH], F32, a_)
    k_pad = sb("k_pad", [P, TT, NKV, 2, 2 * HD], F32, a_)
    kT = sb("kT", [P, NKV, 2, T], F32, a_)
    probsT = sb("probsT", [P, 2, N], F32, a_)
    raw_max = sb("raw_max", [P, TT, NQ], F32, a_)
    neg_max = sb("neg_max", [P, TT, NQ], F32, a_)
    den = sb("den", [P, TT, NQ], F32, a_)
    sink_e = sb("sink_e", [P, TT, NQ], F32, a_)
    o_tok = xn
    a_.close()
    s1.close()
    g_.close()

    ey_lo = sb("ey_lo", [P, D], F32R)
    ring_b = [sb(f"ring{s}", [P, PIECE]) for s in range(RING_A, RING)]
    ring = ring_a + ring_b[2:] + ring_b[:2]
    r_ = ExitStack()
    xT = sb("xT", [P, KT, T], F32, r_)
    r_.close()
    gT_hi = sb("gT_hi", [P, KT, P], F32R)
    gT_lo = sb("gT_lo", [P, KT, P], F32R)
    t_ = ExitStack()
    logits = sb("logits", [P, TT, NE], F32, t_)
    top_v = sb("top_v", [P, TT, 8], F32, t_)
    top_i = sb("top_i", [P, TT, 8], U32, t_)
    top_f = sb("top_f", [P, TT, 2], F32, t_)
    diff = sb("diff", [P, TT], F32, t_)
    p2 = sb("p2", [P, TT], F32, t_)
    psum_g = sb("psum_g", [P, TT], F32, t_)
    g1 = sb("g1", [P, TT], F32, t_)
    g2 = sb("g2", [P, TT], F32, t_)
    oh = sb("oh", [P, TT, 2, NE], F32, t_)
    sel = sb("sel", [P, TT, NE], F32, t_)
    t_.close()
    e_a = sb("e_a", [P, N])
    eT_hi = sb("eT_hi", [P, 4, P], F32R)
    eT_lo = sb("eT_lo", [P, 4, P], F32R)
    ey_hi = sb("ey_hi", [P, D], F32R)
    pick = sb("pick", [P, TT, P])
    gate_col = sb("gate_col", [P, TT])
    pickT = sb("pickT", [P, T], F32R)
    gate_slot = sb("gate_slot", [P, 1])

    bank = [ctx.enter_context(nc.psum_tensor(f"bank{i}", [P, N], F32)) for i in range(8)]

    landed = [sem(f"landed{s}") for s in range(RING)]
    hi_ready, lo_ready, piece_used = sem("hi_ready"), sem("lo_ready"), sem("piece_used")
    ld_x, ld_gain = [sem("ld_x0"), sem("ld_x1")], [sem("ld_gain0"), sem("ld_gain1")]
    ld_spw, ld_even, ld_odd, ld_router = sem("ld_spw"), sem("ld_even"), sem("ld_odd"), sem("ld_router")
    stored = sem("stored")
    pool_step, pool_const, pool_spw = sem("pool_step"), sem("pool_const"), sem("pool_spw")
    dve_step = sem("dve_step")
    dve_const = sem("dve_const")
    spw_t, spw_ready = sem("spw_t"), sem("spw_ready")
    sq_ready, xn_ready = sem("sq_ready"), sem("xn_ready")
    norm_t = sem("norm_t")
    xT_hi_ready, xT_lo_ready = sem("xT_hi_ready"), sem("xT_lo_ready")
    v_gelu = sem("v_gelu")
    vn_ready = sem("vn_ready")
    uT_ready, acT_ready = sem("uT_ready"), sem("acT_ready")
    mix_done, y_ready, yT_hi_ready, yT_lo_ready = sem("mix_done"), sem("y_ready"), sem("yT_hi_ready"), sem("yT_lo_ready")
    acc_done, h_added = sem("acc_done"), sem("h_added")
    silu_ready, act_ready = sem("silu_ready"), sem("act_ready")
    fT_hi_ready, fT_lo_ready = sem("fT_hi_ready"), sem("fT_lo_ready")
    red_ready, trig_ready = sem("red_ready"), sem("trig_ready")
    qkv_done, qkv_ready, rope_ready = sem("qkv_done"), sem("qkv_ready"), sem("rope_ready")
    qk_t, qkT_act, qkT_dve = sem("qk_t"), sem("qkT_act"), sem("qkT_dve")
    s_done, max_ready, probs_ready = sem("s_done"), sem("max_ready"), sem("probs_ready")
    probs_t, probsT_ready, pv_done = sem("probs_t"), sem("probsT_ready"), sem("pv_done")
    sink_arg, sink_ready, o_ready = sem("sink_arg"), sem("sink_ready"), sem("o_ready")
    h_final = sem("h_final")
    logits_done, diff_ready, p2_ready = sem("logits_done"), sem("diff_ready"), sem("p2_ready")
    xTr_ready, sel_ready, rank_done, routed = sem("xTr_ready"), sem("sel_ready"), sem("rank_done"), sem("routed")
    pick_ready, pick_t, pickT_ready = sem("pick_ready"), sem("pick_t"), sem("pickT_ready")
    gathered, gT_hi_ready, gT_lo_ready = sem("gathered"), sem("gT_hi_ready"), sem("gT_lo_ready")
    e_silu, e_act, e_t = sem("e_silu"), sem("e_act"), sem("e_t")
    eT_hi_ready, eT_lo_ready = sem("eT_hi_ready"), sem("eT_lo_ready")
    ey_hi_ready, ey_lo_ready, scattered = sem("ey_hi_ready"), sem("ey_lo_ready"), sem("scattered")
    e_added = sem("e_added")

    x_v = x[0].rearrange("(a p) d -> p a d", p=P)
    out_v = out[0].rearrange("(a p) d -> p a d", p=P)

    def rows(w, k0, nk, c0, ncol):
        return w[k0 * P:(k0 + nk) * P, c0:c0 + ncol].rearrange("(k p) n -> p k n", p=P)

    def spread(v, n):
        return v.rearrange("(o n) -> o n", o=1).broadcast_to([P, n])

    def front_source(p):
        if p < U0:
            return rows(ev_w_in[0], 4 * (p - V0), 4, 3 * CONV + GM, GM), 4
        if p < WOUT0:
            first = {U0: 3 * CONV, C0: CONV, X0: 2 * CONV, B0: 0}[p - p % 2]
            return rows(ev_w_in[0], 0, KT, first + 256 * (p % 2), 256), KT
        if p < FFN0:
            return rows(ev_w_out[0], OUT_KT[2 * (p - WOUT0)], 2, 0, D), 2
        if p < QKV0:
            for u in range(FU):
                g, up, d = ffn_pieces(u)
                if p == g:
                    return rows(ev_ffn_wg[0], 0, KT, 256 * u, 256), KT
                if p == up:
                    return rows(ev_ffn_wu[0], 0, KT, 256 * u, 256), KT
                if p == d:
                    return rows(ev_ffn_wd[0], 2 * u, 2, 0, D), 2
        if p == QKV0:
            return rows(od_w_qkv[0], 0, KT, NQ * HD, 2 * NKV * HD), KT
        if p < WO0:
            c, k = divmod(p - QKV0 - 1, 2)
            return rows(od_w_qkv[0], 4 * k, 4, N * c, N), 4
        return rows(od_w_o[0], 2 * (p - WO0), 2, 0, D), 2

    def hi(p, nk):
        return w_hi[:, p % SPLITS, :].rearrange("p (k n) -> p k n", k=nk)

    def lo(p, nk):
        return w_lo[:, p % SPLITS, :].rearrange("p (k n) -> p k n", k=nk)

    ACC = (2, 3, 6, 7)
    NORM_BANKS = (0, 1, 4, 5)
    O_BANKS = (0, 1, 2, 7)
    S_BANKS = (6, 3, 5)
    PT_BANK = 4
    Q_BANKS = (0, 1, 2, 7)
    OT_BANKS = (0, 1, 3, 6)
    WO_ACC = (4, 5, 2, 7)
    block = ctx.enter_context(nc.Block())

    norm_gains = (ev_norm1_g[0], ev_norm2_g[0], od_norm1_g[0], od_norm2_g[0], final_norm_g)

    def load_gain(eng, n):
        if n >= 2:
            eng.wait_ge(xn_ready, 2 * TT * (n - 1))
        eng.dma_start(gain[n % 2][:], spread(norm_gains[n], D)).then_inc(ld_gain[n % 2], 16)

    @block.sync
    def _(sp):
        sp.dma_start(h[:, 0, :], x_v[:, 0, :]).then_inc(ld_x[0], 16)
        load_gain(sp, 0)
        for p in range(FRONT):
            if p == V0 + 1:
                sp.dma_start(h[:, 1, :], x_v[:, 1, :]).then_inc(ld_x[1], 16)
            if p == U0:
                sp.dma_start(sp_w[:], ev_spatial_w[0].rearrange("h i j -> i h j")).then_inc(ld_spw, 16)
            if p == C0:
                sp.dma_start(ln_g[:], spread(ev_ln_g[0], GM)).then_inc(ld_even, 16)
                sp.dma_start(ln_b[:], spread(ev_ln_b[0], GM)).then_inc(ld_even, 16)
                sp.dma_start(sp_b[:], spread(ev_spatial_b[0].rearrange("h i -> (h i)"), GH * P).rearrange(
                    "p (h i) -> p h i", h=GH)).then_inc(ld_even, 16)
                sp.dma_start(conv_w[:], ev_conv_w[0].rearrange("(c p) k -> p c k", p=P)).then_inc(ld_even, 16)
            if p == WOUT0:
                load_gain(sp, 1)
                sp.dma_start(router[:], od_router_w[0].rearrange("(k p) e -> p k e", p=P)).then_inc(ld_router, 16)
            if p >= RING_A:
                sp.wait_ge(lo_ready, p - RING_A + 1)
            src, nk = front_source(p)
            sp.dma_start(ring_a[p % RING_A][:].rearrange("p (k n) -> p k n", k=nk), src).then_inc(
                landed[p % RING_A], 16)

        def expert_load(wait, e, q):
            for j in range(EU):
                g, up, d = expert_pieces(j)
                for w, first in ((od_exp_wg, g), (od_exp_wu, up)):
                    if first <= q < first + 2:
                        src = w[0][bass.ds(e, 1), (q - first) * 4 * P:(q - first + 1) * 4 * P, N * j:N * j + N]
                        src, nk = src.rearrange("o (k p) n -> p (o k) n", p=P), 4
                if d <= q < d + 2:
                    r0 = N * j + 2 * P * (q - d)
                    src = od_exp_wd[0][bass.ds(e, 1), r0:r0 + 2 * P, :]
                    src, nk = src.rearrange("o (k p) n -> p (o k) n", p=P), 2
            if wait is not None:
                sp.wait_ge(lo_ready, wait)
            sp.dma_start(ring[q % RING][:].rearrange("p (k n) -> p k n", k=nk), src).then_inc(landed[q % RING], 16)

        for q in range(RING):
            if q == RING_A:
                sp.wait_ge(o_ready, 4)
            if q == RING - 2:
                sp.wait_ge(piece_used, FRONT)
            expert_load(FRONT + q - RING_A + 1 if q < RING_A else None, 0, q)
        for q in range(RING, EP):
            expert_load(FRONT + q - RING + 1, 0, q)
        with sp.Fori(1, NE) as e:
            for q in range(EP):
                expert_load(e * EP + (FRONT + q - RING + 1), e, q)
        sp.wait_ge(routed, 1)
        most = nc.sync.value_load(count_max[0:1, 0:1], min_val=0, max_val=T)
        with sp.If(most > P):
            with sp.Fori(0, NE) as e:
                for q in range(EP):
                    expert_load(e * EP + (NE * EP + FRONT + q - RING + 1), e, q)
        for a in range(TT):
            for half in range(2):
                sp.wait_ge(h_final, 2 * a + half + 1)
                c = slice(N * half, N * half + N)
                sp.dma_start(out_v[:, a, c], xn[:, a, c]).then_inc(stored, 16)
        sp.wait_ge(stored, 16 * 2 * TT)

    @block.gpsimd
    def _(pool):
        nc.gpsimd.memset(ident[:], 0.0).then_inc(pool_step, 1)
        nc.gpsimd.memset(ones[:], 1.0).then_inc(pool_step, 1)
        pool.wait_ge(pool_step, 2)
        nc.gpsimd.affine_select(out=ident[:], in_=ident[:], compare_op=ALU.not_equal, fill=1.0, base=0,
                                pattern=[[-1, P]], channel_multiplier=1).then_inc(pool_const, 1)
        nc.gpsimd.affine_select(out=tri[:], in_=ones[:], compare_op=ALU.is_ge, fill=0.0, base=0,
                                pattern=[[1, P]], channel_multiplier=-1).then_inc(pool_const, 1)
        nc.gpsimd.iota(iota_s[:], pattern=[[1, P]], base=1, channel_multiplier=0,
                       allow_small_or_imprecise_dtypes=True).then_inc(pool_const, 1)
        pool.wait_ge(ld_spw, 16)
        nc.gpsimd.affine_select(out=sp_w[:], in_=sp_w[:], compare_op=ALU.is_ge, fill=0.0, base=0,
                                pattern=[[0, GH], [-1, P]], channel_multiplier=1).then_inc(pool_spw, 1)
        pool.wait_ge(h_added, 4)
        nc.gpsimd.memset(mask0[:], 0.0).then_inc(pool_step, 1)
        nc.gpsimd.memset(mask1[:], 0.0).then_inc(pool_step, 1)
        nc.gpsimd.memset(ident_b[:], 0.0).then_inc(pool_step, 1)
        nc.gpsimd.memset(k_pad[:], 0.0).then_inc(pool_step, 1)
        for k in range(RH):
            nc.gpsimd.memset(inv_freq[:, k:k + 1], float(np.float32(THETA ** (-2.0 * k / ROPE)))).then_inc(pool_step, 1)
        pool.wait_ge(pool_step, 6 + RH)
        nc.gpsimd.affine_select(out=ident_b[:], in_=ident_b[:], compare_op=ALU.not_equal, fill=1.0, base=0,
                                pattern=[[-1, P]], channel_multiplier=1).then_inc(pool_const, 1)
        nc.gpsimd.affine_select(out=mask0[:], in_=mask0[:], compare_op=ALU.is_ge, fill=MASKED, base=0,
                                pattern=[[0, 4], [-1, P]], channel_multiplier=1).then_inc(pool_const, 1)
        nc.gpsimd.affine_select(out=mask1[:, :, 0:P], in_=mask1[:, :, 0:P], compare_op=ALU.is_gt, fill=MASKED,
                                base=0, pattern=[[0, 2], [1, P]], channel_multiplier=-1).then_inc(pool_const, 1)
        nc.gpsimd.affine_select(out=mask1[:, :, P:T], in_=mask1[:, :, P:T], compare_op=ALU.is_ge, fill=MASKED,
                                base=0, pattern=[[0, 2], [-1, P]], channel_multiplier=1).then_inc(pool_const, 1)

    @block.scalar
    def _(act):
        act.wait_ge(pool_step, 2)
        nc.scalar.activation(table_warm[:], ones[:, 0:1], ACT.Square)

        at = [0]

        def split_hi(upto):
            for p in range(at[0], upto + 1):
                act.wait_ge(landed[p % RING_A], 16 * (p // RING_A + 1))
                if p >= SPLITS:
                    act.wait_ge(piece_used, p - SPLITS + 1)
                nc.scalar.copy(w_hi[:, p % SPLITS, :], ring_a[p % RING_A][:]).then_inc(hi_ready, 1)
            at[0] = max(at[0], upto + 1)

        def norm_square(n, a):
            if n:
                act.wait_ge(h_added, 4 * (n - 1) + 2 * a + 2)
            else:
                act.wait_ge(ld_x[a], 16)
            nc.scalar.activation(xn[:, a, :], h[:, a, :], ACT.Square, accum_out=ssq[:, a:a + 1]).then_inc(sq_ready, 1)

        def turned_hi(first, a, banks):
            for i in range(2):
                act.wait_ge(norm_t, first + 2 * a + i + 1)
                nc.scalar.copy(xT_hi[:, 4 * i:4 * i + 4, P * a:P * a + P],
                               bank[banks[2 * a + i]][:].rearrange("p (k t) -> p k t", k=4)).then_inc(xT_hi_ready, 1)

        def norm(n, p0):
            norm_square(n, 0)
            if n:
                split_hi(p0)
            turned_hi(4 * n, 0, NORM_BANKS)
            split_hi(p0 + 1)
            norm_square(n, 1)
            turned_hi(4 * n, 1, NORM_BANKS)
            split_hi(p0 + 2)

        norm_square(0, 0)
        turned_hi(0, 0, NORM_BANKS)
        split_hi(V0)
        norm_square(0, 1)
        split_hi(V0 + 1)
        turned_hi(0, 1, NORM_BANKS)
        split_hi(V0 + 1 + 2)
        for a in range(TT):
            act.wait_ge(piece_used, V0 + 2)
            nc.scalar.activation(v_act[:, a, :], bank[6 + a][:], ACT.Gelu).then_inc(v_gelu, 1)
        for c in range(2):
            split_hi(U0 + c + 2)
            act.wait_ge(piece_used, U0 + c + 1)
            nc.scalar.activation(uT[:, 2 * c:2 * c + 2, :], bank[c][:].rearrange("p (c t) -> p c t", c=2),
                                 ACT.Gelu).then_inc(uT_ready, 1)
        for c in range(2):
            split_hi(C0 + c + 2)
            act.wait_ge(piece_used, C0 + c + 1)
            nc.scalar.copy(acT[:, 2 * c:2 * c + 2, :], bank[2 + c][:].rearrange("p (c t) -> p c t", c=2)).then_inc(
                acT_ready, 1)
        split_hi(B0 + 1)
        for i in range(4):
            split_hi((B0 + 1, B0 + 1, WOUT0 + 1, WOUT0 + 2)[i])
            k = (4, 6, 0, 2)[i]
            act.wait_ge(y_ready, i + 1)
            nc.scalar.copy(yT_hi[:, k:k + 2, :], yT[:, k % 4:k % 4 + 2, :]).then_inc(yT_hi_ready, 1)
        split_hi(WOUT0 + 3)

        norm(1, FFN0)
        load_gain(act, 2)
        act.dma_start(b_qkv[:], spread(od_b_qkv[0], QKV)).then_inc(ld_odd, 16)
        act.dma_start(b_o[:], spread(od_b_o[0], D)).then_inc(ld_odd, 16)
        act.dma_start(sinks[:], spread(od_sinks[0], NQ)).then_inc(ld_odd, 16)
        for a in range(TT):
            act.dma_start(pos_i[:, a:a + 1], positions[0, P * a:P * a + P].unsqueeze(1)).then_inc(ld_odd, 16)
        for u in range(FU):
            g, up, d = ffn_pieces(u)
            split_hi(up + 2)
            act.wait_ge(piece_used, g + 1)
            b = bank[(0, 4)[u % 2]]
            nc.scalar.activation(f_s[:], b[:].rearrange("p (c t) -> p c t", c=2), ACT.Silu).then_inc(silu_ready, 1)
            act.wait_ge(act_ready, u + 1)
            if u >= 2:
                act.wait_ge(piece_used, ffn_pieces(u - 2)[2] + 1)
            nc.scalar.copy(fT_hi[:, u % 2], f_a[:]).then_inc(fT_hi_ready, 1)
        split_hi(QKV0 - 1)

        def expert_hi(b, q):
            act.wait_ge(landed[q % RING], b * (16 * (EP // RING)) + 16 * (q // RING + 1 + (FRONT // RING_A if q % RING < RING_A else 0)))
            act.wait_ge(piece_used, b * EP + (FRONT + q - SPLITS + 1))
            nc.scalar.copy(w_hi[:, (FRONT + q) % SPLITS, :], ring[q % RING][:]).then_inc(hi_ready, 1)

        def expert_his(b, q0, q1):
            for q in range(q0, q1):
                expert_hi(b, q)

        norm(2, QKV0)
        load_gain(act, 3)
        act.wait_ge(red_ready, 1)
        nc.scalar.activation(sin_t[:], red[:], ACT.Sin).then_inc(trig_ready, 1)
        nc.scalar.activation(cos_t[:], red_c[:], ACT.Sin).then_inc(trig_ready, 1)
        split_hi(WO0 + 1)

        def turned_queries(a):
            for i in range(2):
                act.wait_ge(qk_t, 3 * a + 2 + i)
                nc.scalar.copy(qT[:, 4 * i:4 * i + 4, P * a:P * a + P],
                               bank[Q_BANKS[2 * a + i]][:].rearrange("p (c t) -> p c t", c=4)).then_inc(qkT_act, 1)

        turned_queries(0)
        split_hi(WO0 + 2)
        for i in range(12):
            a, n, first = (0, 4, 4 * i) if i < 4 else (1, 2, 2 * (i - 4))
            if i == 2:
                turned_queries(1)
            act.wait_ge(max_ready, i + 1)
            if i >= 2:
                act.wait_ge(probs_t, i - 1)
            w = N // n
            for j in range(n):
                hq = first + j
                ins = nc.scalar.activation(probs[:, i % 2, w * j:w * j + w], bank[S_BANKS[i % 3]][:, w * j:w * j + w],
                                           ACT.Exp, bias=neg_max[:, a, hq:hq + 1], scale=SCALE,
                                           accum_out=den[:, a, hq:hq + 1])
            ins.then_inc(probs_ready, 1)
            if i in (3, 11):
                act.wait_ge(sink_arg, a + 1)
                nc.scalar.activation(sink_e[:, a, :], sink_e[:, a, :], ACT.Exp).then_inc(sink_ready, 1)
            if i == 10:
                turned_hi(12, 0, OT_BANKS)
        turned_hi(12, 1, OT_BANKS)
        split_hi(WO0 + 3)
        expert_his(0, 0, 1)

        for a in range(TT):
            norm_square(3, a)
            if a == 0:
                expert_his(0, 1, 2)
            for i in range(2):
                if (a, i) == (1, 0):
                    expert_his(0, 2, AHEAD)
                act.wait_ge(norm_t, 16 + 2 * a + i + 1)
                nc.scalar.copy(xT[:, 4 * i:4 * i + 4, P * a:P * a + P],
                               bank[OT_BANKS[2 * a + i]][:].rearrange("p (k t) -> p k t", k=4)).then_inc(xTr_ready, 1)
        load_gain(act, 4)
        act.wait_ge(diff_ready, 1)
        nc.scalar.activation(p2[:], diff[:], ACT.Exp).then_inc(p2_ready, 1)
        nc.scalar.activation(table_warm[:], ones[:, 0:1], ACT.Silu)

        def gathered_hi(count):
            for i in range(2):
                act.wait_ge(gathered, count + (i + 1))
                nc.scalar.copy(gT_hi[:, 4 * i:4 * i + 4, :], bank[2 + i][:].rearrange("p (k s) -> p k s", k=4)).then_inc(
                    gT_hi_ready, 1)

        def hidden_hi(count):
            act.wait_ge(e_t, count)
            nc.scalar.copy(eT_hi[:], bank[6][:].rearrange("p (k s) -> p k s", k=4)).then_inc(eT_hi_ready, 1)

        def expert_block(b, last):
            at = AHEAD
            for j in range(EU):
                g, up, d = expert_pieces(j)
                if j:
                    expert_his(b, at, g + 4)
                    at = g + 4
                    hidden_hi(b * EU + j)
                expert_his(b, at, min(up + 4, EP))
                at = min(up + 4, EP)
                act.wait_ge(piece_used, b * EP + (FRONT + g + 2))
                nc.scalar.activation(e_a[:], bank[2 * (j % 2)][:], ACT.Silu).then_inc(e_silu, 1)
            expert_his(b, at, EP)
            hidden_hi(b * EU + EU)
            if not last:
                gathered_hi(b * 2 + 2)
                expert_his(b + 1, 0, AHEAD)
            act.wait_ge(piece_used, b * EP + (FRONT + EP))
            act.wait_ge(pickT_ready, b + 1)
            for half in range(2):
                nc.scalar.activation(ey_hi[:, N * half:N * half + N], bank[4 + half][:], ACT.Copy,
                                     scale=gate_slot[:, 0:1]).then_inc(ey_hi_ready, 1)

        def final_squares(n):
            for i in range(4):
                act.wait_ge(e_added, 4 * n + i + 2)
                if i:
                    act.wait_ge(sq_ready, 4 * TT + 4 * (n > NE) + i)
                nc.scalar.activation(e_a[:], h[:, i // 2, N * (i % 2):N * (i % 2) + N], ACT.Square,
                                     accum_out=ssq_half[:, i // 2, i % 2:i % 2 + 1]).then_inc(sq_ready, 1)

        def no_outputs():
            nc.scalar.activation(ey_hi[:].rearrange("p (k n) -> p k n", n=P), ones[:].unsqueeze(1).broadcast_to([P, D // P, P]),
                                 ACT.Copy, scale=0.0).then_inc(ey_hi_ready, 2)

        act.wait_ge(routed, 1)
        gathered_hi(0)
        no_outputs()
        with act.Fori(0, NE - 1) as b:
            expert_block(b, False)
        most = nc.scalar.value_load(count_max[0:1, 0:1], min_val=0, max_val=T)
        expert_block(NE - 1, True)
        final_squares(NE)
        with act.If(most > P):
            act.wait_ge(scattered, 4 * NE + 4)
            no_outputs()
            gathered_hi(2 * NE)
            expert_his(NE, 0, AHEAD)
            with act.Fori(NE, BLOCKS - 1) as b:
                expert_block(b, False)
            expert_block(BLOCKS - 1, True)
            final_squares(BLOCKS + 1)

    @block.vector
    def _(dve):
        steps = [0]

        def then(ins):
            steps[0] += 1
            ins.then_inc(dve_step, 1)
            dve.wait_ge(dve_step, steps[0])

        at = [0]

        def split_lo(upto):
            for p in range(at[0], upto + 1):
                dve.wait_ge(hi_ready, p + 1)
                nc.vector.tensor_tensor(w_lo[:, p % SPLITS, :], ring_a[p % RING_A][:],
                                        w_hi[:, p % SPLITS, :].bitcast(F32), ALU.subtract).then_inc(lo_ready, 1)
            at[0] = max(at[0], upto + 1)

        def rsqrt(tiles):
            k2 = 0.5 ** (1 / 3)
            k1 = (k2 / 2) ** (1 / 3)
            k0 = (k1 / 2) ** (1 / 3)
            magic = float(0x5F3759DF - 2 ** 30 + round(np.log2(k0) * 2 ** 23))
            y, nv, t = ([x[:, a:a + 1] for a in range(TT)] for x in (rstd, neg_var, newton))

            def step(op):
                for a in tiles[:-1]:
                    op(a)
                then(op(tiles[-1]))

            step(lambda a: nc.vector.tensor_scalar(y[a].bitcast(I32), nv[a].bitcast(I32), -0.5, magic, ALU.mult, ALU.add))
            for k in (k0, k1, k2):
                step(lambda a: nc.vector.scalar_tensor_tensor(out=t[a], in0=y[a], scalar=nv[a], in1=y[a],
                                                              op0=ALU.mult, op1=ALU.mult))
                step(lambda a: nc.vector.scalar_tensor_tensor(out=y[a], in0=t[a], scalar=3 * k * k, in1=y[a],
                                                              op0=ALU.add, op1=ALU.mult))

        def norm_scale(n, a):
            dve.wait_ge(sq_ready, TT * n + a + 1)
            then(nc.vector.tensor_scalar(neg_var[:, a:a + 1], ssq[:, a:a + 1], -1.0 / D, -EPS, ALU.mult, ALU.add))
            rsqrt((a,))
            dve.wait_ge(ld_gain[n % 2], 16 * (n // 2 + 1))
            for half in range(2):
                c = slice(N * half, N * half + N)
                nc.vector.scalar_tensor_tensor(out=xn[:, a, c], in0=h[:, a, c], scalar=rstd[:, a:a + 1],
                                               in1=gain[n % 2][:, c], op0=ALU.mult, op1=ALU.mult).then_inc(xn_ready, 1)

        def turned_lo(first, a, banks):
            for i in range(2):
                dve.wait_ge(xT_hi_ready, first + 2 * a + i + 1)
                c = slice(P * a, P * a + P)
                nc.vector.tensor_tensor(xT_lo[:, 4 * i:4 * i + 4, c], bank[banks[2 * a + i]][:].rearrange("p (k t) -> p k t", k=4),
                                        xT_hi[:, 4 * i:4 * i + 4, c].bitcast(F32), ALU.subtract).then_inc(xT_lo_ready, 1)

        def norm(n, last, p0):
            add_to_h(n - 1, last, ACC, 0)
            norm_scale(n, 0)
            split_lo(p0)
            turned_lo(4 * n, 0, NORM_BANKS)
            add_to_h(n - 1, last, ACC, 1)
            split_lo(p0 + 1)
            norm_scale(n, 1)
            turned_lo(4 * n, 1, NORM_BANKS)
            split_lo(p0 + 2)

        def add_to_h(n, last, banks, a):
            for half in range(2):
                if (a, half) == (1, 1):
                    dve.wait_ge(piece_used, last + 1)
                else:
                    dve.wait_ge(acc_done, 3 * n + 2 * a + half + 1)
                hs = h[:, a, N * half:N * half + N]
                nc.vector.tensor_tensor(hs, hs, bank[banks[2 * a + half]][:], ALU.add).then_inc(h_added, 1)

        def reduce_angles():
            two_pi = 2.0 * np.pi
            c1 = 6.28125
            c2 = float(np.round((two_pi - c1) * 2.0 ** 20) / 2.0 ** 20)
            c3 = float(np.float32(two_pi - c1 - c2))
            magic = 1.5 * 2.0 ** 23
            dve.wait_ge(ld_odd, 80)
            dve.wait_ge(pool_const, 7)
            then(nc.vector.tensor_copy(pos_f[:], pos_i[:]))
            for a in range(TT):
                then(nc.vector.tensor_scalar(ang[:, a, :], inv_freq[:], pos_f[:, a:a + 1], None, ALU.mult))
            then(nc.vector.tensor_scalar(turns[:], ang[:], float(np.float32(1.0 / two_pi)), magic, ALU.mult, ALU.add))
            then(nc.vector.tensor_scalar(turns[:], turns[:], magic, None, ALU.subtract))
            for i, c in enumerate((c1, c2, c3)):
                then(nc.vector.scalar_tensor_tensor(out=red[:], in0=turns[:], scalar=-c, in1=(ang if i == 0 else red)[:],
                                                    op0=ALU.mult, op1=ALU.add))
            then(nc.vector.tensor_scalar(red[:], red[:], 3.1415925, -3.1415925, ALU.min, ALU.max))
            then(nc.vector.scalar_tensor_tensor(out=red_c[:], in0=red[:], scalar=-1.0, in1=red[:], op0=ALU.mult, op1=ALU.max))
            nc.vector.tensor_scalar(red_c[:], red_c[:], -1.0, float(np.float32(np.pi / 2)), ALU.mult, ALU.add).then_inc(red_ready, 1)
            then(nc.vector.tensor_scalar(neg_sinks[:], sinks[:], -1.0, None, ALU.mult))

        nc.vector.memset(hc[:, :, 0:CW - 1], 0.0).then_inc(dve_const, 1)
        norm_scale(0, 0)
        turned_lo(0, 0, NORM_BANKS)
        split_lo(V0)
        norm_scale(0, 1)
        split_lo(V0 + 1)
        turned_lo(0, 1, NORM_BANKS)
        split_lo(U0)
        dve.wait_ge(spw_t, 1)
        nc.vector.tensor_copy(sp_wT[:], bank[4][:].rearrange("p (h i) -> p h i", h=GH)).then_inc(spw_ready, 1)
        split_lo(V0 + 1 + 2)
        for a in range(TT):
            dve.wait_ge(v_gelu, a + 1)
            then(nc.vector.bn_stats(bn[:, a, :], v_act[:, a, :]))
            then(nc.vector.bn_aggr(mv[:, a, :], bn[:, a, :]))
        then(nc.vector.tensor_scalar(neg_var[:], mv[:, :, 1], -1.0, -EPS, ALU.mult, ALU.add))
        rsqrt((0, 1))
        split_lo(U0 + 2)
        dve.wait_ge(ld_even, 16 * 4)
        for a in range(TT):
            then(nc.vector.tensor_scalar(v_act[:, a, :], v_act[:, a, :], mv[:, a, 0:1], rstd[:, a:a + 1], ALU.subtract, ALU.mult))
            then(nc.vector.tensor_tensor(v_act[:, a, :], v_act[:, a, :], ln_g[:], ALU.mult))
            nc.vector.tensor_tensor(v_act[:, a, :], v_act[:, a, :], ln_b[:], ALU.add).then_inc(vn_ready, 1)
            split_lo(U0 + 3 + a)
        dve.wait_ge(dve_const, 1)

        def convolve(c):
            dve.wait_ge(acT_ready, c + 1)
            dve.wait_ge(piece_used, X0 + c + 1)
            then(nc.vector.tensor_tensor(hc[:, 2 * c:2 * c + 2, CW - 1:], acT[:, 2 * c:2 * c + 2, :],
                                         bank[6 + c][:].rearrange("p (c t) -> p c t", c=2), ALU.mult))
            for i in (2 * c, 2 * c + 1):
                then(nc.vector.tensor_scalar(cv[:, i, :], hc[:, i, 0:T], conv_w[:, i, 0:1], None, ALU.mult))
                for k in range(1, CW):
                    then(nc.vector.scalar_tensor_tensor(out=cv[:, i, :], in0=hc[:, i, k:k + T], scalar=conv_w[:, i, k:k + 1],
                                                        in1=cv[:, i, :], op0=ALU.mult, op1=ALU.add))

        def low_of_y(i, k):
            dve.wait_ge(yT_hi_ready, i + 1)
            nc.vector.tensor_tensor(yT_lo[:, k:k + 2, :], yT[:, k % 4:k % 4 + 2, :], yT_hi[:, k:k + 2, :].bitcast(F32),
                                    ALU.subtract).then_inc(yT_lo_ready, 1)

        split_lo(X0 + 2)
        convolve(0)
        split_lo(B0 + 1)
        for g in range(2):
            dve.wait_ge(mix_done, 1 + g)
            b = sp_b[:, 2 * g:2 * g + 2, :].unsqueeze(2).broadcast_to([P, 2, TT, P])
            ys = yT[:, 2 * g:2 * g + 2, :]
            then(nc.vector.tensor_tensor(ys.rearrange("p g (a i) -> p g a i", a=TT),
                                         bank[4 + g][:].rearrange("p (g a i) -> p g a i", g=2, a=TT), b, ALU.add))
            nc.vector.tensor_tensor(ys, ys, uT[:, 2 * g:2 * g + 2, :], ALU.mult).then_inc(y_ready, 1)
            low_of_y(g, CT + 2 * g)
        convolve(1)
        dve.wait_ge(yT_lo_ready, 2)
        for c in range(2):
            split_lo(WOUT0 + 1)
            dve.wait_ge(piece_used, B0 + c + 1)
            nc.vector.tensor_tensor(yT[:, 2 * c:2 * c + 2, :], cv[:, 2 * c:2 * c + 2, :],
                                    bank[c][:].rearrange("p (c t) -> p c t", c=2), ALU.mult).then_inc(y_ready, 1)
            low_of_y(2 + c, 2 * c)
        split_lo(WOUT0 + 3)

        norm(1, FFN0 - 1, FFN0)
        for u in range(FU):
            g, up, d = ffn_pieces(u)
            split_lo(up + 2)
            dve.wait_ge(silu_ready, u + 1)
            dve.wait_ge(piece_used, up + 1)
            b = bank[(1, 5)[u % 2]]
            if u:
                dve.wait_ge(fT_lo_ready, u)
            nc.vector.tensor_tensor(f_a[:], f_s[:], b[:].rearrange("p (c t) -> p c t", c=2), ALU.mult).then_inc(act_ready, 1)
            dve.wait_ge(fT_hi_ready, u + 1)
            nc.vector.tensor_tensor(fT_lo[:, u % 2], f_a[:], fT_hi[:, u % 2].bitcast(F32), ALU.subtract).then_inc(fT_lo_ready, 1)
            if u == 3:
                reduce_angles()
        split_lo(QKV0 - 1)

        def expert_lo(b, q):
            dve.wait_ge(hi_ready, b * EP + (FRONT + q + 1))
            nc.vector.tensor_tensor(w_lo[:, (FRONT + q) % SPLITS, :], ring[q % RING][:],
                                    w_hi[:, (FRONT + q) % SPLITS, :].bitcast(F32), ALU.subtract).then_inc(lo_ready, 1)

        def expert_los(b, q0, q1):
            for q in range(q0, q1):
                expert_lo(b, q)

        norm(2, QKV0 - 1, QKV0)

        def add_bias(i, c, a):
            c0, w, b0 = ((NQ * HD, 2 * NKV * HD, 0), (0, N, 2), (N, N, 6))[c]
            if a == 0:
                dve.wait_ge(qkv_done, c + 1)
            else:
                dve.wait_ge(piece_used, (QKV0 + 1, QKV0 + 3, QKV0 + 5)[c])
            nc.vector.tensor_tensor(qkv[:, a, c0:c0 + w], bank[b0 + a][:, 0:w], b_qkv[:, c0:c0 + w],
                                    ALU.add).then_inc(qkv_ready, 1)

        def rotate(a):
            heads = NQ + NKV
            dve.wait_ge(qkv_ready, 5 + a)
            qk = qkv[:, a, 0:heads * HD].rearrange("p (h d) -> p h d", d=HD)
            t1, t2 = qk[:, :, 0:RH], qk[:, :, RH:ROPE]
            r = [rope_t[:, i, a, :].rearrange("p (h d) -> p h d", d=RH) for i in range(4)]
            cs = cos_t[:, a:a + 1, :].broadcast_to([P, heads, RH])
            sn = sin_t[:, a:a + 1, :].broadcast_to([P, heads, RH])
            nc.vector.tensor_tensor(r[0], t1, cs, ALU.mult)
            nc.vector.tensor_tensor(r[1], t2, sn, ALU.mult)
            nc.vector.tensor_tensor(r[2], t2, cs, ALU.mult)
            then(nc.vector.tensor_tensor(r[3], t1, sn, ALU.mult))
            nc.vector.tensor_tensor(t1, r[0], r[1], ALU.subtract)
            then(nc.vector.tensor_tensor(t2, r[2], r[3], ALU.add))
            kk = qkv[:, a, NQ * HD:heads * HD].rearrange("p (g d) -> p g d", d=HD)
            for i in range(2):
                nc.vector.tensor_copy(k_pad[:, a, :, i, HD * i:HD * i + HD], kk).then_inc(rope_ready, 1)

        def turned_keys(a):
            dve.wait_ge(qk_t, 3 * a + 1)
            nc.vector.tensor_copy(kT[:].rearrange("p g i t -> p (g i) t")[:, :, P * a:P * a + P],
                                  bank[4 + a][:].rearrange("p (g t) -> p g t", g=4)).then_inc(qkT_dve, 1)

        for a in range(TT):
            nc.vector.tensor_tensor(h[:, a, :], h[:, a, :], b_o[:], ALU.add).then_inc(dve_const, 1)
        add_bias(0, 0, 0)
        split_lo(QKV0 + 3)
        add_bias(1, 0, 1)
        add_bias(2, 1, 0)
        add_bias(3, 1, 1)
        split_lo(QKV0 + 4)
        dve.wait_ge(trig_ready, 2)
        add_bias(4, 2, 0)
        rotate(0)
        split_lo(WO0)
        add_bias(5, 2, 1)
        turned_keys(0)
        rotate(1)

        def row_max(i):
            a, n, first = (0, 4, 4 * i) if i < 4 else (1, 2, 2 * (i - 4))
            dve.wait_ge(s_done, i + 1)
            then(nc.vector.tensor_reduce(raw_max[:, a, first:first + n],
                                         bank[S_BANKS[i % 3]][:].rearrange("p (h k) -> p h k", h=n), AX_X, ALU.max))
            nc.vector.scalar_tensor_tensor(out=neg_max[:, a, first:first + n], in0=raw_max[:, a, first:first + n],
                                           scalar=-SCALE, in1=neg_sinks[:, first:first + n], op0=ALU.mult,
                                           op1=ALU.min).then_inc(max_ready, 1)
            if i in (3, 11):
                dve.wait_ge(max_ready, i + 1)
                nc.vector.tensor_tensor(sink_e[:, a, :], neg_max[:, a, :], sinks[:], ALU.add).then_inc(sink_arg, 1)

        def evacuate_probs(i):
            dve.wait_ge(probs_t, i + 1)
            if i >= 2:
                dve.wait_ge(pv_done, i - 1)
            nc.vector.tensor_copy(probsT[:, i % 2, :], bank[PT_BANK][:]).then_inc(probsT_ready, 1)

        def normalise(a):
            dve.wait_ge(sink_ready, a + 1)
            then(nc.vector.tensor_tensor(den[:, a, :], den[:, a, :], sink_e[:, a, :], ALU.add))
            then(nc.vector.reciprocal(den[:, a, :], den[:, a, :]))
            for g in range(2):
                dve.wait_ge(pv_done, (2, 4, 8, 12)[2 * a + g])
                nc.vector.tensor_tensor(
                    o_tok[:, a, N * g:N * g + N].rearrange("p (h d) -> p h d", d=HD),
                    bank[O_BANKS[2 * a + g]][:].rearrange("p (h d) -> p h d", d=HD),
                    den[:, a, QPK * g:QPK * g + QPK].unsqueeze(2).broadcast_to([P, QPK, HD]), ALU.mult).then_inc(o_ready, 1)

        for i in range(12):
            row_max(i)
            if i == 1:
                turned_keys(1)
            if i >= 2:
                evacuate_probs(i - 2)
            if i in (3, 9):
                split_lo(WO0 + (1 if i == 3 else 2))
            if i == 7:
                normalise(0)
            if i == 11:
                turned_lo(12, 0, OT_BANKS)
        evacuate_probs(10)
        evacuate_probs(11)
        normalise(1)
        turned_lo(12, 1, OT_BANKS)
        split_lo(WO0 + 3)
        expert_los(0, 0, 1)
        dve.wait_ge(dve_const, 1 + TT)

        for a in range(TT):
            add_to_h(2, FRONT - 1, WO_ACC, a)
            norm_scale(3, a)
        expert_los(0, 1, 2)
        for a in range(TT):
            dve.wait_ge(logits_done, a + 1)
            then(nc.vector.tensor_copy(logits[:, a, :], bank[OT_BANKS[2 * a]][:, 0:NE]))
            then(nc.vector.max(top_v[:, a, :], logits[:, a, :]))
            then(nc.vector.max_index(top_i[:, a, :], top_v[:, a, :], logits[:, a, :]))
            then(nc.vector.tensor_scalar(top_f[:, a, :], top_i[:, a, 0:2], 1.0, None, ALU.add))
            for i in range(2):
                then(nc.vector.tensor_scalar(oh[:, a, i, :], iota_s[:, 0:NE], top_f[:, a, i:i + 1], None, ALU.is_equal))
            nc.vector.tensor_tensor(sel[:, a, :], oh[:, a, 0, :], oh[:, a, 1, :], ALU.add).then_inc(sel_ready, 1)
            if a == 0:
                expert_los(0, 2, AHEAD)
        nc.vector.tensor_tensor(diff[:], top_v[:, :, 1], top_v[:, :, 0], ALU.subtract).then_inc(diff_ready, 1)
        dve.wait_ge(p2_ready, 1)
        then(nc.vector.tensor_scalar(psum_g[:], p2[:], 1.0, None, ALU.add))
        then(nc.vector.reciprocal(g1[:], psum_g[:]))
        then(nc.vector.tensor_tensor(g2[:], p2[:], g1[:], ALU.mult))
        dve.wait_ge(rank_done, 1)
        then(nc.vector.tensor_tensor(slot_of[:, :, 0:NE], sel[:], bank[4][:, 0:TT * NE].rearrange("p (a e) -> p a e", a=TT),
                                     ALU.mult))
        for a in range(TT):
            nc.vector.tensor_scalar(pick[:, a, :], iota_s[:], slot_of[:, a, 0:1], None, ALU.is_equal).then_inc(pick_ready, 1)
        for a in range(TT):
            then(nc.vector.tensor_scalar(gate_of[:, a, 0:NE], oh[:, a, 0, :], g1[:, a:a + 1], None, ALU.mult))
            then(nc.vector.scalar_tensor_tensor(out=gate_of[:, a, 0:NE], in0=oh[:, a, 1, :], scalar=g2[:, a:a + 1],
                                                in1=gate_of[:, a, 0:NE], op0=ALU.mult, op1=ALU.add))
        then(nc.vector.tensor_copy(gate_of[:, :, NE:BLOCKS], gate_of[:, :, 0:NE]))
        nc.vector.tensor_copy(gate_col[:], gate_of[:, :, 0])
        then(nc.vector.tensor_scalar(slot_of[:, :, NE:BLOCKS], slot_of[:, :, 0:NE], float(P), None, ALU.subtract))
        then(nc.vector.tensor_reduce(cmax_f[:], bank[4][:, TT * NE:(TT + 1) * NE], AX_X, ALU.max))
        nc.vector.tensor_copy(count_max[:], cmax_f[:]).then_inc(routed, 1)

        def make_pick(blk):
            nc.vector.tensor_copy(gate_col[:], gate_of[:, :, bass.ds(blk, 1)].rearrange("p a o -> p (a o)"))
            for a in range(TT):
                nc.vector.tensor_scalar(pick[:, a, :], iota_s[:], slot_of[:, a, bass.ds(blk, 1)], None,
                                        ALU.is_equal).then_inc(pick_ready, 1)

        def gathered_lo(count):
            for i in range(2):
                dve.wait_ge(gT_hi_ready, count + (i + 1))
                nc.vector.tensor_tensor(gT_lo[:, 4 * i:4 * i + 4, :], bank[2 + i][:].rearrange("p (k s) -> p k s", k=4),
                                        gT_hi[:, 4 * i:4 * i + 4, :].bitcast(F32), ALU.subtract).then_inc(gT_lo_ready, 1)

        def hidden_lo(count):
            dve.wait_ge(eT_hi_ready, count)
            nc.vector.tensor_tensor(eT_lo[:], bank[6][:].rearrange("p (k s) -> p k s", k=4), eT_hi[:].bitcast(F32),
                                    ALU.subtract).then_inc(eT_lo_ready, 1)

        def add_scattered(n, i, dst_bank):
            dve.wait_ge(scattered, n * 4 + (i + 1))
            dve.wait_ge(e_added, n * 4 + (i + 1))
            hs = h[:, i // 2, N * (i % 2):N * (i % 2) + N]
            nc.vector.tensor_tensor(hs, hs, dst_bank[:], ALU.add).then_inc(e_added, 1)

        def expert_block(b, n, last):
            at = AHEAD
            for j in range(EU):
                g, up, d = expert_pieces(j)
                if j:
                    expert_los(b, at, g + 4)
                    at = g + 4
                    hidden_lo(b * EU + j)
                expert_los(b, at, min(up + 4, EP))
                at = min(up + 4, EP)
                dve.wait_ge(e_silu, b * EU + (j + 1))
                dve.wait_ge(piece_used, b * EP + (FRONT + up + 2))
                nc.vector.tensor_tensor(e_a[:], e_a[:], bank[2 * (j % 2) + 1][:], ALU.mult).then_inc(e_act, 1)
                if j < 4:
                    add_scattered(n, j, bank[7])
                if j == 4:
                    dve.wait_ge(pick_t, b + 1)
                    nc.vector.tensor_copy(gate_slot[:], bank[7][:, T:T + 1])
                    nc.vector.tensor_copy(pickT[:], bank[7][:, 0:T]).then_inc(pickT_ready, 1)
                    if not last:
                        make_pick(b + 1)
            expert_los(b, at, EP - 1)
            hidden_lo(b * EU + EU)
            expert_los(b, EP - 1, EP)
            if not last:
                gathered_lo(b * 2 + 2)
                expert_los(b + 1, 0, AHEAD)
            dve.wait_ge(pickT_ready, b + 1)
            for half in range(2):
                dve.wait_ge(ey_hi_ready, n * 2 + (3 + half))
                c = slice(N * half, N * half + N)
                nc.vector.scalar_tensor_tensor(out=ey_lo[:, c], in0=bank[4 + half][:], scalar=gate_slot[:, 0:1],
                                               in1=ey_hi[:, c].bitcast(F32), op0=ALU.mult,
                                               op1=ALU.subtract).then_inc(ey_lo_ready, 1)

        def last_scatter(n):
            for i in range(4):
                add_scattered(n, i, bank[ACC[i]])
            dve.wait_ge(e_added, 4 * n + 5)
            dve.wait_ge(sq_ready, 4 * TT + (4 if n == NE else 8))

        def nothing_scattered():
            nc.vector.tensor_scalar(pickT[:].rearrange("p (a s) -> p a s", a=TT), pick[:], 0.0, None, ALU.mult)
            nc.vector.tensor_scalar(ey_lo[:], gain[0][:], 0.0, None, ALU.mult).then_inc(ey_lo_ready, 2)

        gathered_lo(0)
        dve.wait_ge(ld_gain[0], 16 * 3)
        dve.wait_ge(pick_ready, TT)
        nothing_scattered()
        nc.vector.memset(cmax_f[:], 0.0).then_inc(e_added, 1)
        with dve.Fori(0, NE - 1) as b:
            expert_block(b, b, False)
        most = nc.vector.value_load(count_max[0:1, 0:1], min_val=0, max_val=T)
        expert_block(NE - 1, NE - 1, True)
        last_scatter(NE)
        with dve.If(most > P):
            make_pick(NE)
            dve.wait_ge(pick_ready, TT * (NE + 1))
            nothing_scattered()
            gathered_lo(2 * NE)
            expert_los(NE, 0, AHEAD)
            with dve.Fori(NE, BLOCKS - 1) as b:
                expert_block(b, b + 1, False)
            expert_block(BLOCKS - 1, BLOCKS, True)
            last_scatter(BLOCKS + 1)

        then(nc.vector.tensor_tensor(ssq[:], ssq_half[:, :, 0], ssq_half[:, :, 1], ALU.add))
        then(nc.vector.tensor_scalar(neg_var[:], ssq[:], -1.0 / D, -EPS, ALU.mult, ALU.add))
        rsqrt((0, 1))
        for a in range(TT):
            for half in range(2):
                c = slice(N * half, N * half + N)
                nc.vector.scalar_tensor_tensor(out=xn[:, a, c], in0=h[:, a, c], scalar=rstd[:, a:a + 1],
                                               in1=gain[0][:, c], op0=ALU.mult, op1=ALU.mult).then_inc(h_final, 1)

    @block.tensor
    def _(pe):
        mm = nc.tensor.matmul

        def mm3(dst, weight_moves, w, t, start, stop):
            (w_h, w_l), (t_h, t_l) = w, t
            for i, (a, b) in enumerate(((w_h, t_h), (w_h, t_l), (w_l, t_h))):
                fixed, moving = (b, a) if weight_moves else (a, b)
                ins = mm(dst, fixed, moving, start=start and i == 0, stop=stop and i == 2)
            return ins

        def turn(src, a, banks, ready):
            for k in range(KT):
                if k % 4 == 0:
                    pe.wait_ge(ready[0], ready[1] + k // 4 + 1)
                ins = nc.tensor.transpose(bank[banks[2 * a + k // 4]][:, P * (k % 4):P * (k % 4) + P],
                                          src[:, a, P * k:P * k + P], ident[:])
                if k % 4 == 3:
                    ins.then_inc(norm_t, 1)

        def norm_turn(n, a, banks=NORM_BANKS):
            turn(xn, a, banks, (xn_ready, 2 * (TT * n + a)))

        def rows_product(p, kts, xh, xl, banks, first, last, tiles=(0, 1)):
            pe.wait_ge(lo_ready, p + 1)
            for a in tiles:
                for half in range(2):
                    for kk, k in enumerate(kts):
                        ins = mm3(bank[banks[2 * a + half]][:], True,
                                  (hi(p, 2)[:, kk, N * half:N * half + N], lo(p, 2)[:, kk, N * half:N * half + N]),
                                  (xh[:, k, P * a:P * a + P], xl[:, k, P * a:P * a + P]),
                                  first and kk == 0, last and kk == 1)
                    if last and (a, half) != (1, 1):
                        ins.then_inc(acc_done, 1)
            if 1 in tiles:
                ins.then_inc(piece_used, 1)

        def columns_product(p, dst, tiles=None):
            pe.wait_ge(lo_ready, p + 1)
            t0, t1 = (0, T) if tiles is None else (P * tiles[0], P * tiles[0] + P)
            for c in range(2):
                for k in range(KT):
                    ins = mm3(dst[:, T * c + t0:T * c + t1], False,
                              (hi(p, KT)[:, k, P * c:P * c + P], lo(p, KT)[:, k, P * c:P * c + P]),
                              (xT_hi[:, k, t0:t1], xT_lo[:, k, t0:t1]), k == 0, k == KT - 1)
            if tiles != (0,):
                ins.then_inc(piece_used, 1)

        def tokens_product(p, k0, nk, w, banks, tiles=(0, 1), signal=None):
            pe.wait_ge(lo_ready, p + 1)
            for a in tiles:
                for kk in range(nk):
                    k = k0 + kk
                    ins = mm3(bank[banks[a]][:, 0:w], True, (hi(p, nk)[:, kk, :], lo(p, nk)[:, kk, :]),
                              (xT_hi[:, k, P * a:P * a + P], xT_lo[:, k, P * a:P * a + P]), k == 0, k == KT - 1)
                if a == 0 and signal is not None:
                    ins.then_inc(signal, 1)
            if 1 in tiles:
                ins.then_inc(piece_used, 1)


        pe.wait_ge(pool_const, 3)
        norm_turn(0, 0)
        pe.wait_ge(xT_lo_ready, 2)
        for i in range(2):
            tokens_product(V0 + i, 4 * i, 4, N, (6, 7), tiles=(0,))
            if i == 0:
                norm_turn(0, 1)
        pe.wait_ge(xT_lo_ready, 4)
        for i in range(2):
            tokens_product(V0 + i, 4 * i, 4, N, (6, 7), tiles=(1,))
        pe.wait_ge(pool_spw, 1)
        for g in range(GH):
            ins = nc.tensor.transpose(bank[4][:, P * g:P * g + P], sp_w[:, g, :], ident[:])
        ins.then_inc(spw_t, 1)
        for c in range(2):
            columns_product(U0 + c, bank[c])
        for c in range(2):
            columns_product(C0 + c, bank[2 + c])
        pe.wait_ge(v_gelu, TT)
        for c in range(2):
            columns_product(X0 + c, bank[6 + c])
        pe.wait_ge(spw_ready, 1)
        pe.wait_ge(vn_ready, TT)
        for g in range(GH):
            for a in range(TT):
                c0 = T * (g % 2) + P * a
                ins = mm(bank[4 + g // 2][:, c0:c0 + P], v_act[:, a, P * g:P * g + P], sp_wT[:, g, :],
                         start=True, stop=True)
            if g % 2:
                ins.then_inc(mix_done, 1)
        pe.wait_ge(uT_ready, 2)
        for c in range(2):
            columns_product(B0 + c, bank[c])

        def mixer_out(i, tiles=(0, 1)):
            rows_product(WOUT0 + i, OUT_KT[2 * i:2 * i + 2], yT_hi, yT_lo, ACC, i == 0, i == 3, tiles)

        pe.wait_ge(yT_lo_ready, 2)
        mixer_out(0)
        mixer_out(1, (0,))
        pe.wait_ge(yT_lo_ready, 4)
        for i in (2, 3):
            mixer_out(i, (0,))
        for i in (1, 2):
            mixer_out(i, (1,))
        norm_turn(1, 0)
        mixer_out(3, (1,))

        def ffn_down(u, tiles=(0, 1)):
            pe.wait_ge(fT_lo_ready, u + 1)
            rows_product(ffn_pieces(u)[2], (0, 1), fT_hi[:, u % 2], fT_lo[:, u % 2], ACC, u == 0, u == FU - 1, tiles)

        for u in range(FU):
            g, up, _ = ffn_pieces(u)
            gb, ub = bank[(0, 4)[u % 2]], bank[(1, 5)[u % 2]]
            if u == 0:
                pe.wait_ge(xT_lo_ready, 6)
                columns_product(g, gb, (0,))
                norm_turn(1, 1)
                columns_product(up, ub, (0,))
                pe.wait_ge(xT_lo_ready, 8)
                columns_product(g, gb, (1,))
                columns_product(up, ub, (1,))
            else:
                if u >= 2:
                    pe.wait_ge(act_ready, u - 1)
                columns_product(g, gb)
                columns_product(up, ub)
                ffn_down(u - 1, (0, 1) if u < FU - 1 else (0,))
        ffn_down(FU - 1, (0,))
        ffn_down(FU - 2, (1,))
        ffn_down(FU - 1, (1,))
        norm_turn(2, 0)

        KV, Q0, Q1 = (0, 1), (2, 3), (6, 7)
        pe.wait_ge(xT_lo_ready, 10)
        tokens_product(QKV0, 0, KT, 2 * NKV * HD, KV, (0,), qkv_done)
        norm_turn(2, 1)
        tokens_product(QKV0 + 1, 0, 4, N, Q0, (0,))
        pe.wait_ge(xT_lo_ready, 12)
        tokens_product(QKV0, 0, KT, 2 * NKV * HD, KV, (1,))
        tokens_product(QKV0 + 1, 0, 4, N, Q0, (1,))
        tokens_product(QKV0 + 2, 4, 4, N, Q0, (0, 1), qkv_done)
        for a in range(TT):
            tokens_product(QKV0 + 3, 0, 4, N, Q1, (a,))
            tokens_product(QKV0 + 4, 4, 4, N, Q1, (a,), qkv_done if a == 0 else None)

        def turn_heads(a):
            pe.wait_ge(rope_ready, 2 * a + 2)
            for g in range(NKV):
                for i in range(2):
                    c0 = P * (2 * g + i)
                    ins = nc.tensor.transpose(bank[4 + a][:, c0:c0 + P], k_pad[:, a, g, i, :], ident[:])
            ins.then_inc(qk_t, 1)
            for c in range(NQ // 2):
                ins = nc.tensor.transpose(bank[Q_BANKS[2 * a + c // 4]][:, P * (c % 4):P * (c % 4) + P],
                                          qkv[:, a, P * c:P * c + P], ident[:])
                if c % 4 == 3:
                    ins.then_inc(qk_t, 1)

        def scores(i):
            a, n, first = (0, 4, 4 * i) if i < 4 else (1, 2, 2 * (i - 4))
            if i >= 3:
                pe.wait_ge(probs_ready, i - 2)
            s, w = bank[S_BANKS[i % 3]], N // n
            mask = mask0 if a == 0 else mask1
            mm(s[:], ident_b[:], mask[:].rearrange("p h k -> p (h k)"), start=True, stop=False)
            for j in range(n):
                hq = first + j
                ins = mm(s[:, w * j:w * j + w], qT[:, hq // 2, P * a:P * a + P], kT[:, hq // QPK, hq % 2, 0:w],
                         start=False, stop=j == n - 1)
            ins.then_inc(s_done, 1)

        def transpose_probs(i):
            pe.wait_ge(probs_ready, i + 1)
            if i:
                pe.wait_ge(probsT_ready, i)
            for c in range(4):
                ins = nc.tensor.transpose(bank[PT_BANK][:, P * c:P * c + P], probs[:, i % 2, P * c:P * c + P], ident[:])
            ins.then_inc(probs_t, 1)

        def weigh_values(i):
            a, n, first = (0, 4, 4 * i) if i < 4 else (1, 2, 2 * (i - 4))
            pe.wait_ge(probsT_ready, i + 1)
            for j in range(n):
                hq = first + j
                o = bank[O_BANKS[2 * a + hq // QPK]][:, HD * (hq % QPK):HD * (hq % QPK) + HD]
                v0 = (NQ + NKV + hq // QPK) * HD
                for kt in range(a + 1):
                    c = (a + 1) * j + kt
                    ins = mm(o, probsT[:, i % 2, P * c:P * c + P], qkv[:, kt, v0:v0 + HD], start=kt == 0, stop=kt == a)
            ins.then_inc(pv_done, 1)

        turn_heads(0)
        pe.wait_ge(pool_const, 7)
        pe.wait_ge(qkT_act, 2)
        pe.wait_ge(qkT_dve, 1)
        for i in range(15):
            if i == 2:
                turn_heads(1)
                pe.wait_ge(qkT_dve, 2)
            if i == 4:
                pe.wait_ge(qkT_act, 4)
            if i < 12:
                scores(i)
            if 2 <= i < 14:
                transpose_probs(i - 2)
            if i >= 3:
                weigh_values(i - 3)
            if i == 10:
                turn(o_tok, 0, OT_BANKS, (o_ready, 0))

        def attention_out(i, tiles):
            rows_product(WO0 + i, (2 * i, 2 * i + 1), xT_hi, xT_lo, WO_ACC, i == 0, i == 3, tiles)

        pe.wait_ge(xT_lo_ready, 14)
        attention_out(0, (0,))
        attention_out(1, (0,))
        turn(o_tok, 1, OT_BANKS, (o_ready, 2))
        attention_out(2, (0,))
        pe.wait_ge(xT_lo_ready, 16)
        for i in range(3):
            attention_out(i, (1,))
        attention_out(3, (0,))
        attention_out(3, (1,))
        norm_turn(3, 0, OT_BANKS)

        pe.wait_ge(ld_router, 16)
        for a in range(TT):
            if a:
                norm_turn(3, 1, OT_BANKS)
            pe.wait_ge(xTr_ready, 2 * a + 2)
            for k in range(KT):
                ins = mm(bank[OT_BANKS[2 * a]][:, 0:NE], xT[:, k, P * a:P * a + P], router[:, k, :],
                         start=k == 0, stop=k == KT - 1)
            ins.then_inc(logits_done, 1)
        pe.wait_ge(sel_ready, TT)
        r = bank[4]
        mm(r[:, 0:NE], tri[:], sel[:, 0, :], start=True, stop=True)
        mm(r[:, NE:2 * NE], ones[:], sel[:, 0, :], start=True, stop=False)
        mm(r[:, NE:2 * NE], tri[:], sel[:, 1, :], start=False, stop=True)
        mm(r[:, 2 * NE:3 * NE], ones[:], sel[:, 0, :], start=True, stop=False)
        mm(r[:, 2 * NE:3 * NE], ones[:], sel[:, 1, :], start=False, stop=True).then_inc(rank_done, 1)

        def gather():
            for k in range(KT):
                for a in range(TT):
                    ins = mm(bank[2 + k // 4][:, P * (k % 4):P * (k % 4) + P], xn[:, a, P * k:P * k + P], pick[:, a, :],
                             start=a == 0, stop=a == TT - 1)
                if k % 4 == 3:
                    ins.then_inc(gathered, 1)

        def expert_in(b, q, k0, dst):
            s = FRONT + q
            pe.wait_ge(lo_ready, b * EP + (s + 1))
            for kk in range(4):
                k = k0 + kk
                ins = mm3(dst[:], True, (hi(s, 4)[:, kk, :], lo(s, 4)[:, kk, :]), (gT_hi[:, k, :], gT_lo[:, k, :]),
                          k == 0, k == KT - 1)
            ins.then_inc(piece_used, 1)

        def expert_down(b, j):
            d = expert_pieces(j)[2]
            pe.wait_ge(eT_lo_ready, b * EU + (j + 1))
            for i in range(2):
                s = FRONT + d + i
                pe.wait_ge(lo_ready, b * EP + (s + 1))
                for kk in range(2):
                    k = 2 * i + kk
                    for half in range(2):
                        ins = mm3(bank[4 + half][:], True,
                                  (hi(s, 2)[:, kk, N * half:N * half + N], lo(s, 2)[:, kk, N * half:N * half + N]),
                                  (eT_hi[:, k, :], eT_lo[:, k, :]), j == 0 and k == 0, j == EU - 1 and k == 3)
                ins.then_inc(piece_used, 1)

        def transpose_hidden(b, j):
            pe.wait_ge(e_act, b * EU + (j + 1))
            for k in range(4):
                ins = nc.tensor.transpose(bank[6][:, P * k:P * k + P], e_a[:, P * k:P * k + P], ident[:])
            ins.then_inc(e_t, 1)

        def scatter(i, dst_bank):
            a, c = i // 2, slice(N * (i % 2), N * (i % 2) + N)
            mm(dst_bank[:], pickT[:, P * a:P * a + P], ey_hi[:, c], start=True, stop=False)
            mm(dst_bank[:], pickT[:, P * a:P * a + P], ey_lo[:, c], start=False, stop=True).then_inc(scattered, 1)

        def turn_pick(b):
            for a in range(TT):
                nc.tensor.transpose(bank[7][:, P * a:P * a + P], pick[:, a, :], ident[:])
            for a in range(TT):
                ins = mm(bank[7][:, T:T + 1], pick[:, a, :], gate_col[:, a:a + 1], start=a == 0, stop=a == TT - 1)
            ins.then_inc(pick_t, 1)

        def expert_block(b, n, last):
            for j in range(EU):
                g, up, _ = expert_pieces(j)
                if j >= 2:
                    pe.wait_ge(e_act, b * EU + (j - 1))
                for i in range(2):
                    if j == 0:
                        pe.wait_ge(gT_lo_ready, b * 2 + (i + 1))
                    expert_in(b, g + i, 4 * i, bank[2 * (j % 2)])
                if j:
                    transpose_hidden(b, j - 1)
                if j == 4:
                    pe.wait_ge(e_added, n * 4 + 5)
                    turn_pick(b)
                for i in range(2):
                    expert_in(b, up + i, 4 * i, bank[2 * (j % 2) + 1])
                if j < 2:
                    pe.wait_ge(ey_lo_ready, n * 2 + (j + 1))
                if j < 4:
                    pe.wait_ge(e_added, n * 4 + (j + 1))
                    scatter(j, bank[7])
                if j:
                    expert_down(b, j - 1)
            transpose_hidden(b, EU - 1)
            if not last:
                pe.wait_ge(pick_ready, b * TT + 2 * TT)
                gather()
            expert_down(b, EU - 1)
            if last:
                for i in range(4):
                    if i < 2:
                        pe.wait_ge(ey_lo_ready, n * 2 + (3 + i))
                    scatter(i, bank[ACC[i]])

        pe.wait_ge(pick_ready, TT)
        gather()
        with pe.Fori(0, NE - 1) as b:
            expert_block(b, b, False)
        most = nc.tensor.value_load(count_max[0:1, 0:1], min_val=0, max_val=T)
        expert_block(NE - 1, NE - 1, True)
        with pe.If(most > P):
            pe.wait_ge(pick_ready, NE * TT + TT)
            gather()
            with pe.Fori(NE, BLOCKS - 1) as b:
                expert_block(b, b + 1, False)
            expert_block(BLOCKS - 1, BLOCKS, True)

    ctx.close()


_INS = ['x', 'positions', 'final_norm_g', 'ev_norm1_g', 'ev_w_in', 'ev_conv_w', 'ev_ln_g', 'ev_ln_b',
        'ev_spatial_w', 'ev_spatial_b', 'ev_w_out', 'ev_norm2_g', 'ev_ffn_wg', 'ev_ffn_wu', 'ev_ffn_wd',
        'od_norm1_g', 'od_w_qkv', 'od_b_qkv', 'od_sinks', 'od_w_o', 'od_b_o', 'od_norm2_g', 'od_router_w',
        'od_exp_wg', 'od_exp_wu', 'od_exp_wd']


def kernel(**inputs):
    import concourse.bacc as bacc
    from concourse.bass_utils import run_bass_kernel_spmd

    nc = bacc.Bacc("TRN2", target_bir_lowering=False, num_devices=1)
    arrays, args = {}, []
    for name in _INS:
        a = np.ascontiguousarray(inputs[name])
        arrays[f"in_{name}"] = a
        args.append(nc.dram_tensor(f"in_{name}", a.shape, mybir.dt.from_np(a.dtype), kind="ExternalInput").ap())
    out = nc.dram_tensor("out_0", (1, T, D), F32, kind="ExternalOutput").ap()
    build(nc, *args, out)
    return run_bass_kernel_spmd(nc, [arrays], core_ids=[0]).results[0]["out_0"]
```
